# Optimizing a Trainium2 kernel written in Bass

```python
import jax, jax.numpy as jnp
from jax import lax
import numpy as np

D_MODEL = 1024
BATCH = 1
SEQ = 512
DEPTH = 1
DEC_BATCH = 8
DEC_SEQ = 8
PAST_LEN = 2048
PAGE_SIZE = 128

POOL_WIDTH = D_MODEL // 4
POOL_WINDOWS = (2, 4, 8, 16)
POOL_GROUP = POOL_WIDTH // len(POOL_WINDOWS)
POOL_HIST = max(POOL_WINDOWS) - 1
HEAD_DIM = 64
NSA_WIDTH = D_MODEL - POOL_WIDTH
N_HEADS = NSA_WIDTH // HEAD_DIM
GQA_GROUP = 4
KV_HEADS = N_HEADS // GQA_GROUP
KV_WIDTH = KV_HEADS * HEAD_DIM
CMP_BLOCK = 32
CMP_STRIDE = 16
CMP_HID = 2 * HEAD_DIM
SEL_BLOCK = 64
N_SEL = 16
WINDOW = 512
N_BRANCH = 3
Q_BLOCK = 128
IN_WIDTH = 2 * POOL_WIDTH + 2 * NSA_WIDTH + N_BRANCH * 2 * KV_WIDTH + N_BRANCH * N_HEADS
EPS = 1e-6
NEG = -1e30
FORCE = 1e4

kernel_name = 'hymba_pool_nsa_decoder_step'

def _rmsnorm(x, g):
    xf = x.astype(jnp.float32)
    y = xf * lax.rsqrt(jnp.mean(xf * xf, axis=-1, keepdims=True) + EPS)
    return (y * g.astype(jnp.float32)).astype(x.dtype)

def _masked_softmax(s, mask):
    s = jnp.where(mask, s.astype(jnp.float32), NEG)
    m = jnp.max(s, axis=-1, keepdims=True)
    e = jnp.where(mask, jnp.exp(s - m), 0.0)
    return e / jnp.maximum(jnp.sum(e, axis=-1, keepdims=True), 1e-30)

def _in_proj(x, c, norm_w, w_ada, b_ada, w_in):
    B, T = x.shape[0], x.shape[1]
    ada = jax.nn.silu(c) @ w_ada + b_ada
    shift, scale, gate = jnp.split(ada, 3, axis=-1)
    h = _rmsnorm(x, norm_w) * (1.0 + scale[:, None, :]) + shift[:, None, :]
    z = h @ w_in
    sizes = [POOL_WIDTH, POOL_WIDTH, NSA_WIDTH, NSA_WIDTH, 2 * KV_WIDTH, 2 * KV_WIDTH, 2 * KV_WIDTH]
    cuts = [sum(sizes[:i + 1]) for i in range(len(sizes))]
    u, zp, q, zn, kvc, kvs, kvw, gl = jnp.split(z, cuts, axis=-1)
    q = q.reshape(B, T, KV_HEADS, GQA_GROUP, HEAD_DIM)
    kv_shape = (B, T, 2, KV_HEADS, HEAD_DIM)
    g = jax.nn.sigmoid(gl.astype(jnp.float32)).astype(x.dtype)
    g = g.reshape(B, T, KV_HEADS, GQA_GROUP, N_BRANCH)
    return u, zp, q, zn, kvc.reshape(kv_shape), kvs.reshape(kv_shape), kvw.reshape(kv_shape), g, gate

def _pool_mix(u_hist, u, pos0, pool_w, pool_scale):
    B, P, C = u_hist.shape
    T = u.shape[1]
    ue = jnp.concatenate([u_hist, u], axis=1)
    uf = ue.astype(jnp.float32)
    cs = jnp.concatenate([jnp.zeros((B, 1, C), jnp.float32), jnp.cumsum(uf, axis=1)], axis=1)
    e = P + jnp.arange(T)
    pos = pos0 + jnp.arange(T)
    hi = cs[:, e + 1]
    means = []
    for gi, w in enumerate(POOL_WINDOWS):
        sl = slice(gi * POOL_GROUP, (gi + 1) * POOL_GROUP)
        lo = cs[:, jnp.maximum(e + 1 - w, 0), sl]
        cnt = jnp.minimum(w, pos + 1).astype(jnp.float32)[None, :, None]
        means.append((hi[..., sl] - lo) / cnt)
    d = (jnp.concatenate(means, axis=-1) - uf[:, P:]).astype(u.dtype)
    d = d.reshape(B, T, len(POOL_WINDOWS), POOL_GROUP)
    y = jnp.einsum('btgc,gcd->btgd', d, pool_w).reshape(B, T, POOL_WIDTH) * pool_scale
    return y, ue[:, -POOL_HIST:]

def _compress(kv, w1, pe, w2):
    B, L = kv.shape[0], kv.shape[1]
    n_str = -(-L // CMP_STRIDE)
    span = CMP_BLOCK // CMP_STRIDE
    n_cmp = n_str - span + 1
    kv = jnp.pad(kv, ((0, 0), (0, n_str * CMP_STRIDE - L), (0, 0), (0, 0), (0, 0)))
    ch = kv.reshape(B, n_str, CMP_STRIDE, 2, KV_HEADS, HEAD_DIM)
    pre = 0.0
    for m in range(span):
        sl = slice(m * CMP_STRIDE, (m + 1) * CMP_STRIDE)
        a = jnp.einsum('bnjkgd,jkdh->bnkgh', ch, w1[sl]) + jnp.einsum('jkd,jkdh->kh', pe[sl], w1[sl])[:, None, :]
        pre = pre + a[:, m:m + n_cmp]
    comp = jnp.einsum('bnkgh,khd->bnkgd', jax.nn.gelu(pre), w2)
    cend = jnp.arange(n_cmp) * CMP_STRIDE + (CMP_BLOCK - 1)
    return comp, cend

def _nsa_core(q, qpos, comp, cend, gather_sel, n_sel, kvw, wpos, g):
    B, T, G, R = q.shape[0], q.shape[1], q.shape[2], q.shape[3]
    scale = HEAD_DIM ** -0.5
    s = jnp.einsum('btgrd,bngd->btgrn', q, comp[:, :, 0]) * scale
    p = _masked_softmax(s, (cend[None, :] <= qpos[:, None])[None, :, None, None, :])
    o_c = jnp.einsum('btgrn,bngd->btgrd', p.astype(q.dtype), comp[:, :, 1])
    pg = jnp.sum(p, axis=3)
    span = CMP_BLOCK // CMP_STRIDE
    n_str = cend.shape[0] + span - 1
    pp = jnp.pad(pg, ((0, 0), (0, 0), (0, 0), (span - 1, span - 1)))
    ps = sum(pp[..., span - 1 - m:span - 1 - m + n_str] for m in range(span))
    ratio = SEL_BLOCK // CMP_STRIDE
    ps = jnp.pad(ps, ((0, 0), (0, 0), (0, 0), (0, n_sel * ratio - n_str)))
    imp = ps.reshape(B, T, G, n_sel, ratio).sum(-1)
    blk = jnp.arange(n_sel)[None, :]
    cur = (qpos // SEL_BLOCK)[:, None]
    forced = (blk == 0) | (blk == cur) | (blk == cur - 1)
    score = jnp.where((blk <= cur)[None, :, None, :], imp, -1.0)
    score = jnp.where(forced[None, :, None, :], FORCE, score)
    k_top = min(N_SEL, n_sel)
    idx = lax.top_k(score, k_top)[1].transpose(0, 2, 1, 3)
    kvg = gather_sel(idx)
    kpos = idx[..., None] * SEL_BLOCK + jnp.arange(SEL_BLOCK)
    smask = (kpos <= qpos[None, None, :, None, None]).reshape(B, G, T, 1, k_top * SEL_BLOCK)
    s = jnp.einsum('btgrd,bgtnjd->bgtrnj', q, kvg[..., 0, :]) * scale
    p = _masked_softmax(s.reshape(B, G, T, R, k_top * SEL_BLOCK), smask).reshape(B, G, T, R, k_top, SEL_BLOCK)
    o_s = jnp.einsum('bgtrnj,bgtnjd->btgrd', p.astype(q.dtype), kvg[..., 1, :])
    dq = qpos[:, None] - wpos[None, :]
    wmask = (dq >= 0) & (dq < WINDOW) & (wpos[None, :] >= 0)
    s = jnp.einsum('btgrd,blgd->btgrl', q, kvw[:, :, 0]) * scale
    p = _masked_softmax(s, wmask[None, :, None, None, :])
    o_w = jnp.einsum('btgrl,blgd->btgrd', p.astype(q.dtype), kvw[:, :, 1])
    o = g[..., 0:1] * o_c + g[..., 1:2] * o_s + g[..., 2:3] * o_w
    return o.reshape(B, T, NSA_WIDTH)

def _nsa_prompt(q, kvc, kvs, kvw, g, w1, pe, w2):
    B, S = q.shape[0], q.shape[1]
    comp, cend = _compress(kvc, w1, pe, w2)
    n_sel = -(-S // SEL_BLOCK)
    kvs_b = jnp.pad(kvs, ((0, 0), (0, n_sel * SEL_BLOCK - S), (0, 0), (0, 0), (0, 0)))
    kvs_b = kvs_b.reshape(B, n_sel, SEL_BLOCK, 2, KV_HEADS, HEAD_DIM)
    bidx = jnp.arange(B)[:, None, None, None]
    gidx = jnp.arange(KV_HEADS)[None, :, None, None]

    def gather_sel(idx):
        return kvs_b[bidx, idx, :, :, gidx]

    kvw_pad = jnp.pad(kvw, ((0, 0), (WINDOW, 0), (0, 0), (0, 0), (0, 0)))

    def body(i):
        qs = i * Q_BLOCK
        qc = lax.dynamic_slice_in_dim(q, qs, Q_BLOCK, axis=1)
        gc = lax.dynamic_slice_in_dim(g, qs, Q_BLOCK, axis=1)
        kw = lax.dynamic_slice_in_dim(kvw_pad, qs, WINDOW + Q_BLOCK, axis=1)
        qpos = qs + jnp.arange(Q_BLOCK)
        wpos = qs - WINDOW + jnp.arange(WINDOW + Q_BLOCK)
        return _nsa_core(qc, qpos, comp, cend, gather_sel, n_sel, kw, wpos, gc)

    o = lax.map(body, jnp.arange(S // Q_BLOCK))
    return o.transpose(1, 0, 2, 3).reshape(B, S, NSA_WIDTH)

def _nsa_sample(q, kvc, kvs, kvw, g, cache_cmp, cache_slc, win_buf, page_table, w1, pe, w2):
    DB, T = q.shape[0], q.shape[1]
    n_pages = page_table.shape[1]
    past = n_pages * PAGE_SIZE
    qpos = past + jnp.arange(T)
    past_cmp = cache_cmp[page_table].reshape(DB, past, 2, KV_HEADS, HEAD_DIM)
    comp, cend = _compress(jnp.concatenate([past_cmp, kvc], axis=1), w1, pe, w2)
    n_sel = -(-(past + T) // SEL_BLOCK)
    n_past_blk = past // SEL_BLOCK
    n_new_blk = n_sel - n_past_blk
    new_b = jnp.pad(kvs, ((0, 0), (0, n_new_blk * SEL_BLOCK - T), (0, 0), (0, 0), (0, 0)))
    new_b = new_b.reshape(DB, n_new_blk, SEL_BLOCK, 2, KV_HEADS, HEAD_DIM)
    bpp = PAGE_SIZE // SEL_BLOCK
    pool_b = cache_slc.reshape(-1, SEL_BLOCK, 2, KV_HEADS, HEAD_DIM)
    bidx = jnp.arange(DB)[:, None, None, None]
    gidx = jnp.arange(KV_HEADS)[None, :, None, None]

    def gather_sel(idx):
        page = page_table[bidx, jnp.clip(idx // bpp, 0, n_pages - 1)]
        old = pool_b[page * bpp + idx % bpp, :, :, gidx]
        new = new_b[bidx, jnp.clip(idx - n_past_blk, 0, n_new_blk - 1), :, :, gidx]
        return jnp.where((idx >= n_past_blk)[..., None, None, None], new, old)

    buf = win_buf.shape[1]
    kw = jnp.concatenate([win_buf, kvw], axis=1)
    wpos = past - buf + jnp.arange(buf + T)
    o = _nsa_core(q, qpos, comp, cend, gather_sel, n_sel, kw, wpos, g)
    return o, kw[:, -buf:]

def _out(x, pool_o, zp, nsa_o, zn, gate, gn_pool, gn_nsa, w_out):
    m = jnp.concatenate([_rmsnorm(pool_o, gn_pool) * jax.nn.silu(zp),
                         _rmsnorm(nsa_o, gn_nsa) * jax.nn.silu(zn)], axis=-1)
    return x + gate[:, None, :] * (m @ w_out)

def setup_inputs(seed: int = 0) -> dict:
    key = jax.random.key(seed)
    ks = jax.random.split(key, 24)
    n_pages = PAST_LEN // PAGE_SIZE
    n_used = DEC_BATCH * n_pages
    n_phys = n_used + n_used // 4
    win_len = min(WINDOW, PAST_LEN)
    f32 = jnp.float32
    nrm = lambda k, shape, s=1.0: jax.random.normal(k, shape, f32) * s
    page_table = jax.random.permutation(ks[0], n_phys)[:n_used].reshape(DEC_BATCH, n_pages).astype(jnp.int32)
    return {
        'x_prompt': nrm(ks[1], (BATCH, SEQ, D_MODEL)),
        'x_sample': nrm(ks[2], (DEC_BATCH, DEC_SEQ, D_MODEL)),
        'c_prompt': nrm(ks[3], (BATCH, D_MODEL)),
        'c_sample': nrm(ks[4], (DEC_BATCH, D_MODEL)),
        'cache_cmp_kv': nrm(ks[5], (DEPTH, n_phys, PAGE_SIZE, 2, KV_HEADS, HEAD_DIM)),
        'cache_slc_kv': nrm(ks[6], (DEPTH, n_phys, PAGE_SIZE, 2, KV_HEADS, HEAD_DIM)),
        'state_win_kv': nrm(ks[7], (DEPTH, DEC_BATCH, win_len, 2, KV_HEADS, HEAD_DIM)),
        'state_pool': nrm(ks[8], (DEPTH, DEC_BATCH, POOL_HIST, POOL_WIDTH)),
        'page_table': page_table,
        'norm_w': 1.0 + nrm(ks[9], (DEPTH, D_MODEL), 0.05),
        'w_ada': nrm(ks[10], (DEPTH, D_MODEL, 3 * D_MODEL), 0.5 * D_MODEL ** -0.5),
        'b_ada': nrm(ks[11], (DEPTH, 3 * D_MODEL), 0.02),
        'w_in': nrm(ks[12], (DEPTH, D_MODEL, IN_WIDTH), D_MODEL ** -0.5),
        'pool_w': nrm(ks[13], (DEPTH, len(POOL_WINDOWS), POOL_GROUP, POOL_GROUP), POOL_GROUP ** -0.5),
        'pool_scale': 1.0 + nrm(ks[14], (DEPTH, POOL_WIDTH), 0.1),
        'phi_w1': nrm(ks[15], (DEPTH, CMP_BLOCK, 2, HEAD_DIM, CMP_HID), (CMP_BLOCK * HEAD_DIM) ** -0.5),
        'phi_pe': nrm(ks[16], (DEPTH, CMP_BLOCK, 2, HEAD_DIM), 0.1),
        'phi_w2': nrm(ks[17], (DEPTH, 2, CMP_HID, HEAD_DIM), 1.4 * CMP_HID ** -0.5),
        'gn_pool': 1.0 + nrm(ks[18], (DEPTH, POOL_WIDTH), 0.05),
        'gn_nsa': 1.0 + nrm(ks[19], (DEPTH, NSA_WIDTH), 0.05),
        'w_out': nrm(ks[20], (DEPTH, D_MODEL, D_MODEL), D_MODEL ** -0.5),
        'final_norm': 1.0 + nrm(ks[21], (D_MODEL,), 0.05),
    }

def reference(x_prompt, x_sample, c_prompt, c_sample, cache_cmp_kv, cache_slc_kv, state_win_kv, state_pool,
              page_table, norm_w, w_ada, b_ada, w_in, pool_w, pool_scale, phi_w1, phi_pe, phi_w2,
              gn_pool, gn_nsa, w_out, final_norm):
    past = page_table.shape[1] * PAGE_SIZE
    xp, xs = x_prompt, x_sample
    cmp_p, cmp_s, slc_p, slc_s = [], [], [], []
    win_p, win_s, pool_p, pool_s = [], [], [], []
    for l in range(DEPTH):
        u, zp, q, zn, kvc, kvs, kvw, g, gate = _in_proj(xp, c_prompt, norm_w[l], w_ada[l], b_ada[l], w_in[l])
        pool_o, hist = _pool_mix(u[:, :0], u, 0, pool_w[l], pool_scale[l])
        nsa_o = _nsa_prompt(q, kvc, kvs, kvw, g, phi_w1[l], phi_pe[l], phi_w2[l])
        xp = _out(xp, pool_o, zp, nsa_o, zn, gate, gn_pool[l], gn_nsa[l], w_out[l])
        cmp_p.append(kvc)
        slc_p.append(kvs)
        win_p.append(kvw[:, -min(WINDOW, kvw.shape[1]):])
        pool_p.append(hist)
        u, zp, q, zn, kvc, kvs, kvw, g, gate = _in_proj(xs, c_sample, norm_w[l], w_ada[l], b_ada[l], w_in[l])
        pool_o, hist = _pool_mix(state_pool[l], u, past, pool_w[l], pool_scale[l])
        nsa_o, win_new = _nsa_sample(q, kvc, kvs, kvw, g, cache_cmp_kv[l], cache_slc_kv[l], state_win_kv[l],
                                     page_table, phi_w1[l], phi_pe[l], phi_w2[l])
        xs = _out(xs, pool_o, zp, nsa_o, zn, gate, gn_pool[l], gn_nsa[l], w_out[l])
        cmp_s.append(kvc)
        slc_s.append(kvs)
        win_s.append(win_new)
        pool_s.append(hist)
    y_prompt = _rmsnorm(xp, final_norm)
    y_sample = _rmsnorm(xs, final_norm)
    return (y_prompt, y_sample, jnp.stack(cmp_p), jnp.stack(cmp_s), jnp.stack(slc_p), jnp.stack(slc_s),
            jnp.stack(win_p), jnp.stack(win_s), jnp.stack(pool_p), jnp.stack(pool_s))


_drawn_inputs = setup_inputs


def setup_inputs(seed=0):
    import zlib

    import numpy as np

    out = dict(_drawn_inputs(seed))
    spreads = {}
    factors = {'cache_slc_kv': 2.861, 'pool_scale': 6.357, 'gn_pool': 8.0, 'gn_nsa': 6.854}
    for name, (base, spread) in spreads.items():
        noise = np.random.default_rng([zlib.crc32(name.encode()), seed]).standard_normal(out[name].shape)
        drawn = base * np.exp(spread * noise) if base else spread * noise
        out[name] = __import__('jax').numpy.asarray(drawn.astype(out[name].dtype))
    for name, factor in factors.items():
        out[name] = (out[name] * factor).astype(out[name].dtype)
    return out
```

```python
from contextlib import ExitStack

import concourse.bass as bass
from concourse import mybir
from concourse.alu_op_type import AluOpType as ALU

ACT = mybir.ActivationFunctionType
AX = mybir.AxisListType.X
F32 = mybir.dt.float32
I32 = mybir.dt.int32
P = 128
EPS = 1e-6
NEG = -1e30
FORCE = 1e4


class Steps:

    def __init__(self, eng, sem):
        self.eng, self.sem, self.n, self.at = eng, sem, 0, None

    def enter(self, turn, per_turn):
        self.before, self.at, self.per_turn, self.n = self.n, turn * per_turn, per_turn, 0

    def leave(self, turns):
        assert self.n == self.per_turn, self.n
        self.n, self.at = self.before + turns * self.per_turn, None

    def done(self, ins, passed=None):
        ins.then_inc(self.sem, 1)
        self.n += 1
        if self.at is None:
            self.eng.wait_ge(self.sem, self.n)
        else:
            self.eng.wait_ge(self.sem, self.at + (self.before + self.n))
        if passed is not None:
            self.eng.sem_inc(passed, 1)


def program(nc, x_prompt, x_sample, c_prompt, c_sample, cache_cmp_kv, cache_slc_kv, state_win_kv, state_pool,
            page_table, norm_w, w_ada, b_ada, w_in, pool_w, pool_scale, phi_w1, phi_pe, phi_w2,
            gn_pool, gn_nsa, w_out, final_norm,
            y_prompt, y_sample, new_cmp_p, new_cmp_s, new_slc_p, new_slc_s, new_win_p, new_win_s,
            new_pool_p, new_pool_s):
    T, D = x_prompt.shape[1:]
    DB, TS = x_sample.shape[:2]
    NS = DB * TS
    n_phys, page, _, G, d = cache_cmp_kv.shape[1:]
    n_pages = page_table.shape[1]
    PAST = n_pages * page
    KV = 2 * G * d
    PW = pool_w.shape[1] * pool_w.shape[2]
    NW = D - PW
    H = NW // d
    R = H // G
    HID = phi_w1.shape[4]
    SPAN = phi_w1.shape[1]
    ST = SPAN // 2
    KC = D // P
    NT = T // P
    WIN = state_win_kv.shape[2]
    WJ = WIN // P
    HIST = state_pool.shape[2]
    SB = 64
    NSTR = PAST // ST
    NC = NSTR - 1
    PSTR = T // ST
    PC = PSTR - 1
    JP = ST // 2
    NB = DB + 1
    GR = G * R * TS
    SCALE = d ** -0.5
    NSEL = PAST // SB + 1
    KEEP = 16
    assert NSEL - 1 > KEEP and SB // ST * (NSEL - 1) == NSTR and TS <= SB
    POOL_WINDOWS = (2, 4, 8, 16)
    assert PW == 2 * P and HIST == POOL_WINDOWS[-1] - 1
    assert NSTR == P and d == 64 and G == 3 and HID == P and GR == 96 and T <= WIN and KC == 8
    PPS = page // ST

    cmp_rows = cache_cmp_kv.rearrange("l n (s j) k g d -> (l n s) (j k g d)", j=ST)
    slc_rows = cache_slc_kv.rearrange("l n (s j) k g d -> (l n s) (j k g d)", j=ST)

    with ExitStack() as ctx:
        def sem(name):
            return ctx.enter_context(nc.semaphore(name))

        def at(name, shape, offset, dtype=F32):
            return nc.alloc_sbuf_tensor_at(name, shape, dtype, offset=offset)

        top = -(-nc.sbuf_base // 64) * 64

        def region(nbytes):
            nonlocal top
            start = top
            top += -(-nbytes // 32) * 32
            assert top <= nc.sbuf_usable_end, top
            return start

        def own(name, shape, dtype=F32):
            n = 4
            for s in shape[1:]:
                n *= s
            return at(name, shape, region(n), dtype)

        ident = own("ident", [P, P])
        ones = own("ones", [P, P])
        sel_page = own("sel_page", [n_pages, P])
        sel_prompt = own("sel_prompt", [NB, P])
        sel_seq = own("sel_seq", [NB, NS])
        sel_sum_r = own("sel_sum_r", [GR, G, TS])
        sel_rep_r = own("sel_rep_r", [G * TS, G, R, TS])
        causal = own("causal", [P, P])
        cmp_mask = own("cmp_mask", [P, NT, PC])
        cmp_any = own("cmp_any", [P, NT])
        win_mask = own("win_mask", [P, WJ + 1, H, TS])
        NVEC = 3 * KC + KC + KC + 4 * SPAN // 4
        vec_t = own("vec_t", [P, NVEC])
        ada_t = own("ada_t", [P, 3 * KC, NB])
        ada_mul = own("ada_mul", [P, KC, NB])
        pe_bias = own("pe_bias", [P, 2])
        w2 = own("w2", [P, 2, d])
        page_f = own("page_f", [n_pages, DB + 1])
        page_i = own("page_i", [n_pages, DB], I32)
        stride_f = own("stride_f", [P, DB + 2])
        stride_i = own("stride_i", [P, DB], I32)
        gates = own("gates", [P, NT + 1, 3 * H])

        cs_t = own("cs_t", [P, KC, NB])
        sumsq = own("sumsq", [P, NT + 1])
        rstd = own("rstd", [P, NT + 1])
        q_heads = own("q_heads", [P, H, NS])
        pool_bd = own("pool_bd", [P, PW // P, P])
        ramp = own("ramp", [P, PW // P, HIST + 1])
        mix_seq = own("mix_seq", [P, PW // P, NS])
        gate_rows = own("gate_rows", [GR, DB, 3])
        u_seq = own("u_seq", [P, PW // P, DB, HIST + TS])

        R_HT = region(KC * (T + NS) * 4)
        R_Z = region((NT + 1) * D * 4)
        R_KV = region((NT + 1) * (2 * KV + 3 * H) * 4)
        R_D = region((NW // P * T + PW // P * T + G * 2 * T) * 4)
        R_W1 = region(16384)
        R_CK = region(DB * 2 * NC * 4)
        R_CV = region(DB * G * d * 4)
        R_PCK = region(G * PC * 4)
        R_PCV = region(G * d * 4)
        R_X = region(2 * ST * KV * 4)
        R_W = region(2 * KC * 512 * 4)

        hT = at("hT", [P, KC, T + NS], R_HT)
        vec = at("vec", [NVEC, P], R_HT)
        c_rows = at("c_rows", [NB, D], R_HT + 1024)
        c_silu = at("c_silu", [NB, D], R_HT + 1024 + 4 * D)
        w1 = at("w1", [P, 2 * JP, 2, HID], R_W1)
        caches = [at(f"cache{u}", [P, ST, KV], R_X + u * ST * KV * 4) for u in range(2)]
        NXT = 4
        xt = [at(f"xt{s}", [P, 2 * G, P], R_D + s * 2 * G * P * 4) for s in range(NXT)]
        hid = at("hid", [P, 2, G, NC], R_D + NXT * 2 * G * P * 4)
        comp_k = at("comp_k", [P, DB, 2, NC], R_CK)
        comp_v = at("comp_v", [P, DB, G * d], R_CV)

        hist_rows = at("hist_rows", [DB * HIST, PW], R_HT + 1024 + 8 * D)
        scale_row = at("scale_row", [P, PW], R_HT + 1024 + 8 * D + 4 * PW)
        ramp_i = at("ramp_i", [P, PW // P, HIST + 1], R_HT + 16384, I32)
        x_rows = at("x_rows", [P, NT + 1, D], R_Z)
        x_sq = at("x_sq", [P, D], R_KV)
        wcols = [at(f"wcols{u}", [P, KC, 512], R_W + u * KC * 512 * 4) for u in range(2)]
        z_gate = at("z_gate", [P, NT + 1, D], R_Z)
        kv = at("kv", [P, NT + 1, 2 * KV + 3 * H], R_KV)
        qT = at("qT", [P, NW // P, T], R_D)
        uT = at("uT", [P, PW // P, T], R_D + NW // P * T * 4)
        R_KT = R_D + (NW + PW) // P * T * 4
        kT = at("kT", [d, 2, G, T], R_KT)
        cmp_new = at("cmp_new", [P, NT + 1, KV], R_KT)
        qS = at("qS", [P, NW // P, NS], R_KT + (NT + 1) * KV * 4)
        xp = at("xp", [PSTR, ST, KV], R_W)
        xpt = at("xpt", [P, JP, 2 * G, PSTR], R_W + ST * KV * 4)
        nsa = at("nsa", [P, NT + 1, NW], R_HT)
        hid_p = at("hid_p", [P, 2, G, PC], R_HT + (NT + 1) * NW * 4)
        u_last = at("u_last", [NS, 2, PW], R_HT + (NT + 1) * NW * 4 + 1024)
        uS = at("uS", [P, PW // P, NS], R_KT + (NT + 1) * KV * 4 + NW // P * NS * 4)
        pcomp_k = at("pcomp_k", [d, G * PC], R_PCK)
        w_at = R_W
        def in_w(name, shape):
            nonlocal w_at
            n = 4
            for x in shape[1:]:
                n *= x
            n = -(-n // 32) * 32
            w_at += n
            return at(name, shape, w_at - n)
        q_head = [in_w(f"q_head{u}", [d, T]) for u in range(2)]
        probs = [in_w(f"probs{u}", [P, 2, T]) for u in range(2)]
        probs_t = [in_w(f"probs_t{u}", [P, 2, NT, P]) for u in range(2)]
        cprobs = [in_w(f"cprobs{u}", [P, NT, PC]) for u in range(2)]
        cprobs_t = [in_w(f"cprobs_t{u}", [PC, NT, P]) for u in range(2)]
        peak = [in_w(f"peak{u}", [P, NT]) for u in range(2)]
        total = [in_w(f"total{u}", [P, NT]) for u in range(4)]
        share = [in_w(f"share{u}", [P, NT]) for u in range(2)]
        assert w_at <= R_W + 2 * KC * 512 * 4
        PAD = HIST + 1
        sums = [at(f"sums{u}", [P, PW // P, PAD + T], R_W1 + u * (PAD + T) * 8) for u in range(2)]
        seq_sums = [at(f"seq_sums{u}", [P, PW // P, DB, HIST + TS], R_W1 + (PAD + T) * 16 + u * 2048) for u in range(2)]
        pcomp_v = at("pcomp_v", [P, G * d], R_PCV)

        C_Q, C_ZN, C_KVC = 2 * PW, 2 * PW + NW, 2 * PW + 2 * NW
        C_GL = C_KVC + 3 * KV
        IN_BLOCKS = [(C_KVC, KV), (C_KVC + KV, KV), (C_KVC + 2 * KV, KV + 3 * H), (C_Q, 512), (C_Q + 512, 512),
                     (0, 512), (C_ZN + 256, 512)]
        assert C_Q + 1024 == C_ZN + 256 and C_ZN + 768 == C_KVC and C_GL + 3 * H == w_in.shape[2]
        jobs = []
        for n, (c0, width) in enumerate(IN_BLOCKS):
            at_col = 0
            while at_col < width:
                c = c0 + at_col
                if c < PW or C_Q <= c < C_ZN:
                    jobs.append((n, True, at_col, P, None, "prompt", c))
                    jobs.append((n, True, at_col, P, None, "sample", c))
                    at_col += P
                else:
                    w = 256 if n == 5 else (width - at_col)
                    for t in range(NT + 1):
                        jobs.append((n, False, at_col, w, t, "rows", c))
                    at_col += w
        by = []
        count = [0, 0]
        for j, (n, turned, _, _, t, what, c) in enumerate(jobs):
            gate = not turned and (PW <= c < C_Q or C_ZN <= c < C_KVC)
            e = 0 if gate else (1 if (turned and what == "sample") or n < 3 else j // 2 % 2)
            count[e] += 1
            by.append((e, count[e]))
        block_jobs = [sum(1 for j in jobs if j[0] <= n) for n in range(len(IN_BLOCKS))]
        first_job = [0] + block_jobs

        SL, WL = ST + 1, WJ + 1
        key_t01 = at("key_t01", [P, ST, P], R_D)
        key_t2 = at("key_t2", [P, ST // 2, P], R_D + ST * P * 4)
        wkey_t01 = at("wkey_t01", [P, WJ, P], R_KT)
        wkey_t2 = at("wkey_t2", [P, WJ // 2, P], R_KT + WJ * P * 4)
        r_at = R_KT + WJ * P * 6
        new_t01 = at("new_t01", [P, 2, NS], r_at)
        new_t2 = at("new_t2", [d, 2, NS], r_at + 8 * NS)
        ckeys = at("ckeys", [P, 2, P], r_at + 16 * NS)
        new_pad01 = at("new_pad01", [P, 2, P], r_at + 16 * NS + 1024)
        new_pad2 = at("new_pad2", [d, 2, P], r_at + 16 * NS + 2048)
        q01 = at("q01", [P, 2 * R * TS], r_at + 16 * NS + 3072)
        q2 = at("q2", [P, 2 * R * TS], r_at + 16 * NS + 3072 + 256)
        out_rows = at("out_rows", [GR, d], r_at + 16 * NS + 3072 + 512)
        sc = at("sc", [P, SL + WL, GR], R_KV)
        k_at = R_KV + (SL + WL) * GR * 4
        def in_k(name, shape):
            nonlocal k_at
            n = 4
            for x in shape[1:]:
                n *= x
            n = -(-n // 32) * 32
            k_at += n
            assert k_at <= R_KV + (NT + 1) * (2 * KV + 3 * H) * 4
            return at(name, shape, k_at - n)
        cp = in_k("cp", [GR, NC])
        cp_t = in_k("cp_t", [NC, GR])
        cpeak = in_k("cpeak", [GR, 4])
        groups = in_k("groups", [G * TS, 1 + NSTR])
        imp = in_k("imp", [G * TS, NSEL])
        imp8 = in_k("imp8", [G * TS, 16])
        chosen = in_k("chosen", [G * TS, NSTR])
        bias = in_k("bias", [P, GR])
        peak2 = in_k("peak2", [P, 2, GR])
        peak_row = in_k("peak_row", [GR, 2])
        peak_diag = in_k("peak_diag", [GR, 2, GR])
        sum2 = in_k("sum2", [P, 2, GR])
        coef = in_k("coef", [GR, 4])
        win_rows = [at(f"win_rows{u}", [P, WJ, KV], R_W1 + u * WJ * KV * 4) for u in range(2)]
        new_v = [at(f"new_v{u}", [TS, 2, G * d], R_W1 + 2 * WJ * KV * 4 + u * 2 * G * d * 4) for u in range(2)]
        gate_dram = nc.dram_tensor("gate_dram", [NS, 3 * H], F32).ap()
        out_dram = nc.dram_tensor("out_dram", [DB, GR, d], F32).ap()
        w_o = at("w_o", [P, KC, D], R_W)
        mixT = [at(f"mixT{u}", [P, KC, P], R_D + u * 4 * D) for u in range(2)]
        mixed_rows = [at("mixed_rows0", [P, D], R_D + 8 * D), at("mixed_rows1", [P, D], R_KT)]
        y_rows = [at(f"y_rows{u}", [P, D], R_KT + (1 + u) * 4 * D) for u in range(2)]
        gate_all = at("gate_all", [P, 2, D], R_KV)
        norm_row = at("norm_row", [P, D], R_X)
        gate_bc = at("gate_bc", [NB, D], R_W1)
        x_again = [at(f"x_again{u}", [P, D], R_W1 + (1 + u) * 4 * D) for u in range(2)]
        osq = [at(f"osq{u}", [P, D], R_X + (1 + u) * 4 * D) for u in range(2)]
        ostat = at("ostat", [P, NT + 1, 4], R_X + 12 * D)
        orstd = at("orstd", [P, NT + 1, 4], R_X + 12 * D + 128)

        UNITS = NT + 1

        ps = ctx.enter_context(nc.psum_tensor("ps", [P, 8, 512], F32))

        const_made = sem("const_made")
        pool_own = sem("pool_own")
        vec_in = sem("vec_in")
        phi_in = sem("phi_in")
        dve_own = sem("dve_own")
        act_own = sem("act_own")
        silu_c = sem("silu_c")
        page_cast = sem("page_cast")
        turned_small = sem("turned_small")
        vec_made = sem("vec_made")
        pe_sum = sem("pe_sum")
        pe_bias_made = sem("pe_bias_made")
        strides_made = sem("strides_made")
        cache_in = [sem(f"cache_in{u}") for u in range(2)]
        pairs_turned = [sem(f"pairs_turned{u}") for u in range(2)]
        pairs_out = [sem(f"pairs_out{u}") for u in range(2)]
        pairs_used = sem("pairs_used")
        hidden = sem("hidden")
        comp_sum = sem("comp_sum")
        comp_k_out = sem("comp_k_out")
        comp_v_out = sem("comp_v_out")

        mix_in = sem("mix_in")
        mix_made = sem("mix_made")
        ramp_made = sem("ramp_made")
        u_last_turned = sem("u_last_turned")
        u_last_out = sem("u_last_out")
        mixed = sem("mixed")
        sums_own = sem("sums_own")
        q_in = [sem(f"q_in{u}") for u in range(2)]
        passed = sem("passed")
        scores = sem("scores")
        peaks = sem("peaks")
        probs_made = sem("probs_made")
        probs_turned = sem("probs_turned")
        probs_out = [sem("probs_out0"), sem("probs_out1")]
        values = sem("values")
        values_out = sem("values_out")
        gates_in = sem("gates_in")
        gates_stored = sem("gates_stored")
        seq_in = [sem(f"seq_in{u}") for u in range(2)]
        win_in = [sem(f"win_in{u}") for u in range(2)]
        win_stored = sem("win_stored")
        new_turned = sem("new_turned")
        new_t_made = sem("new_t_made")
        staged = sem("staged")
        cscores = sem("cscores")
        cpeaks = sem("cpeaks")
        cexp = sem("cexp")
        cp_made = sem("cp_made")
        cp_turned = sem("cp_turned")
        cp_out = sem("cp_out")
        chosen_made = sem("chosen_made")
        bias_sum = sem("bias_sum")
        keys_turned = sem("keys_turned")
        keys_out = [sem("keys_out0"), sem("keys_out1")]
        seq_scores = sem("seq_scores")
        peaks_made = sem("peaks_made")
        peaks_turned = sem("peaks_turned")
        diag_made = sem("diag_made")
        peaks_spread = sem("peaks_spread")
        shifted = sem("shifted")
        seq_exp = sem("seq_exp")
        sums_made = sem("sums_made")
        seq_values = sem("seq_values")
        cvalues = sem("cvalues")
        cvalues_out = sem("cvalues_out")
        out_made = sem("out_made")
        out_stored = sem("out_stored")
        nsa_in = sem("nsa_in")
        w_o_in = sem("w_o_in")
        norm_in = sem("norm_in")
        gate_turned = sem("gate_turned")
        gate_copied = sem("gate_copied")
        gate_spread = sem("gate_spread")
        gate_made = sem("gate_made")
        pool_values = sem("pool_values")
        osums = sem("osums")
        omeans = sem("omeans")
        oroots = sem("oroots")
        mixed_made = sem("mixed_made")
        mixed_turned = sem("mixed_turned")
        mixT_made = [sem("mixT_made0"), sem("mixT_made1")]
        projected = sem("projected")
        y_sum = sem("y_sum")
        ysq = sem("ysq")
        ymeans = sem("ymeans")
        yroots = sem("yroots")
        y_made = sem("y_made")
        y_stored = [sem(f"y_stored{u}") for u in range(2)]
        x_again_in = [sem(f"x_again_in{u}") for u in range(2)]
        passed_dve = sem("passed_dve")
        x_in = sem("x_in")
        sumsq_made = sem("sumsq_made")
        rstd_root = sem("rstd_root")
        ms_made = sem("ms_made")
        xhat_made = sem("xhat_made")
        cs_made = sem("cs_made")
        wcols_in = [sem(f"wcols_in{u}") for u in range(2)]
        ada_used = sem("ada_used")
        ada_made = sem("ada_made")
        x_turned = sem("x_turned")
        x_out = [sem("x_out0"), sem("x_out1")]
        job_done = sem("job_done")
        job_out = [sem("job_out0"), sem("job_out1")]
        stored = sem("stored")
        cmp_stored = sem("cmp_stored")
        xp_in = sem("xp_in")
        q_moved = sem("q_moved")
        xp_turned = sem("xp_turned")
        xp_out = [sem("xp_out0"), sem("xp_out1")]
        hid_p_sum = sem("hid_p_sum")
        hid_p_made = sem("hid_p_made")
        pcomp_sum = sem("pcomp_sum")
        pcomp_made = sem("pcomp_made")
        kt_turned = sem("kt_turned")
        kt_made = [sem("kt_made0"), sem("kt_made1")]
        gates_made = sem("gates_made")

        block = ctx.enter_context(nc.Block())

        @block.gpsimd
        def _(pool):
            own_step = Steps(pool, pool_own)

            def select(out, in_, pattern, base, cm, op, fill):
                own_step.done(pool.affine_select(out=out, in_=in_, compare_op=op, fill=fill, base=base,
                                                 pattern=pattern, channel_multiplier=cm))

            pool.memset(ident[:], 0.0)
            pool.memset(ones[:], 1.0)
            pool.memset(sel_page[:], 1.0)
            pool.memset(sel_prompt[:], 0.0)
            pool.memset(sel_seq[:], 1.0)
            pool.memset(sel_sum_r[:], 0.0)
            pool.memset(sel_rep_r[:], 0.0)
            pool.memset(causal[:], 0.0)
            pool.memset(cmp_mask[:], 0.0)
            pool.memset(cmp_any[:], 1.0)
            own_step.done(pool.memset(win_mask[:], 0.0))
            select(ident[:], ident[:], [[-1, P]], 0, 1, ALU.not_equal, 1.0)
            select(sel_page[:], sel_page[:], [[1, P]], 0, -PPS, ALU.is_ge, 0.0)
            select(sel_page[:], sel_page[:], [[-1, P]], PPS - 1, PPS, ALU.is_ge, 0.0)
            own_step.done(pool.iota(page_i[:, 0:1], pattern=[[0, 1]], base=0, channel_multiplier=1))
            own_step.done(pool.tensor_copy(page_f[:, DB:DB + 1], page_i[:, 0:1]))
            own_step.done(pool.iota(stride_i[:, 0:1], pattern=[[0, 1]], base=0, channel_multiplier=1))
            own_step.done(pool.tensor_copy(stride_f[:, DB:DB + 1], stride_i[:, 0:1]))
            select(sel_prompt[:], sel_prompt[:], [[0, P]], 0, 1, ALU.not_equal, 1.0)
            select(sel_seq[:], sel_seq[:], [[1, NS]], TS, -TS, ALU.is_ge, 0.0)
            select(sel_seq[:], sel_seq[:], [[-1, NS]], -1, TS, ALU.is_ge, 0.0)
            for r in range(R):
                select(sel_sum_r[:], sel_sum_r[:], [[-R * TS, G], [-1, TS]], -r * TS, 1, ALU.not_equal, 1.0)
            select(sel_rep_r[:], sel_rep_r[:], [[-TS, G], [0, R], [-1, TS]], 0, 1, ALU.not_equal, 1.0)
            select(causal[:], causal[:], [[-1, P]], 0, 1, ALU.is_ge, NEG)
            select(cmp_mask[:], cmp_mask[:], [[P, NT], [-ST, PC]], -(SPAN - 1), 1, ALU.is_ge, NEG)
            select(cmp_any[:], cmp_any[:], [[P, NT]], -(SPAN - 1), 1, ALU.is_ge, 0.0)
            select(win_mask[:, 0:WJ], win_mask[:, 0:WJ], [[1, WJ], [0, H], [-1, TS]], -1, WJ, ALU.is_ge, NEG)
            select(win_mask[:, WJ], win_mask[:, WJ], [[0, H], [1, TS]], 0, -1, ALU.is_ge, NEG)
            own_step.done(pool.memset(pool_bd[:], 0.0))
            own_step.done(pool.iota(ramp_i[:], pattern=[[0, PW // P], [1, HIST + 1]], base=1, channel_multiplier=0))
            own_step.done(pool.tensor_copy(ramp[:], ramp_i[:]))
            pool.drain().then_inc(const_made, 1)
            pool.wait_ge(strides_made, 1)
            for b in range(DB):
                if b >= 2:
                    pool.wait_ge(pairs_turned[1], (b - 1) * JP)
                pool.indirect_dma_start(
                    out=caches[b % 2][:].rearrange("p j c -> p (j c)"), out_offset=None, in_=cmp_rows,
                    in_offset=bass.IndirectOffsetOnAxis(ap=stride_i[:, b:b + 1], axis=0),
                ).then_inc(cache_in[b % 2], 16)

            def gather_selection(b):
                pool.indirect_dma_start(
                    out=caches[b % 2][:].rearrange("p j c -> p (j c)"), out_offset=None, in_=slc_rows,
                    in_offset=bass.IndirectOffsetOnAxis(ap=stride_i[:, b:b + 1], axis=0),
                ).then_inc(seq_in[b % 2], 16)

            for b in range(2):
                pool.wait_ge(pairs_turned[1], (DB - 1 + b) * JP)
                gather_selection(b)
            for b in range(2):
                pool.wait_ge(seq_in[b], 16)
            pool.wait_ge(xp_turned, 2 * JP)
            pool.wait_ge(pcomp_made, 1)
            for a in sums:
                pool.memset(a[:, :, 0:PAD], 0.0)
            own_step.done(pool.tensor_copy(sums[0][:, :, PAD:PAD + 1], uT[:, :, 0:1]))
            own_step.done(pool.tensor_tensor(sums[0][:, :, PAD + 1:], uT[:, :, 1:], uT[:, :, 0:T - 1], ALU.add))
            own_step.done(pool.tensor_tensor(seq_sums[0][:, :, :, 1:], u_seq[:, :, :, 1:],
                                             u_seq[:, :, :, 0:HIST + TS - 1], ALU.add))

            def double(dst, src, parts, m, step):
                pool.tensor_tensor(sums[dst][parts, m, PAD:], sums[src][parts, m, PAD:],
                                   sums[src][parts, m, PAD - step:PAD + T - step], ALU.add)
                first = 2 * step - 1
                own_step.done(pool.tensor_tensor(seq_sums[dst][parts, m, :, first:], seq_sums[src][parts, m, :, first:],
                                                 seq_sums[src][parts, m, :, first - step:HIST + TS - step], ALU.add))

            low, high, whole = slice(0, d), slice(d, P), slice(0, P)
            double(1, 0, high, 0, 2)
            double(1, 0, whole, 1, 2)
            double(0, 1, whole, 1, 4)
            double(1, 0, high, 1, 8)
            for n, w in enumerate(POOL_WINDOWS):
                m, parts = n // 2, (low, high)[n % 2]
                a, b = sums[n % 2][parts, m, PAD:], seq_sums[n % 2][parts, m, :, HIST:]
                pool.tensor_scalar(b, b, 1.0 / w, None, ALU.mult)
                own_step.done(pool.tensor_scalar(a, a, 1.0 / w, None, ALU.mult))
            for n in range(len(POOL_WINDOWS)):
                m, parts = n // 2, (low, high)[n % 2]
                a = sums[n % 2][parts, m, PAD:PAD + HIST + 1]
                own_step.done(pool.tensor_tensor(a, a, ramp[parts, m], ALU.mult))
            for n in range(len(POOL_WINDOWS)):
                m, parts = n // 2, (low, high)[n % 2]
                u = uT[parts, m]
                pool.tensor_tensor(u, sums[n % 2][parts, m, PAD:], u, ALU.subtract)
                last = pool.tensor_tensor(mix_seq[parts, m].rearrange("p (b t) -> p b t", t=TS),
                                          seq_sums[n % 2][parts, m, :, HIST:], u_seq[parts, m, :, HIST:], ALU.subtract)
            pool.drain().then_inc(mixed, 1)
            for b in range(2, DB):
                pool.wait_ge(seq_values, b + 1)
                gather_selection(b)

        N_STORED = 1 + 2 * (DB + 1) + 1 + 1 + DB + 1

        @block.sync
        def _(sp):
            def store_y(t):
                rows, y = ((P, y_prompt[0, t * P:(t + 1) * P]) if t < NT else
                           (NS, y_sample.rearrange("b t c -> (b t) c")))
                sp.wait_ge(y_made, t + 1)
                sp.dma_start(y, y_rows[t % 2][0:rows]).then_inc(y_stored[t % 2], 16)

            def vec_load(out, in_):
                sp.dma_start(out, in_).then_inc(vec_in, 16)

            sp.wait_ge(const_made, 1)
            sp.dma_start(page_i[:], page_table.rearrange("b i -> i b"), allow_slow_non_contiguous=True).then_inc(vec_in, 16)
            vec_load(c_rows[0:1, :], c_prompt)
            vec_load(c_rows[1:NB, :], c_sample)
            r = 0
            for src, n in ((b_ada, 3 * KC), (norm_w, KC), (gn_pool, PW // P), (gn_nsa, NW // P)):
                vec_load(vec[r:r + n, :], src.rearrange("l (n p) -> (l n) p", p=P))
                r += n
            pe_rows = phi_pe.rearrange("l (c j) k d -> k (l c) j d", j=2)
            for k in range(2):
                vec_load(vec[r + k * 2 * JP:r + (k + 1) * 2 * JP, :].rearrange("c (j d) -> c j d", j=2), pe_rows[k])
            w1_rows = phi_w1.rearrange("l (c j) k d h -> j k d (l c) h", j=2)
            for j in range(2):
                for k in range(2):
                    sp.dma_start(w1[j * d:(j + 1) * d, :, k, :], w1_rows[j, k]).then_inc(phi_in, 16)
            sp.dma_start(w2[:], phi_w2.rearrange("l k h d -> h (l k) d")).then_inc(phi_in, 16)
            for n in range(len(POOL_WINDOWS)):
                a, b = n % 2 * d, n // 2
                sp.dma_start(pool_bd[a:a + d, b, a:a + d], pool_w[0, n]).then_inc(mix_in, 16)
            sp.dma_start(scale_row[:], pool_scale[0:1, :].to_broadcast([P, PW])).then_inc(mix_in, 16)
            sp.dma_start(hist_rows[:], state_pool[0].rearrange("b h c -> (b h) c")).then_inc(mix_in, 16)
            sp.dma_start(x_rows[:, 0:NT, :], x_prompt[0].rearrange("(t p) c -> p t c", p=P)).then_inc(x_in, 16)
            sp.dma_start(x_rows[0:NS, NT, :], x_sample.rearrange("b t c -> (b t) c")).then_inc(x_in, 16)
            n_ada = 3 * D // 512
            for n in range(n_ada + len(IN_BLOCKS)):
                if n >= 2:
                    if n - 2 < n_ada:
                        sp.wait_ge(ada_used, n - 1)
                    else:
                        sp.wait_ge(job_done, block_jobs[n - 2 - n_ada])
                c0, width = (n * 512, 512) if n < n_ada else IN_BLOCKS[n - n_ada]
                src = (w_ada if n < n_ada else w_in)[0, :, c0:c0 + width]
                sp.dma_start(wcols[n % 2][:, :, 0:width], src.rearrange("(c p) n -> p c n", p=P)).then_inc(wcols_in[n % 2], 16)
                if n - n_ada == 3:
                    sp.wait_ge(job_out[1], by[first_job[1] - 1][1])
                    sp.dma_start(new_cmp_p[0, 0].rearrange("(t p) k g d -> p t (k g d)", p=P),
                                 cmp_new[:, 0:NT, :]).then_inc(cmp_stored, 16)
                    sp.dma_start(new_cmp_s[0].rearrange("b t k g d -> (b t) (k g d)"),
                                 cmp_new[0:NS, NT, :]).then_inc(stored, 16)
            sp.wait_ge(job_out[1], by[first_job[3] - 1][1])
            for n, (prompt, sample) in enumerate(((new_slc_p, new_slc_s[0]), (new_win_p, new_win_s[0, :, WIN - TS:]))):
                sp.dma_start(prompt[0, 0].rearrange("(t p) k g d -> p t (k g d)", p=P),
                             kv[:, 0:NT, n * KV:(n + 1) * KV]).then_inc(stored, 16)
                for b in range(DB):
                    sp.dma_start(sample[b].rearrange("t k g d -> t (k g d)"),
                                 kv[b * TS:(b + 1) * TS, NT, n * KV:(n + 1) * KV]).then_inc(stored, 16)
            sp.dma_start(new_win_s[0, :, 0:WIN - TS].rearrange("b t k g d -> b (t k g d)"),
                         state_win_kv[0, :, TS:WIN].rearrange("b t k g d -> b (t k g d)")).then_inc(stored, 16)
            sp.wait_ge(cmp_stored, 16)
            sp.wait_ge(job_done, block_jobs[-1])
            sp.dma_start(xp[:].rearrange("p j c -> p (j c)"),
                         new_cmp_p[0, 0].rearrange("(s j) k g d -> s (j k g d)", j=ST)).then_inc(xp_in, 16)
            sp.wait_ge(job_out[1], by[first_job[5] - 1][1] if by[first_job[5] - 1][0] == 1 else count[1])
            for to in range(2):
                for fr in range(2):
                    sp.dma_start(q_heads[to * d:(to + 1) * d, fr:H:2, :], qS[fr * d:(fr + 1) * d, :, :]).then_inc(q_moved, 16)
            sp.wait_ge(u_last_out, 1)
            sp.dma_start(new_pool_p[0, 0], u_last[0:HIST, 0, :]).then_inc(stored, 16)
            for b in range(DB):
                sp.dma_start(new_pool_s[0, b, HIST - TS:], u_last[b * TS:(b + 1) * TS, 1, :]).then_inc(stored, 16)
            sp.dma_start(new_pool_s[0, :, 0:HIST - TS], state_pool[0, :, TS:]).then_inc(stored, 16)
            sp.wait_ge(xp_turned, 2 * JP)
            with sp.Fori(0, G) as g:
                for r in range(R):
                    sp.wait_ge(scores, g * (UNITS * R) + (UNITS * r + UNITS))
                    sp.dma_start(q_head[r % 2][:], qT[r % 2 * d:(r % 2 + 1) * d, bass.ds(g * (R // 2) + r // 2, 1), :]
                                 .rearrange("p a t -> p (a t)")).then_inc(q_in[r % 2], 16)
            sp.wait_ge(gates_made, 1)
            sp.dma_start(gate_dram, gates[0:NS, NT, :]).then_inc(gates_stored, 16)
            sp.wait_ge(gates_stored, 16)
            for h in range(H):
                sp.dma_start(gate_rows[h * TS:(h + 1) * TS], gate_dram[:, 3 * h:3 * h + 3]
                             .rearrange("(b t) a -> t b a", t=TS)).then_inc(gates_in, 16)
            sp.wait_ge(mixed, 1)
            sp.wait_ge(stored, 16 * N_STORED)
            def load_window(b, u):
                sp.dma_start(win_rows[u][:].rearrange("p j c -> p (j c)"),
                             state_win_kv[0, bass.ds(b, 1)].rearrange("b (p j) k g d -> (b p) (j k g d)", j=WJ))\
                    .then_inc(win_in[u], 16)
                for n, rows in enumerate((new_slc_s[0], new_win_s[0, :, WIN - TS:])):
                    sp.dma_start(new_v[u][:, n, :], rows[bass.ds(b, 1), :, 1].rearrange("b t g d -> (b t) (g d)"))\
                        .then_inc(win_in[u], 16)

            def store_out(b):
                sp.wait_ge(out_made, b + 1)
                sp.dma_start(out_dram[bass.ds(b, 1)].rearrange("b s c -> (b s) c"), out_rows[:]).then_inc(out_stored, 16)

            for u in range(2):
                load_window(u, u)
            sp.wait_ge(values_out, 2 + G * R * UNITS)
            sp.dma_start(w_o[:], w_out[0].rearrange("(c p) n -> p c n", p=P)).then_inc(w_o_in, 16)
            with sp.Fori(0, DB // 2 - 1) as i:
                for u in range(2):
                    store_out(i * 2 + u)
                    load_window(i * 2 + u + 2, u)
            for b in range(DB - 2, DB):
                store_out(b)
            sp.wait_ge(out_stored, 16 * DB)
            for b in range(DB):
                sp.dma_start(nsa[b * TS:(b + 1) * TS, NT, :].rearrange("t (h c) -> t h c", c=d),
                             out_dram[b].rearrange("(h t) c -> t h c", t=TS)).then_inc(nsa_in, 16)
            sp.dma_start(norm_row[:], final_norm.rearrange("(a n) -> a n", a=1).to_broadcast([P, D])).then_inc(norm_in, 16)
            for t in range(NT + 1):
                rows, x = ((P, x_prompt[0, t * P:(t + 1) * P]) if t < NT else
                           (NS, x_sample.rearrange("b t c -> (b t) c")))
                if t >= 2:
                    sp.wait_ge(y_made, t - 1)
                sp.dma_start(x_again[t % 2][0:rows], x).then_inc(x_again_in[t % 2], 16)
                if t >= 1:
                    store_y(t - 1)
            store_y(NT)
            for u in range(2):
                sp.wait_ge(y_stored[u], 16 * ((NT + 2 - u) // 2))

        @block.tensor
        def _(pe):
            pe.wait_ge(const_made, 1)
            pe.wait_ge(vec_in, 16 * 9)
            pe.transpose(ps[:, 0, 0:NVEC], vec[:], ident[0:NVEC, 0:NVEC]).then_inc(turned_small, 1)
            pe.wait_ge(page_cast, 1)
            pe.matmul(ps[:, 1, 0:DB + 1], sel_page[:], page_f[:], start=True, stop=True).then_inc(turned_small, 1)
            pe.wait_ge(silu_c, 1)
            for c in range(KC):
                last = pe.transpose(ps[:, 2, c * NB:(c + 1) * NB], c_silu[:, c * P:(c + 1) * P], ident[0:NB, 0:NB])
            last.then_inc(turned_small, 1)
            pe.wait_ge(mix_in, 16 * 6)
            for m in range(PW // P):
                last = pe.transpose(ps[:, 4, m * DB * HIST:(m + 1) * DB * HIST], hist_rows[:, m * P:(m + 1) * P],
                                    ident[0:DB * HIST, 0:DB * HIST])
            last.then_inc(turned_small, 1)
            pe.wait_ge(vec_made, 1)
            pe.wait_ge(phi_in, 16 * 5)
            pe0 = 5 * KC
            for k in range(2):
                for c in range(2 * JP):
                    last = pe.matmul(ps[:, 3, k:k + 1], w1[:, c, k, :],
                                     vec_t[:, pe0 + k * 2 * JP + c:pe0 + k * 2 * JP + c + 1],
                                     start=(c == 0), stop=(c == 2 * JP - 1))
            last.then_inc(pe_sum, 1)
            pe.wait_ge(pe_bias_made, 1)
            with pe.Fori(0, DB // 2) as i:
                for u in range(2):
                    b = i * 2 + u
                    pe.wait_ge(cache_in[u], i * 16 + 16)
                    for s in range(JP + 1):
                        if s < JP:
                            n = i * (2 * JP) + (u * JP + s)
                            for j in range(2):
                                bank = 2 * j + s % 2
                                pe.wait_ge(pairs_out[j], n + 1)
                                for c in range(KV // P):
                                    last = pe.transpose(ps[:, bank, c * P:(c + 1) * P],
                                                        caches[u][:, 2 * s + j, c * P:(c + 1) * P], ident[:])
                                last.then_inc(pairs_turned[j], 1)
                        if s == 0:
                            pe.wait_ge(hidden, b * 2 + 1)
                        if s > 0:
                            n = i * (2 * JP) + (u * JP + s - 1)
                            for j in range(2):
                                pe.wait_ge(pairs_out[j], n + 3)
                            for k in range(2):
                                for m in range(2):
                                    last = pe.matmul(ps[:, 4 + k, 0:G * NC].rearrange("p (g n) -> p g n", g=G),
                                                     w1[:, m * JP + s - 1, k, :],
                                                     xt[(s - 1) % NXT][:, k * G:(k + 1) * G, m:m + NC],
                                                     start=(s == 1 and m == 0), stop=(s == JP and m == 1))
                            last.then_inc(pairs_used, 1)
                    pe.wait_ge(hidden, b * 2 + 3)
                    pe.wait_ge(comp_k_out, b + 1)
                    pe.wait_ge(comp_v_out, b + 1)
                    pe.matmul(ps[0:d, 6, 0:G * NC], w2[:, 0, :], hid[:, 0].rearrange("p g n -> p (g n)"),
                              start=True, stop=True)
                    for g in range(G):
                        last = pe.matmul(ps[0:NC, 7, g * d:(g + 1) * d], hid[:, 1, g, :], w2[:, 1, :],
                                         start=True, stop=True)
                    last.then_inc(comp_sum, 1)
            pe.wait_ge(cs_made, 1)
            for e in range(2):
                pe.wait_ge(pairs_out[e], DB * JP + 2)
            n_ada = 3 * D // 512
            for n in range(n_ada):
                pe.wait_ge(wcols_in[n % 2], 16 * (n // 2 + 1))
                for q in range(4):
                    m = n * 4 + q
                    for c in range(KC):
                        last = pe.matmul(ps[:, 0, m * NB:(m + 1) * NB], wcols[n % 2][:, c, q * P:(q + 1) * P],
                                         cs_t[:, c, :], start=(c == 0), stop=(c == KC - 1))
                last.then_inc(ada_used, 1)
            pe.wait_ge(xhat_made, 1)
            for n in range(2 * (NT + 1)):
                t, half = n // 2, n % 2
                rows = P if t < NT else NS
                if n >= 4:
                    pe.wait_ge(x_out[1 - half], n // 2 - 1)
                for c in range(4):
                    ch = half * 4 + c
                    last = pe.transpose(ps[:, 1 + n % 4, c * rows:(c + 1) * rows],
                                        x_rows[0:rows, t, ch * P:(ch + 1) * P], ident[0:rows, 0:rows])
                last.then_inc(x_turned, 1)
            pe.wait_ge(x_out[0], NT)
            pe.wait_ge(x_out[1], NT + 2)
            pe.wait_ge(hidden, 1 + 2 * DB)
            pe.wait_ge(comp_k_out, 1 + DB)
            pe.wait_ge(comp_v_out, 1 + DB)
            for j, (n, turned, col, width, t, what, _) in enumerate(jobs):
                if j == first_job[n]:
                    pe.wait_ge(wcols_in[(n + n_ada) % 2], 16 * ((n + n_ada) // 2 + 1))
                if j >= 8:
                    pe.wait_ge(job_out[by[j - 8][0]], by[j - 8][1])
                w = wcols[(n + n_ada) % 2]
                for c in range(KC):
                    flags = dict(start=(c == 0), stop=(c == KC - 1))
                    if turned:
                        rows = slice(0, T) if what == "prompt" else slice(T, T + NS)
                        last = pe.matmul(ps[:, j % 8, 0:rows.stop - rows.start], w[:, c, col:col + P], hT[:, c, rows], **flags)
                    else:
                        rows = P if t < NT else NS
                        last = pe.matmul(ps[0:rows, j % 8, 0:width], hT[:, c, t * P:t * P + rows],
                                         w[:, c, col:col + width], **flags)
                last.then_inc(job_done, 1)
            for e in range(2):
                pe.wait_ge(job_out[e], count[e])
            for m in range(PW // P):
                pe.transpose(ps[0:HIST, 6, m * P:(m + 1) * P], uT[:, m, T - HIST:], ident[:])
                last = pe.transpose(ps[0:NS, 6, PW + m * P:PW + (m + 1) * P], uS[:, m, :], ident[:])
            last.then_inc(u_last_turned, 1)
            for n in range(2 * G):
                s, g = divmod(n, G)
                for t in range(NT):
                    last = pe.transpose(ps[0:d, n, t * P:(t + 1) * P], kv[:, t, s * KV + g * d:s * KV + (g + 1) * d], ident[:])
                last.then_inc(kt_turned, 1)
            pe.wait_ge(u_last_out, 1)
            pe.wait_ge(xp_in, 16)
            for s in range(JP):
                for j in range(2):
                    n = 2 * s + j
                    if n >= 2:
                        pe.wait_ge(xp_out[j], s)
                    for c in range(KV // P):
                        last = pe.transpose(ps[:, 6 + j, c * PSTR:(c + 1) * PSTR], xp[:, n, c * P:(c + 1) * P],
                                            ident[0:PSTR, 0:PSTR])
                    last.then_inc(xp_turned, 1)
            for e in range(2):
                pe.wait_ge(kt_made[e], G)
                pe.wait_ge(xp_out[e], JP)
            for k in range(2):
                for c in range(JP):
                    for m in range(2):
                        last = pe.matmul(ps[:, k, 0:G * PC].rearrange("p (g n) -> p g n", g=G), w1[:, m * JP + c, k, :],
                                         xpt[:, c, k * G:(k + 1) * G, m:m + PC],
                                         start=(c == 0 and m == 0), stop=(c == JP - 1 and m == 1))
                last.then_inc(hid_p_sum, 1)
            pe.wait_ge(hid_p_made, 2)
            pe.matmul(ps[0:d, 2, 0:G * PC], w2[:, 0, :], hid_p[:, 0].rearrange("p g n -> p (g n)"),
                      start=True, stop=True)
            for g in range(G):
                last = pe.matmul(ps[0:PC, 4, g * d:(g + 1) * d], hid_p[:, 1, g, :], w2[:, 1, :], start=True, stop=True)
            last.then_inc(pcomp_sum, 1)
            pe.wait_ge(pcomp_made, 1)
            N = R * UNITS
            with pe.Fori(0, G) as g:
                for step in range(N + 2):
                    if step < N:
                        r, t = divmod(step, UNITS)
                        t -= 1
                        q = q_head[r % 2]
                        pe.wait_ge(probs_made, g * N + (step + 1))
                        if t < 0:
                            pe.wait_ge(q_in[r % 2], g * (16 * R // 2) + 16 * (r // 2 + 1))
                        pe.sem_inc(passed, 1)
                        if t < 0:
                            for tt in range(NT):
                                last = pe.matmul(ps[:, step % 2 * 2, tt * PC:(tt + 1) * PC], q[:, tt * P:(tt + 1) * P],
                                                 pcomp_k[:, bass.ds(g * PC, PC)], start=True, stop=True)
                        else:
                            for s in range(2):
                                last = pe.matmul(ps[:, step % 2 * 2 + s, 0:(t + 1) * P], q[:, t * P:(t + 1) * P],
                                                 kT[:, s, bass.ds(g, 1), 0:(t + 1) * P].rearrange("p a n -> p (a n)"),
                                                 start=True, stop=True)
                        last.then_inc(scores, 1)
                    if 1 <= step <= N:
                        n = step - 1
                        t = n % UNITS - 1
                        pe.wait_ge(probs_made, g * N + (n + 3))
                        for e in range(2):
                            pe.wait_ge(probs_out[e], g * N + (n + 1))
                        if t < 0:
                            for tt in range(NT):
                                last = pe.transpose(ps[0:PC, 4 + tt // 2, tt % 2 * P:(tt % 2 + 1) * P],
                                                    cprobs[n % 2][:, tt, :], ident[:])
                        else:
                            for s in range(2):
                                for k in range(t + 1):
                                    last = pe.transpose(ps[:, 4 + s, k * P:(k + 1) * P],
                                                        probs[n % 2][:, s, k * P:(k + 1) * P], ident[:])
                        last.then_inc(probs_turned, 1)
                    if step >= 2:
                        n = step - 2
                        t = n % UNITS - 1
                        for e in range(2):
                            pe.wait_ge(probs_out[e], g * N + (n + 2))
                        pe.wait_ge(values_out, g * N + (n + 1))
                        pe.sem_inc(passed, 1)
                        bank = ps[:, 6 + n % 2, :]
                        if t < 0:
                            for tt in range(NT):
                                last = pe.matmul(bank[:, tt * d:(tt + 1) * d], cprobs_t[n % 2][:, tt, :],
                                                 pcomp_v[0:PC, bass.ds(g * d, d)], start=True, stop=True)
                        else:
                            for s in range(2):
                                for k in range(t + 1):
                                    last = pe.matmul(bank[:, s * d:(s + 1) * d], probs_t[n % 2][:, s, k, :],
                                                     kv[:, k, bass.ds(g * d + (s * KV + KV // 2), d)],
                                                     start=(k == 0), stop=(k == t))
                        last.then_inc(values, 1)
            pe.wait_ge(values_out, 2 + G * N)
            pe.wait_ge(probs_out[0], 1 + G * N)
            pe.wait_ge(probs_out[1], 1 + G * N)
            for n in range(2):
                pe.transpose(ps[:, 7, n * NS:(n + 1) * NS], kv[0:NS, NT, n * KV:n * KV + P], ident[0:NS, 0:NS])
                last = pe.transpose(ps[0:d, 7, (2 + n) * NS:(3 + n) * NS], kv[0:NS, NT, n * KV + P:n * KV + P + d],
                                    ident[0:NS, 0:NS])
            last.then_inc(new_turned, 1)
            pe.wait_ge(new_t_made, 1)
            pe.wait_ge(mixed, 1)
            KT_TURNS = (ST + WJ) // 4 * 2
            with pe.Fori(0, DB // 2) as i:
                for u in range(2):
                    b = i * 2 + u
                    pe.wait_ge(staged, b + 1)
                    pe.sem_inc(passed, 1)
                    for g in range(G):
                        lhs = (q01[0:d, 0:R * TS], q01[d:P, R * TS:], q2[0:d, 0:R * TS])[g]
                        keys = (ckeys[0:d, 0, 0:NC], ckeys[d:P, 0, 0:NC], ckeys[0:d, 1, 0:NC])[g]
                        last = pe.matmul(ps[g * R * TS:(g + 1) * R * TS, 7, 0:NC], lhs, keys, start=True, stop=True)
                    last.then_inc(cscores, 1)
                    pe.wait_ge(seq_in[u], i * 16 + 16)
                    pe.wait_ge(win_in[u], i * 48 + 48)
                    for n in range(KT_TURNS):
                        j4, two = divmod(n, 2)
                        rows, j0 = (caches[u], 4 * j4) if j4 < ST // 4 else (win_rows[u], 0)
                        pe.wait_ge(keys_out[two], b * (KT_TURNS // 2) + (j4 + 1))
                        if two:
                            pe.sem_inc(passed, 1)
                        for j in range(4):
                            if two:
                                last = pe.transpose(ps[0:d, 6, j * P:(j + 1) * P], rows[:, j0 + j, P:P + d], ident[:])
                            else:
                                last = pe.transpose(ps[:, 5, j * P:(j + 1) * P], rows[:, j0 + j, 0:P], ident[:])
                        last.then_inc(keys_turned, 1)
                    pe.wait_ge(cp_made, b + 1)
                    pe.transpose(ps[0:NC, 7, P:P + GR], cp[:], ident[0:GR, 0:GR])
                    pe.matmul(ps[0:G * TS, 7, 2 * P:2 * P + NC], sel_sum_r[:].rearrange("p g t -> p (g t)"), cp[:],
                              start=True, stop=True).then_inc(cp_turned, 1)
                    for e in range(2):
                        pe.wait_ge(keys_out[e], (b + 1) * (KT_TURNS // 2) + 1)
                    pe.wait_ge(shifted, b + 1)
                    for j2 in range((ST + WJ) // 2):
                        win = j2 >= ST // 2
                        jj = j2 - ST // 2 if win else j2
                        bank = ps[:, 4 if win else jj // 2, :]
                        at0 = 2 * jj * GR if win else jj % 2 * 2 * GR
                        k01, k2 = (wkey_t01, wkey_t2) if win else (key_t01, key_t2)
                        for a in range(2):
                            pe.matmul(bank[:, at0 + a * GR:at0 + a * GR + 2 * R * TS], k01[:, 2 * jj + a, :], q01[:],
                                      start=True, stop=True)
                        pe.matmul(bank[:, at0:at0 + 2 * GR].rearrange("p (a c) -> p a c", a=2)[:, :, 2 * R * TS:],
                                  k2[:, jj, :], q2[:], start=True, stop=True)
                    for n in range(2):
                        bank = ps[:, 3 + n, 4 * GR:5 * GR]
                        pe.matmul(bank[:, 0:2 * R * TS], new_pad01[:, n, :], q01[:], start=True, stop=True)
                        last = pe.matmul(bank[:, 2 * R * TS:], new_pad2[:, n, :], q2[0:d, 0:R * TS], start=True, stop=True)
                    last.then_inc(seq_scores, 1)
                    pe.wait_ge(cp_out, b + 1)
                    pe.sem_inc(passed, 1)
                    pe.matmul(ps[0:GR, 7, 0:G * d], cp_t[:], comp_v[0:NC, bass.ds(b, 1), :].rearrange("p a c -> p (a c)"),
                              start=True, stop=True).then_inc(cvalues, 1)
                    pe.wait_ge(chosen_made, b + 1)
                    pe.matmul(ps[:, 6, 0:GR], chosen[:], sel_rep_r[:].rearrange("p g r t -> p (g r t)"),
                              start=True, stop=True).then_inc(bias_sum, 1)
                    pe.wait_ge(peaks_made, b + 1)
                    for n in range(2):
                        last = pe.transpose(ps[0:GR, 5, n * P:(n + 1) * P], peak2[:, n, :], ident[:])
                    last.then_inc(peaks_turned, 1)
                    pe.wait_ge(diag_made, b + 1)
                    pe.matmul(ps[:, 6, 0:2 * GR], ones[0:GR, :], peak_diag[:].rearrange("p a c -> p (a c)"),
                              start=True, stop=True).then_inc(peaks_spread, 1)
                    pe.wait_ge(sums_made, b + 1)
                    pe.wait_ge(cvalues_out, b + 1)
                    for n in range(2):
                        pe.matmul(ps[0:GR, 7, 2 * G * d + n:2 * G * d + n + 1], sum2[:, n, :], ones[:, 0:1],
                                  start=True, stop=True)
                    for j in range(ST):
                        pe.matmul(ps[0:GR, 7, 0:G * d], sc[:, j, :], caches[u][:, j, KV // 2:], start=(j == 0), stop=False)
                    pe.matmul(ps[0:GR, 7, 0:G * d], sc[0:TS, ST, :], new_v[u][:, 0, :], start=False, stop=True)
                    for j in range(WJ):
                        pe.matmul(ps[0:GR, 7, G * d:2 * G * d], sc[:, SL + j, :], win_rows[u][:, j, KV // 2:],
                                  start=(j == 0), stop=False)
                    pe.matmul(ps[0:GR, 7, G * d:2 * G * d], sc[0:TS, SL + WJ, :], new_v[u][:, 1, :],
                              start=False, stop=True).then_inc(seq_values, 1)
                    pe.wait_ge(out_made, b + 1)
            for c in range(KC):
                last = pe.transpose(ps[0:NB, c // 4, c % 4 * P:(c % 4 + 1) * P], ada_t[:, 2 * KC + c, :], ident[:])
            last.then_inc(gate_turned, 1)
            pe.wait_ge(gate_copied, 1)
            for n in range(2):
                for s in range(2):
                    rows, sel = ((P, sel_prompt), (NS, sel_seq))[s]
                    last = pe.matmul(ps[0:rows, 2 + 2 * s + n, :], sel[:], gate_bc[:, n * 512:(n + 1) * 512],
                                     start=True, stop=True)
            last.then_inc(gate_spread, 1)
            pe.wait_ge(nsa_in, 16 * DB)
            pe.wait_ge(w_o_in, 16)
            for t in range(NT + 2):
                if t <= NT:
                    rows = P if t < NT else NS
                    if t >= 1:
                        pe.wait_ge(mixed_made, t)
                    if t == 0:
                        pe.wait_ge(gate_made, 1)
                    for m in range(PW // P):
                        mix = uT[:, m, t * P:(t + 1) * P] if t < NT else mix_seq[:, m, :]
                        last = pe.matmul(ps[0:rows, 0, m * P:(m + 1) * P], mix, pool_bd[:, m, :], start=True, stop=True)
                    last.then_inc(pool_values, 1)
                if t >= 1:
                    n = t - 1
                    rows = P if n < NT else NS
                    pe.wait_ge(mixed_made, n + 1)
                    for half in range(2):
                        if n >= 1:
                            pe.wait_ge(mixT_made[half], n)
                        for c in range(4):
                            ch = half * 4 + c
                            last = pe.transpose(ps[:, 1 + half, c * rows:(c + 1) * rows],
                                                mixed_rows[n % 2][0:rows, ch * P:(ch + 1) * P], ident[0:rows, 0:rows])
                        last.then_inc(mixed_turned, 1)
                    for half in range(2):
                        pe.wait_ge(mixT_made[half], n + 1)
                    if n >= 2:
                        pe.wait_ge(y_sum, n - 1)
                    for half in range(2):
                        for c in range(KC):
                            last = pe.matmul(ps[0:rows, 3 + n % 2 * 2 + half, :], mixT[n % 2][:, c, 0:rows],
                                             w_o[:, c, half * 512:(half + 1) * 512], start=(c == 0), stop=(c == KC - 1))
                    last.then_inc(projected, 1)

        def copy_pairs(eng, copy, j, n, s):
            eng.wait_ge(pairs_turned[j], n + 1)
            eng.wait_ge(pairs_used, n + 1)
            bank = ps[:, 2 * j + s % 2, 0:KV].rearrange("p (c n) -> p c n", n=P)
            slot = xt[s % NXT][:].rearrange("p (c h) n -> p c h n", h=2)
            copy(slot[j * d:(j + 1) * d, :, 0, :], bank[0:d])
            copy(slot[j * d:(j + 1) * d, :, 1, :], bank[d:P]).then_inc(pairs_out[j], 1)

        def copy_jobs(eng, e):
            copy = eng.copy if e == 0 else eng.tensor_copy
            for j, (n, turned, col, width, t, what, c) in enumerate(jobs):
                if by[j][0] != e:
                    continue
                eng.wait_ge(job_done, j + 1)
                bank = ps[:, j % 8, :]
                rows = P if t is None or t < NT else NS
                if turned and c < PW:
                    if what == "prompt":
                        last = copy(uT[:, c // P, :], bank[:, 0:T])
                    else:
                        copy(uS[:, c // P, :], bank[:, 0:NS])
                        last = copy(u_seq[:, c // P, :, HIST:], bank[:, 0:NS].rearrange("p (b t) -> p b t", t=TS))
                elif turned:
                    last = copy((qT if what == "prompt" else qS)[:, (c - C_Q) // P, :],
                                bank[:, 0:T if what == "prompt" else NS])
                elif n == 0:
                    last = copy(cmp_new[0:rows, t, :], bank[0:rows, 0:KV])
                elif n < 3:
                    last = copy(kv[0:rows, t, (n - 1) * KV:(n - 1) * KV + width], bank[0:rows, 0:width])
                else:
                    c_gate = c - PW if c < C_Q else c - C_ZN + PW
                    last = eng.activation(z_gate[0:rows, t, c_gate:c_gate + width], bank[0:rows, 0:width], ACT.Silu)
                last.then_inc(job_out[e], 1)

        def copy_keys(eng, copy, e):
            eng.wait_ge(u_last_turned, 1)
            eng.wait_ge(cmp_stored, 16)
            eng.wait_ge(stored, 16)
            eng.wait_ge(q_moved, 64)
            for n in range(2 * G):
                if n % 2 != e:
                    continue
                s, g = divmod(n, G)
                eng.wait_ge(kt_turned, n + 1)
                copy(kT[:, s, g, :], ps[0:d, n, :]).then_inc(kt_made[e], 1)

        def copy_prompt_pairs(eng, copy, j):
            for s in range(JP):
                eng.wait_ge(xp_turned, 2 * s + j + 1)
                bank = ps[:, 6 + j, 0:KV // P * PSTR].rearrange("p (c n) -> p c n", n=PSTR)
                slot = xpt[:, s].rearrange("p (c h) n -> p c h n", h=2)
                copy(slot[j * d:(j + 1) * d, :, 0, :], bank[0:d])
                copy(slot[j * d:(j + 1) * d, :, 1, :], bank[d:P]).then_inc(xp_out[j], 1)

        def copy_key2(eng, b, j4):
            eng.wait_ge(keys_turned, b * ((ST + WJ) // 2) + (2 * j4 + 2))
            bank = ps[0:d, 6, :].rearrange("p (a h n) -> p a h n", h=2, n=P)
            dst = key_t2[:, 2 * j4:2 * j4 + 2, :] if j4 < ST // 4 else wkey_t2[:]
            eng.tensor_copy(dst[0:d], bank[:, :, 0])
            eng.tensor_copy(dst[d:P], bank[:, :, 1]).then_inc(keys_out[1], 1)

        def copy_rows_turned(act, copy):
            with act.Fori(0, DB // 2) as i:
                for u in range(2):
                    b = i * 2 + u
                    act.wait_ge(cpeaks, b + 1)
                    act.activation(cp[:], ps[0:GR, 7, 0:NC], ACT.Exp, bias=cpeak[:, 0:1], scale=SCALE,
                                   accum_out=cpeak[:, 1:2]).then_inc(cexp, 1)
                    for j4 in range((ST + WJ) // 4):
                        act.wait_ge(keys_turned, b * ((ST + WJ) // 2) + (2 * j4 + 1))
                        dst = key_t01[:, 4 * j4:4 * j4 + 4, :] if j4 < ST // 4 else wkey_t01[:]
                        copy(dst.rearrange("p j n -> p (j n)"), ps[:, 5, :]).then_inc(keys_out[0], 1)
                    act.wait_ge(shifted, b + 2)
                    act.activation(sc[:].rearrange("p j c -> p (j c)"), sc[:].rearrange("p j c -> p (j c)"),
                                   ACT.Exp, scale=SCALE).then_inc(seq_exp, 1)

        @block.scalar
        def _(act):
            own_step = Steps(act, act_own)
            act.sem_inc(pairs_out[0], 2)
            act.sem_inc(pairs_used, NXT)
            act.sem_inc(hidden, 1)
            act.sem_inc(keys_out[0], 1)
            act.sem_inc(probs_made, 2)
            act.sem_inc(probs_out[1], 1)
            act.wait_ge(vec_in, 16 * 9)
            act.activation(c_silu[:], c_rows[:], ACT.Silu).then_inc(silu_c, 1)
            act.wait_ge(sumsq_made, 1)
            act.wait_ge(x_in, 32)
            for t in range(NT + 1):
                rows = P if t < NT else NS
                own_step.done(act.activation(x_sq[0:rows], x_rows[0:rows, t, :], ACT.Square,
                                             accum_out=sumsq[0:rows, t:t + 1]))
            act.drain().then_inc(sumsq_made, 1)
            act.wait_ge(ms_made, 1)
            act.sqrt(rstd[:], rstd[:]).then_inc(rstd_root, 1)
            act.wait_ge(pe_bias_made, 1)
            with act.Fori(0, DB // 2) as i:
                for u in range(2):
                    b = i * 2 + u
                    for s in range(JP):
                        copy_pairs(act, act.copy, 0, i * (2 * JP) + (u * JP + s), s)
                    act.wait_ge(pairs_used, i * (2 * JP) + ((u + 1) * JP + NXT))
                    for k in range(2):
                        act.activation(hid[:, k].rearrange("p g n -> p (g n)"), ps[:, 4 + k, 0:G * NC],
                                       ACT.Gelu_apprx_tanh, bias=pe_bias[:, k:k + 1]).then_inc(hidden, 1)
                    act.wait_ge(comp_sum, b + 1)
                    act.copy(comp_v[0:NC, b, :], ps[0:NC, 7, 0:G * d]).then_inc(comp_v_out, 1)
            act.wait_ge(ada_made, 1)
            for t in range(NT):
                act.wait_ge(x_turned, 2 * t + 2)
                for c in range(4):
                    last = act.activation(hT[:, 4 + c, t * P:(t + 1) * P], ps[:, 1 + (2 * t + 1) % 4, c * P:(c + 1) * P],
                                          ACT.Identity, bias=ada_t[:, 4 + c, 0:1], scale=ada_mul[:, 4 + c, 0:1])
                last.then_inc(x_out[0], 1)
            copy_jobs(act, 0)
            copy_keys(act, act.copy, 0)
            act.wait_ge(job_out[1], by[first_job[3] - 1][1])
            act.activation(gates[:, 0:NT], kv[:, 0:NT, 2 * KV:], ACT.Sigmoid)
            act.activation(gates[0:NS, NT], kv[0:NS, NT, 2 * KV:], ACT.Sigmoid).then_inc(gates_made, 1)
            copy_prompt_pairs(act, act.copy, 0)
            for k in range(2):
                act.wait_ge(hid_p_sum, k + 1)
                act.activation(hid_p[:, k].rearrange("p g n -> p (g n)"), ps[:, k, 0:G * PC],
                               ACT.Gelu_apprx_tanh, bias=pe_bias[:, k:k + 1]).then_inc(hid_p_made, 1)
            N = R * UNITS
            with act.Fori(0, G) as g:
                for step in range(N + 1):
                    if step < N:
                        t, u = step % UNITS - 1, step % 2
                        act.wait_ge(peaks, g * N + (step + 1))
                        if t < 0:
                            last = act.activation(cprobs[u][:], cprobs[u][:], ACT.Exp, scale=SCALE)
                        else:
                            for s in range(2):
                                last = act.activation(probs[u][:, s, 0:(t + 1) * P], ps[:, u * 2 + s, 0:(t + 1) * P],
                                                      ACT.Exp, bias=peak[u][:, s:s + 1], scale=SCALE,
                                                      accum_out=total[step % 4][:, s:s + 1])
                        last.then_inc(probs_made, 1)
                    if step >= 1:
                        t, u = (step - 1) % UNITS - 1, (step - 1) % 2
                        act.wait_ge(probs_turned, g * N + step)
                        if t < 0:
                            last = act.copy(cprobs_t[u][:, 2:4, :].rearrange("p a b -> p (a b)"), ps[0:PC, 5, 0:2 * P])
                        else:
                            last = act.copy(probs_t[u][:, 1, 0:t + 1, :].rearrange("p a b -> p (a b)"),
                                            ps[:, 5, 0:(t + 1) * P])
                        last.then_inc(probs_out[1], 1)

            copy_rows_turned(act, act.copy)

            def turned_scaled(n):
                rows = P if n < NT else NS
                act.wait_ge(mixed_turned, 2 * n + 1)
                if n >= 2:
                    act.wait_ge(projected, n - 1)
                for c in range(4):
                    last = act.activation(mixT[n % 2][:, c, 0:rows], ps[:, 1, c * rows:(c + 1) * rows],
                                          ACT.Copy, scale=vec_t[:, 4 * KC + c:4 * KC + c + 1])
                last.then_inc(mixT_made[0], 1)

            act.wait_ge(nsa_in, 16 * DB)
            act.wait_ge(gate_made, 1)
            for t in range(NT + 3):
                if t <= NT:
                    rows = P if t < NT else NS
                    own_step.done(act.activation(osq[0][0:rows, 0:NW], nsa[0:rows, t, :], ACT.Square,
                                                 accum_out=ostat[0:rows, t, 1:2]))
                    act.wait_ge(pool_values, t + 1)
                    act.activation(osq[0][0:rows, 0:PW], ps[0:rows, 0, 0:PW], ACT.Square,
                                   accum_out=ostat[0:rows, t, 0:1]).then_inc(osums, 1)
                    act.wait_ge(omeans, t + 1)
                    act.sqrt(orstd[0:rows, t, 0:2], orstd[0:rows, t, 0:2]).then_inc(oroots, 1)
                if 1 <= t <= NT + 1:
                    turned_scaled(t - 1)
                if t >= 2:
                    n = t - 2
                    rows = P if n < NT else NS
                    act.wait_ge(y_sum, n + 1)
                    own_step.done(act.activation(osq[0][0:rows], y_rows[n % 2][0:rows], ACT.Square,
                                                 accum_out=ostat[0:rows, n, 2:3]))
                    act.sem_inc(ysq, 1)
                    act.wait_ge(ymeans, n + 1)
                    act.sqrt(orstd[0:rows, n, 2:3], orstd[0:rows, n, 2:3]).then_inc(yroots, 1)

        @block.vector
        def _(dve):
            own_step = Steps(dve, dve_own)
            dve.sem_inc(pairs_out[1], 2)
            dve.sem_inc(comp_k_out, 1)
            dve.sem_inc(comp_v_out, 1)
            dve.sem_inc(scores, 2 * UNITS)
            dve.sem_inc(probs_out[0], 1)
            dve.sem_inc(values_out, 2)
            dve.sem_inc(keys_out[1], 1)
            dve.sem_inc(shifted, 1)
            dve.sem_inc(seq_values, 2)
            dve.memset(sumsq[:], 1.0).then_inc(sumsq_made, 1)
            dve.wait_ge(vec_in, 16 * 9)
            dve.wait_ge(const_made, 1)
            dve.tensor_copy(page_f[:, 0:DB], page_i[:]).then_inc(page_cast, 1)
            dve.wait_ge(turned_small, 1)
            dve.tensor_copy(vec_t[:], ps[:, 0, 0:NVEC]).then_inc(vec_made, 1)
            dve.wait_ge(turned_small, 3)
            dve.tensor_copy(cs_t[:].rearrange("p c b -> p (c b)"), ps[:, 2, 0:KC * NB]).then_inc(cs_made, 1)
            for n, w in enumerate(POOL_WINDOWS):
                a = ramp[n % 2 * d:(n % 2 + 1) * d, n // 2]
                own_step.done(dve.tensor_scalar(a, a, float(w), 1.0 / w, ALU.min, ALU.mult))
            dve.reciprocal(ramp[:], ramp[:]).then_inc(ramp_made, 1)
            dve.wait_ge(mix_in, 16 * 6)
            dve.tensor_tensor(pool_bd[:].rearrange("p a b -> p (a b)"), pool_bd[:].rearrange("p a b -> p (a b)"),
                              scale_row[:], ALU.mult).then_inc(mix_made, 1)
            dve.wait_ge(turned_small, 4)
            for m in range(PW // P):
                dve.tensor_copy(u_seq[:, m, :, 0:HIST],
                                ps[:, 4, m * DB * HIST:(m + 1) * DB * HIST].rearrange("p (b h) -> p b h", h=HIST))
            dve.wait_ge(turned_small, 2)
            own_step.done(dve.scalar_tensor_tensor(out=stride_f[:, DB + 1:DB + 2], in0=ps[:, 1, DB:DB + 1],
                                                   scalar=-float(PPS), in1=stride_f[:, DB:DB + 1],
                                                   op0=ALU.mult, op1=ALU.add))
            own_step.done(dve.tensor_scalar(stride_f[:, 0:DB], ps[:, 1, 0:DB], float(PPS), stride_f[:, DB + 1:DB + 2],
                                            ALU.mult, ALU.add))
            dve.tensor_copy(stride_i[:], stride_f[:, 0:DB]).then_inc(strides_made, 1)
            dve.wait_ge(sumsq_made, 2)
            dve.tensor_scalar(rstd[:], sumsq[:], 1.0 / D, EPS, ALU.mult, ALU.add).then_inc(ms_made, 1)
            dve.wait_ge(rstd_root, 1)
            own_step.done(dve.reciprocal(rstd[:], rstd[:]))
            for t in range(NT + 1):
                rows = P if t < NT else NS
                last = dve.tensor_scalar(x_rows[0:rows, t, :], x_rows[0:rows, t, :], rstd[0:rows, t:t + 1], None, ALU.mult)
            last.then_inc(xhat_made, 1)
            dve.wait_ge(pe_sum, 1)
            dve.tensor_copy(pe_bias[:], ps[:, 3, 0:2]).then_inc(pe_bias_made, 1)
            with dve.Fori(0, DB // 2) as i:
                for u in range(2):
                    b = i * 2 + u
                    for s in range(JP):
                        copy_pairs(dve, dve.tensor_copy, 1, i * (2 * JP) + (u * JP + s), s)
                    dve.wait_ge(comp_sum, b + 1)
                    keys = ps[0:d, 6, 0:G * NC].rearrange("p (g n) -> p g n", g=G)
                    dve.tensor_copy(comp_k[0:d, b], keys[:, 0:G:2])
                    dve.tensor_copy(comp_k[d:P, b, 0], keys[:, 1]).then_inc(comp_k_out, 1)
            dve.wait_ge(ada_used, 3 * D // 512)
            own_step.done(dve.tensor_tensor(ada_t[:], ps[:, 0, 0:3 * KC * NB].rearrange("p (c b) -> p c b", b=NB),
                                            vec_t[:, 0:3 * KC].unsqueeze(2).to_broadcast([P, 3 * KC, NB]), ALU.add))
            dve.scalar_tensor_tensor(out=ada_mul[:], in0=ada_t[:, KC:2 * KC, :], scalar=1.0,
                                     in1=vec_t[:, 3 * KC:4 * KC].unsqueeze(2).to_broadcast([P, KC, NB]),
                                     op0=ALU.add, op1=ALU.mult).then_inc(ada_made, 1)
            dve.wait_ge(ada_made, 1)
            for t in range(NT):
                dve.wait_ge(x_turned, 2 * t + 1)
                for c in range(4):
                    last = dve.tensor_scalar(hT[:, c, t * P:(t + 1) * P], ps[:, 1 + 2 * t % 4, c * P:(c + 1) * P],
                                             ada_mul[:, c, 0:1], ada_t[:, c, 0:1], ALU.mult, ALU.add)
                last.then_inc(x_out[1], 1)
            for half in range(2):
                dve.wait_ge(x_turned, 2 * NT + half + 1)
                rows = hT[:, half * 4:half * 4 + 4, T:T + NS].rearrange("p c (b t) -> p c b t", t=TS)
                bank = ps[:, 1 + (2 * NT + half) % 4, 0:4 * NS].rearrange("p (c b t) -> p c b t", b=DB, t=TS)

                def per_seq(a):
                    return a[:, half * 4:half * 4 + 4, 1:NB].unsqueeze(3).to_broadcast([P, 4, DB, TS])

                own_step.done(dve.tensor_tensor(rows, bank, per_seq(ada_mul), ALU.mult))
                dve.tensor_tensor(rows, rows, per_seq(ada_t), ALU.add).then_inc(x_out[1], 1)
            copy_jobs(dve, 1)
            dve.wait_ge(u_last_turned, 1)
            dve.tensor_copy(u_last[0:HIST, 0, :], ps[0:HIST, 6, 0:PW])
            dve.tensor_copy(u_last[:, 1, :], ps[0:NS, 6, PW:]).then_inc(u_last_out, 1)
            copy_keys(dve, dve.tensor_copy, 1)
            copy_prompt_pairs(dve, dve.tensor_copy, 1)
            dve.wait_ge(pcomp_sum, 1)
            dve.tensor_copy(pcomp_k[:], ps[0:d, 2, 0:G * PC])
            dve.tensor_copy(pcomp_v[0:PC], ps[0:PC, 4, 0:G * d]).then_inc(pcomp_made, 1)
            N = R * UNITS
            dve.wait_ge(gates_made, 1)
            with dve.Fori(0, G) as g:
                own_step.enter(g, R * (NT * 6 + 6))
                for step in range(N + 2):
                    if step < N:
                        t, u = step % UNITS - 1, step % 2
                        dve.wait_ge(scores, g * N + (step + 1 + 2 * UNITS))
                        if t < 0:
                            c = cprobs[u][:]
                            own_step.done(dve.tensor_tensor(
                                c, ps[:, u * 2, 0:NT * PC].rearrange("p (t n) -> p t n", n=PC), cmp_mask[:], ALU.add))
                            own_step.done(dve.tensor_reduce(peak[u][:], c, AX, ALU.max))
                            dve.tensor_tensor(c, c, peak[u][:].unsqueeze(2).to_broadcast([P, NT, PC]),
                                              ALU.subtract).then_inc(peaks, 1)
                        else:
                            diag = ps[:, u * 2:u * 2 + 2, t * P:(t + 1) * P]
                            own_step.done(dve.tensor_tensor(diag, diag, causal[:].unsqueeze(1).to_broadcast([P, 2, P]),
                                                            ALU.add))
                            own_step.done(dve.tensor_reduce(peak[u][:, 0:2], ps[:, u * 2:u * 2 + 2, 0:(t + 1) * P],
                                                            AX, ALU.max))
                            dve.tensor_scalar(peak[u][:, 0:2], peak[u][:, 0:2], -SCALE, None, ALU.mult).then_inc(peaks, 1)
                    if 1 <= step <= N:
                        t, u = (step - 1) % UNITS - 1, (step - 1) % 2
                        dve.wait_ge(probs_turned, g * N + step)
                        if t < 0:
                            last = dve.tensor_copy(cprobs_t[u][:, 0:2, :].rearrange("p a b -> p (a b)"),
                                                   ps[0:PC, 4, 0:2 * P])
                        else:
                            last = dve.tensor_copy(probs_t[u][:, 0, 0:t + 1, :].rearrange("p a b -> p (a b)"),
                                                   ps[:, 4, 0:(t + 1) * P])
                        last.then_inc(probs_out[0], 1)
                    if step >= 2:
                        n = step - 2
                        r, t = divmod(n, UNITS)
                        t, u = t - 1, n % 2
                        bank = ps[:, 6 + u, :]
                        if t < 0:
                            own_step.done(dve.tensor_reduce(total[n % 4][:], cprobs[u][:], AX, ALU.add))
                            own_step.done(dve.reciprocal(share[u][:], total[n % 4][:]))
                            own_step.done(dve.tensor_tensor(share[u][:], share[u][:], cmp_any[:], ALU.mult))
                            own_step.done(dve.tensor_tensor(
                                share[u][:], share[u][:],
                                gates[:, 0:NT, bass.ds(g * (3 * R) + 3 * r, 1)].rearrange("p t a -> p (t a)"), ALU.mult))
                            dve.wait_ge(values, g * N + (n + 1))
                            dve.tensor_tensor(nsa[:, 0:NT, bass.ds(g * (R * d) + r * d, d)],
                                              bank[:, 0:NT * d].rearrange("p (t c) -> p t c", c=d),
                                              share[u][:].unsqueeze(2).to_broadcast([P, NT, d]),
                                              ALU.mult).then_inc(values_out, 1)
                        else:
                            own_step.done(dve.reciprocal(share[u][:, 0:2], total[n % 4][:, 0:2]))
                            own_step.done(dve.tensor_tensor(share[u][:, 0:2], share[u][:, 0:2],
                                                            gates[:, t, bass.ds(g * (3 * R) + (3 * r + 1), 2)], ALU.mult))
                            dve.wait_ge(values, g * N + (n + 1))
                            out = nsa[:, t, bass.ds(g * (R * d) + r * d, d)]
                            own_step.done(dve.scalar_tensor_tensor(out=out, in0=bank[:, 0:d], scalar=share[u][:, 0:1],
                                                                   in1=out, op0=ALU.mult, op1=ALU.add))
                            own_step.done(dve.scalar_tensor_tensor(out=out, in0=bank[:, d:2 * d], scalar=share[u][:, 1:2],
                                                                   in1=out, op0=ALU.mult, op1=ALU.add))
                            dve.sem_inc(values_out, 1)
                own_step.leave(G)
            dve.wait_ge(new_turned, 1)
            dve.tensor_copy(new_t01[:].rearrange("p a n -> p (a n)"), ps[:, 7, 0:2 * NS])
            dve.tensor_copy(new_t2[:].rearrange("p a n -> p (a n)"), ps[0:d, 7, 2 * NS:4 * NS]).then_inc(new_t_made, 1)
            dve.wait_ge(new_t_made, 1)
            dve.memset(q01[:], 0.0)
            dve.memset(q2[:], 0.0)
            dve.memset(new_pad01[:], 0.0)
            dve.memset(new_pad2[:], 0.0)
            own_step.done(dve.memset(groups[:], 0.0))
            dve.wait_ge(gates_in, 16 * H)
            dve.wait_ge(q_moved, 64)
            RT = R * TS
            SEQ_STEPS = 22
            with dve.Fori(0, DB // 2) as i:
                own_step.enter(i, 2 * SEQ_STEPS)
                for u in range(2):
                    b = i * 2 + u
                    for g in range(G):
                        for half in range(2):
                            if g < 2 and half != g:
                                continue
                            parts = slice(half * d, half * d + d)
                            dst = (q01 if g < 2 else q2)[parts, half * RT:(half + 1) * RT].rearrange("p (r t) -> p r t", t=TS)
                            dve.tensor_copy(dst, q_heads[parts, g * R:(g + 1) * R, bass.ds(b * TS, TS)])
                    dve.tensor_copy(new_pad01[:, :, 0:TS], new_t01[:, :, bass.ds(b * TS, TS)])
                    dve.tensor_copy(new_pad2[:, :, 0:TS], new_t2[:, :, bass.ds(b * TS, TS)])
                    dve.tensor_copy(ckeys[0:d, :, 0:NC], comp_k[0:d, bass.ds(b, 1)].rearrange("p a s n -> p (a s) n"))
                    dve.tensor_copy(ckeys[d:P, 0, 0:NC], comp_k[d:P, bass.ds(b, 1), 0].rearrange("p a n -> p (a n)"))\
                       .then_inc(staged, 1)
                    dve.wait_ge(cscores, b + 1)
                    own_step.done(dve.tensor_reduce(cpeak[:, 2:3], ps[0:GR, 7, 0:NC], AX, ALU.max))
                    dve.tensor_scalar(cpeak[:, 0:1], cpeak[:, 2:3], -SCALE, None, ALU.mult).then_inc(cpeaks, 1)
                    for j4 in range(2):
                        copy_key2(dve, b, j4)
                    dve.wait_ge(cexp, b + 1)
                    own_step.done(dve.reciprocal(cpeak[:, 3:4], cpeak[:, 1:2]))
                    dve.tensor_scalar(cp[:], cp[:], cpeak[:, 3:4], None, ALU.mult).then_inc(cp_made, 1)
                    for j4 in range(2, (ST + WJ) // 4):
                        copy_key2(dve, b, j4)
                    dve.wait_ge(cp_turned, b + 1)
                    dve.tensor_copy(cp_t[:], ps[0:NC, 7, P:P + GR])
                    own_step.done(dve.tensor_copy(groups[:, 1:1 + NC], ps[0:G * TS, 7, 2 * P:2 * P + NC]))
                    dve.sem_inc(cp_out, 1)
                    blocks = groups[:, 0:NSTR].rearrange("p (s n) -> p s n", n=SB // ST)
                    own_step.done(dve.tensor_reduce(imp[:, 0:NSEL - 1], blocks[:, :, 1:], AX, ALU.add))
                    own_step.done(dve.scalar_tensor_tensor(out=imp[:, 0:NSEL - 1], in0=imp[:, 0:NSEL - 1], scalar=2.0,
                                                           in1=blocks[:, :, 0], op0=ALU.mult, op1=ALU.add))
                    own_step.done(dve.tensor_tensor(
                        imp[:, 0:NSEL - 1], imp[:, 0:NSEL - 1],
                        groups[:, 1:1 + NSTR].rearrange("p (s n) -> p s n", n=SB // ST)[:, :, SB // ST - 1], ALU.add))
                    dve.memset(imp[:, 0:1], FORCE)
                    own_step.done(dve.memset(imp[:, NSEL - 2:NSEL], FORCE), passed_dve)
                    for n in range(KEEP // 8):
                        own_step.done(dve.max(imp8[:, n * 8:(n + 1) * 8], imp[:]), passed_dve)
                        own_step.done(dve.match_replace(imp[:], imp8[:, n * 8:(n + 1) * 8], imp[:], NEG), passed_dve)
                    dve.tensor_scalar(chosen[:].rearrange("p (s n) -> p s n", n=SB // ST),
                                      imp[:, 0:NSEL - 1].unsqueeze(2).to_broadcast([G * TS, NSEL - 1, SB // ST]),
                                      -1.0, NEG, ALU.is_gt, ALU.mult).then_inc(chosen_made, 1)
                    dve.wait_ge(cvalues, b + 1)
                    for g in range(G):
                        rows = slice(g * RT, (g + 1) * RT)
                        last = dve.tensor_scalar(out_rows[rows], ps[rows, 7, g * d:(g + 1) * d],
                                                 gate_rows[rows, bass.ds(b, 1), 0:1].rearrange("p a c -> p (a c)"), None,
                                                 ALU.mult)
                    own_step.done(last)
                    dve.sem_inc(cvalues_out, 1)
                    dve.wait_ge(bias_sum, b + 1)
                    own_step.done(dve.tensor_copy(bias[:], ps[:, 6, 0:GR]))
                    dve.wait_ge(seq_scores, b + 1)
                    selection = ps[:, 0:4, 0:4 * GR].rearrange("p a (j c) -> p a j c", c=GR)
                    dve.tensor_reduce(peak2[:, 0, :], selection.rearrange("p a j c -> p c a j"), mybir.AxisListType.XY, ALU.max)
                    own_step.done(dve.tensor_tensor(sc[:, ST, :], ps[:, 3, 4 * GR:5 * GR],
                                                    win_mask[:, WJ].rearrange("p h t -> p (h t)"), ALU.add))
                    dve.tensor_tensor(sc[:, SL:, :], ps[:, 4, 0:5 * GR].rearrange("p (j c) -> p j c", c=GR),
                                      win_mask[:].rearrange("p j h t -> p j (h t)"), ALU.add)
                    own_step.done(dve.tensor_tensor(peak2[:, 0, :], peak2[:, 0, :], bias[:], ALU.add))
                    dve.tensor_tensor(peak2[:, 0, :], peak2[:, 0, :], sc[:, ST, :], ALU.max)
                    dve.tensor_reduce(peak2[:, 1, :], sc[:, SL:, :].rearrange("p j c -> p c j"), AX, ALU.max)\
                       .then_inc(peaks_made, 1)
                    dve.wait_ge(peaks_turned, b + 1)
                    own_step.done(dve.tensor_reduce(peak_row[:], ps[0:GR, 5, 0:2 * P].rearrange("p (a n) -> p a n", a=2),
                                                    AX, ALU.max))
                    for n in range(2):
                        last = dve.tensor_scalar(peak_diag[:, n, :], ident[0:GR, 0:GR], peak_row[:, n:n + 1], -1.0,
                                                 ALU.mult, ALU.mult)
                    last.then_inc(diag_made, 1)
                    dve.wait_ge(peaks_spread, b + 1)
                    own_step.done(dve.tensor_tensor(bias[:], bias[:], ps[:, 6, 0:GR], ALU.add))
                    for a in range(4):
                        dve.tensor_tensor(sc[:, 4 * a:4 * a + 4, :], selection[:, a], bias[:].unsqueeze(1).to_broadcast([P, 4, GR]),
                                          ALU.add)
                    dve.tensor_tensor(sc[:, ST, :], sc[:, ST, :], ps[:, 6, 0:GR], ALU.add)
                    own_step.done(dve.tensor_tensor(sc[:, SL:, :], sc[:, SL:, :],
                                                    ps[:, 6, GR:2 * GR].unsqueeze(1).to_broadcast([P, WL, GR]), ALU.add))
                    dve.sem_inc(shifted, 1)
                    dve.wait_ge(seq_exp, b + 1)
                    dve.tensor_reduce(sum2[:, 0, :], sc[:, 0:SL, :].rearrange("p j c -> p c j"), AX, ALU.add)
                    dve.tensor_reduce(sum2[:, 1, :], sc[:, SL:, :].rearrange("p j c -> p c j"), AX, ALU.add)\
                       .then_inc(sums_made, 1)
                    dve.wait_ge(seq_values, b + 3)
                    own_step.done(dve.reciprocal(coef[:, 0:2], ps[0:GR, 7, 2 * G * d:2 * G * d + 2]))
                    own_step.done(dve.tensor_tensor(coef[:, 2:4], coef[:, 0:2],
                                                    gate_rows[:, bass.ds(b, 1), 1:3].rearrange("p a c -> p (a c)"), ALU.mult))
                    for n in range(2):
                        for g in range(G):
                            rows = slice(g * RT, (g + 1) * RT)
                            last = dve.scalar_tensor_tensor(
                                out=out_rows[rows], in0=ps[rows, 7, (n * G + g) * d:(n * G + g + 1) * d],
                                scalar=coef[rows, 2 + n:3 + n], in1=out_rows[rows], op0=ALU.mult, op1=ALU.add)
                        own_step.done(last)
                    dve.sem_inc(out_made, 1)
                    dve.wait_ge(out_stored, b * 16 + 16)
                own_step.leave(DB // 2)
            dve.wait_ge(gate_turned, 1)
            dve.tensor_copy(gate_bc[:].rearrange("p (a n) -> p a n", a=2), ps[0:NB, 0:2, :]).then_inc(gate_copied, 1)
            dve.wait_ge(gate_spread, 1)
            dve.tensor_copy(gate_all[:, 0, :].rearrange("p (a n) -> p a n", a=2), ps[:, 2:4, :])
            dve.tensor_copy(gate_all[0:NS, 1, :].rearrange("p (a n) -> p a n", a=2), ps[0:NS, 4:6, :]).then_inc(gate_made, 1)
            dve.wait_ge(norm_in, 16)
            for t in range(NT + 3):
                if t <= NT:
                    rows = P if t < NT else NS
                    dve.wait_ge(osums, t + 1)
                    for n, width in enumerate((PW, NW)):
                        last = dve.tensor_scalar(orstd[0:rows, t, n:n + 1], ostat[0:rows, t, n:n + 1], 1.0 / width, EPS,
                                                 ALU.mult, ALU.add)
                    last.then_inc(omeans, 1)
                    dve.wait_ge(oroots, t + 1)
                    own_step.done(dve.reciprocal(orstd[0:rows, t, 0:2], orstd[0:rows, t, 0:2]))
                    if t >= 2:
                        dve.wait_ge(mixed_turned, 2 * (t - 1))
                    m = mixed_rows[t % 2]
                    dve.scalar_tensor_tensor(out=m[0:rows, 0:PW], in0=ps[0:rows, 0, 0:PW], scalar=orstd[0:rows, t, 0:1],
                                             in1=z_gate[0:rows, t, 0:PW], op0=ALU.mult, op1=ALU.mult)
                    dve.scalar_tensor_tensor(out=m[0:rows, PW:], in0=nsa[0:rows, t, :], scalar=orstd[0:rows, t, 1:2],
                                             in1=z_gate[0:rows, t, PW:], op0=ALU.mult, op1=ALU.mult).then_inc(mixed_made, 1)
                if 1 <= t <= NT + 1:
                    n = t - 1
                    rows = P if n < NT else NS
                    dve.wait_ge(mixed_turned, 2 * n + 2)
                    if n >= 2:
                        dve.wait_ge(projected, n - 1)
                    for c in range(4):
                        last = dve.tensor_scalar(mixT[n % 2][:, 4 + c, 0:rows], ps[:, 2, c * rows:(c + 1) * rows],
                                                 vec_t[:, 4 * KC + 4 + c:4 * KC + 5 + c], None, ALU.mult)
                    last.then_inc(mixT_made[1], 1)
                if t >= 2:
                    n = t - 2
                    rows = P if n < NT else NS
                    y = y_rows[n % 2][0:rows]
                    dve.wait_ge(projected, n + 1)
                    if n >= 2:
                        dve.wait_ge(y_stored[n % 2], 16 * (n // 2))
                    own_step.done(dve.tensor_tensor(y.rearrange("p (a n) -> p a n", a=2),
                                                    ps[0:rows, 3 + n % 2 * 2:5 + n % 2 * 2, :],
                                                    gate_all[0:rows, n // NT, :].rearrange("p (a n) -> p a n", a=2), ALU.mult))
                    dve.wait_ge(x_again_in[n % 2], 16 * (n // 2 + 1))
                    dve.tensor_tensor(y, y, x_again[n % 2][0:rows], ALU.add).then_inc(y_sum, 1)
                    dve.wait_ge(ysq, n + 1)
                    dve.tensor_scalar(orstd[0:rows, n, 2:3], ostat[0:rows, n, 2:3], 1.0 / D, EPS,
                                      ALU.mult, ALU.add).then_inc(ymeans, 1)
                    dve.wait_ge(yroots, n + 1)
                    own_step.done(dve.reciprocal(orstd[0:rows, n, 2:3], orstd[0:rows, n, 2:3]))
                    dve.scalar_tensor_tensor(out=y, in0=y, scalar=orstd[0:rows, n, 2:3], in1=norm_row[0:rows],
                                             op0=ALU.mult, op1=ALU.mult).then_inc(y_made, 1)


_INS = ["x_prompt", "x_sample", "c_prompt", "c_sample", "cache_cmp_kv", "cache_slc_kv", "state_win_kv", "state_pool",
        "page_table", "norm_w", "w_ada", "b_ada", "w_in", "pool_w", "pool_scale", "phi_w1", "phi_pe", "phi_w2",
        "gn_pool", "gn_nsa", "w_out", "final_norm"]


def _outs(i):
    depth, batch, seq = i["w_in"].shape[0], i["x_prompt"].shape[0], i["x_prompt"].shape[1]
    rows = i["cache_cmp_kv"].shape[3:]
    win, hist = i["state_win_kv"].shape, i["state_pool"].shape
    new = (depth, *i["x_sample"].shape[:2], *rows)
    prompt = (depth, batch, seq, *rows)
    return [i["x_prompt"].shape, i["x_sample"].shape, prompt, new, prompt, new,
            (depth, batch, min(win[2], seq), *rows), win, (depth, batch, *hist[2:]), hist]


def kernel(**inputs):
    import numpy as np
    import concourse.bacc as bacc
    from concourse.bass_utils import run_bass_kernel_spmd

    nc = bacc.Bacc("TRN2", target_bir_lowering=False, num_devices=1)
    arrays, args = {}, []
    for name in _INS:
        a = np.ascontiguousarray(inputs[name])
        arrays[f"in_{name}"] = a
        args.append(nc.dram_tensor(f"in_{name}", a.shape, mybir.dt.from_np(a.dtype), kind="ExternalInput").ap())
    shapes = _outs({name: inputs[name] for name in _INS})
    for n, shape in enumerate(shapes):
        args.append(nc.dram_tensor(f"out_{n}", shape, F32, kind="ExternalOutput").ap())
    program(nc, *args)
    r = run_bass_kernel_spmd(nc, [arrays], core_ids=[0])
    return tuple(r.results[0][f"out_{n}"] for n in range(len(shapes)))
```

```python
from contextlib import ExitStack

import concourse.bass as bass
from concourse import mybir
from concourse.alu_op_type import AluOpType as ALU

ACT = mybir.ActivationFunctionType
AX = mybir.AxisListType.X
F32 = mybir.dt.float32
I32 = mybir.dt.int32
P = 128
EPS = 1e-6
NEG = -1e30
FORCE = 1e4


class Steps:

    def __init__(self, eng, sem):
        self.eng, self.sem, self.n, self.at = eng, sem, 0, None

    def enter(self, turn, per_turn):
        self.before, self.at, self.per_turn, self.n = self.n, turn * per_turn, per_turn, 0

    def leave(self, turns):
        assert self.n == self.per_turn, self.n
        self.n, self.at = self.before + turns * self.per_turn, None

    def done(self, ins, passed=None):
        ins.then_inc(self.sem, 1)
        self.n += 1
        if self.at is None:
            self.eng.wait_ge(self.sem, self.n)
        else:
            self.eng.wait_ge(self.sem, self.at + (self.before + self.n))
        if passed is not None:
            self.eng.sem_inc(passed, 1)


def program(nc, x_prompt, x_sample, c_prompt, c_sample, cache_cmp_kv, cache_slc_kv, state_win_kv, state_pool,
            page_table, norm_w, w_ada, b_ada, w_in, pool_w, pool_scale, phi_w1, phi_pe, phi_w2,
            gn_pool, gn_nsa, w_out, final_norm,
            y_prompt, y_sample, new_cmp_p, new_cmp_s, new_slc_p, new_slc_s, new_win_p, new_win_s,
            new_pool_p, new_pool_s):
    T, D = x_prompt.shape[1:]
    DB, TS = x_sample.shape[:2]
    NS = DB * TS
    n_phys, page, _, G, d = cache_cmp_kv.shape[1:]
    n_pages = page_table.shape[1]
    PAST = n_pages * page
    KV = 2 * G * d
    PW = pool_w.shape[1] * pool_w.shape[2]
    NW = D - PW
    H = NW // d
    R = H // G
    HID = phi_w1.shape[4]
    SPAN = phi_w1.shape[1]
    ST = SPAN // 2
    KC = D // P
    NT = T // P
    WIN = state_win_kv.shape[2]
    WJ = WIN // P
    HIST = state_pool.shape[2]
    SB = 64
    NSTR = PAST // ST
    NC = NSTR - 1
    PSTR = T // ST
    PC = PSTR - 1
    JP = ST // 2
    NB = DB + 1
    GR = G * R * TS
    SCALE = d ** -0.5
    NSEL = PAST // SB + 1
    KEEP = 16
    assert NSEL - 1 > KEEP and SB // ST * (NSEL - 1) == NSTR and TS <= SB
    POOL_WINDOWS = (2, 4, 8, 16)
    assert PW == 2 * P and HIST == POOL_WINDOWS[-1] - 1
    assert NSTR == P and d == 64 and G == 3 and HID == P and GR == 96 and T <= WIN and KC == 8
    PPS = page // ST

    cmp_rows = cache_cmp_kv.rearrange("l n (s j) k g d -> (l n s) (j k g d)", j=ST)
    slc_rows = cache_slc_kv.rearrange("l n (s j) k g d -> (l n s) (j k g d)", j=ST)

    with ExitStack() as ctx:
        def sem(name):
            return ctx.enter_context(nc.semaphore(name))

        def at(name, shape, offset, dtype=F32):
            return nc.alloc_sbuf_tensor_at(name, shape, dtype, offset=offset)

        top = -(-nc.sbuf_base // 64) * 64

        def region(nbytes):
            nonlocal top
            start = top
            top += -(-nbytes // 32) * 32
            assert top <= nc.sbuf_usable_end, top
            return start

        def own(name, shape, dtype=F32):
            n = 4
            for s in shape[1:]:
                n *= s
            return at(name, shape, region(n), dtype)

        ident = own("ident", [P, P])
        ones = own("ones", [P, P])
        sel_page = own("sel_page", [n_pages, P])
        sel_prompt = own("sel_prompt", [NB, P])
        sel_seq = own("sel_seq", [NB, NS])
        sel_sum_r = own("sel_sum_r", [GR, G, TS])
        sel_rep_r = own("sel_rep_r", [G * TS, G, R, TS])
        causal = own("causal", [P, P])
        cmp_mask = own("cmp_mask", [P, NT, PC])
        cmp_any = own("cmp_any", [P, NT])
        win_mask = own("win_mask", [P, WJ + 1, H, TS])
        NVEC = 3 * KC + KC + KC + 4 * SPAN // 4
        vec_t = own("vec_t", [P, NVEC])
        ada_t = own("ada_t", [P, 3 * KC, NB])
        ada_mul = own("ada_mul", [P, KC, NB])
        pe_bias = own("pe_bias", [P, 2])
        w2 = own("w2", [P, 2, d])
        page_f = own("page_f", [n_pages, DB + 1])
        page_i = own("page_i", [n_pages, DB + 1], I32)
        stride_f = own("stride_f", [P, DB + 2])
        stride_i = own("stride_i", [P, DB], I32)
        gates = own("gates", [P, NT + 1, 3 * H])

        cs_t = own("cs_t", [P, KC, NB])
        sumsq = own("sumsq", [P, NT + 1])
        rstd = own("rstd", [P, NT + 1])
        q_heads = own("q_heads", [P, H, NS])
        pool_bd = own("pool_bd", [P, PW // P, P])
        ramp = own("ramp", [P, PW // P, HIST + 1])
        mix_seq = own("mix_seq", [P, PW // P, NS])
        gate_rows = own("gate_rows", [GR, DB, 3])
        u_seq = own("u_seq", [P, PW // P, DB, HIST + TS])

        R_HT = region(KC * (T + NS) * 4)
        R_Z = region((NT + 1) * D * 4)
        R_KV = region((NT + 1) * (2 * KV + 3 * H) * 4)
        R_D = region((NW // P * T + PW // P * T + G * 2 * T) * 4)
        R_W1 = region(16384)
        R_CK = region(DB * 2 * NC * 4)
        R_CV = region(DB * G * d * 4)
        R_PCK = region(G * PC * 4)
        R_PCV = region(G * d * 4)
        R_X = region(2 * ST * KV * 4)
        R_W = region(2 * KC * 512 * 4)

        hT = at("hT", [P, KC, T + NS], R_HT)
        vec = at("vec", [NVEC, P], R_HT)
        c_rows = at("c_rows", [NB, D], R_HT + 1024)
        c_silu = at("c_silu", [NB, D], R_HT + 1024 + 4 * D)
        w1 = at("w1", [P, 2 * JP, 2, HID], R_W1)
        caches = [at(f"cache{u}", [P, ST, KV], R_X + u * ST * KV * 4) for u in range(2)]
        NXT = 4
        xt = [at(f"xt{s}", [P, 2 * G, P], R_D + s * 2 * G * P * 4) for s in range(NXT)]
        hid = at("hid", [P, 2, G, NC], R_D + NXT * 2 * G * P * 4)
        comp_k = at("comp_k", [P, DB, 2, NC], R_CK)
        comp_v = at("comp_v", [P, DB, G * d], R_CV)

        hist_rows = at("hist_rows", [DB * HIST, PW], R_HT + 1024 + 8 * D)
        scale_row = at("scale_row", [P, PW], R_HT + 1024 + 8 * D + 4 * PW)
        ramp_i = at("ramp_i", [P, PW // P, HIST + 1], R_HT + 16384, I32)
        x_rows = at("x_rows", [P, NT + 1, D], R_Z)
        x_sq = at("x_sq", [P, D], R_KV)
        pe_rows_sum = at("pe_rows_sum", [2, 2 * HID], R_KV + 4 * D)
        wcols = [at(f"wcols{u}", [P, KC, 512], R_W + u * KC * 512 * 4) for u in range(2)]
        z_gate = at("z_gate", [P, NT + 1, D], R_Z)
        kv = at("kv", [P, NT + 1, 2 * KV + 3 * H], R_KV)
        qT = at("qT", [P, NW // P, T], R_D)
        uT = at("uT", [P, PW // P, T], R_D + NW // P * T * 4)
        R_KT = R_D + (NW + PW) // P * T * 4
        kT = at("kT", [d, 2, G, T], R_KT)
        cmp_new = at("cmp_new", [P, NT + 1, KV], R_KT)
        qS = at("qS", [P, NW // P, NS], R_KT + (NT + 1) * KV * 4)
        xp = at("xp", [PSTR, ST, KV], R_X)
        xpt = at("xpt", [P, JP, 2 * G, PSTR], R_X + ST * KV * 4)
        hid_p = at("hid_p", [P, 2, G, PC], R_X + ST * KV * 4 + JP * 2 * G * PSTR * 4)
        nsa = at("nsa", [P, NT + 1, NW], R_HT)
        u_last = at("u_last", [NS, 2, PW], R_HT + (NT + 1) * NW * 4 + 1024)
        uS = at("uS", [P, PW // P, NS], R_KT + (NT + 1) * KV * 4 + NW // P * NS * 4)
        pcomp_k = at("pcomp_k", [d, G * PC], R_PCK)
        w_at = R_W
        def in_w(name, shape):
            nonlocal w_at
            n = 4
            for x in shape[1:]:
                n *= x
            n = -(-n // 32) * 32
            w_at += n
            return at(name, shape, w_at - n)
        q_head = [in_w(f"q_head{u}", [d, T]) for u in range(2)]
        probs = [in_w(f"probs{u}", [P, 2, T]) for u in range(2)]
        probs_t = [in_w(f"probs_t{u}", [P, 2, NT, P]) for u in range(2)]
        cprobs = [in_w(f"cprobs{u}", [P, NT, PC]) for u in range(2)]
        cprobs_t = [in_w(f"cprobs_t{u}", [PC, NT, P]) for u in range(2)]
        peak = [in_w(f"peak{u}", [P, NT]) for u in range(2)]
        total = [in_w(f"total{u}", [P, NT]) for u in range(4)]
        share = [in_w(f"share{u}", [P, NT]) for u in range(2)]
        assert w_at <= R_W + 2 * KC * 512 * 4
        PAD = HIST + 1
        sums = [at(f"sums{u}", [P, PW // P, PAD + T], R_W1 + u * (PAD + T) * 8) for u in range(2)]
        seq_sums = [at(f"seq_sums{u}", [P, PW // P, DB, HIST + TS], R_W1 + (PAD + T) * 16 + u * 2048) for u in range(2)]
        pcomp_v = at("pcomp_v", [P, G * d], R_PCV)

        C_Q, C_ZN, C_KVC = 2 * PW, 2 * PW + NW, 2 * PW + 2 * NW
        C_GL = C_KVC + 3 * KV
        IN_BLOCKS = [(C_KVC, KV), (C_KVC + KV, KV), (C_KVC + 2 * KV, KV + 3 * H), (C_Q, 512), (C_Q + 512, 512),
                     (0, 512), (C_ZN + 256, 512)]
        assert C_Q + 1024 == C_ZN + 256 and C_ZN + 768 == C_KVC and C_GL + 3 * H == w_in.shape[2]
        jobs = []
        for n, (c0, width) in enumerate(IN_BLOCKS):
            at_col = 0
            while at_col < width:
                c = c0 + at_col
                if c < PW or C_Q <= c < C_ZN:
                    jobs.append((n, True, at_col, P, None, "prompt", c))
                    jobs.append((n, True, at_col, P, None, "sample", c))
                    at_col += P
                else:
                    w = 256 if n == 5 else (width - at_col)
                    for t in range(NT + 1):
                        jobs.append((n, False, at_col, w, t, "rows", c))
                    at_col += w
        by = []
        count = [0, 0]
        for j, (n, turned, _, _, t, what, c) in enumerate(jobs):
            gate = not turned and (PW <= c < C_Q or C_ZN <= c < C_KVC)
            e = 0 if gate else (1 if (turned and what == "sample") or n < 3 else j // 2 % 2)
            count[e] += 1
            by.append((e, count[e]))
        block_jobs = [sum(1 for j in jobs if j[0] <= n) for n in range(len(IN_BLOCKS))]
        first_job = [0] + block_jobs
        XP_BLOCK = 4
        xp_job = first_job[XP_BLOCK]
        xp_bank = [[(xp_job + 2 * s + j) % 8 for j in range(2)] for s in range(3)]
        hid_p_bank = [(xp_job + 6 + k) % 8 for k in range(2)]

        SL, WL = ST + 1, WJ + 1
        key_t01 = at("key_t01", [P, ST, P], R_D)
        key_t2 = at("key_t2", [P, ST // 2, P], R_D + ST * P * 4)
        wkey_t01 = at("wkey_t01", [P, WJ, P], R_KT)
        wkey_t2 = at("wkey_t2", [P, WJ // 2, P], R_KT + WJ * P * 4)
        r_at = R_KT + WJ * P * 6
        new_t01 = at("new_t01", [P, 2, NS], r_at)
        new_t2 = at("new_t2", [d, 2, NS], r_at + 8 * NS)
        ckeys = at("ckeys", [P, 2, P], r_at + 16 * NS)
        new_pad01 = at("new_pad01", [P, 2, P], r_at + 16 * NS + 1024)
        new_pad2 = at("new_pad2", [d, 2, P], r_at + 16 * NS + 2048)
        q01 = at("q01", [P, 2 * R * TS], r_at + 16 * NS + 3072)
        q2 = at("q2", [P, 2 * R * TS], r_at + 16 * NS + 3072 + 256)
        out_rows = [at(f"out_rows{u}", [GR, d], r_at + 16 * NS + 3072 + 512 + u * 256) for u in range(3)]
        sc = at("sc", [P, SL + WL, GR], R_KV)
        k_at = R_KV + (SL + WL) * GR * 4
        def in_k(name, shape):
            nonlocal k_at
            n = 4
            for x in shape[1:]:
                n *= x
            n = -(-n // 32) * 32
            k_at += n
            assert k_at <= R_KV + (NT + 1) * (2 * KV + 3 * H) * 4
            return at(name, shape, k_at - n)
        cp = in_k("cp", [GR, NC])
        cp_t = in_k("cp_t", [NC, GR])
        cpeak = in_k("cpeak", [GR, 4])
        groups = in_k("groups", [G * TS, 1 + NSTR])
        imp = in_k("imp", [G * TS, NSEL])
        imp8 = in_k("imp8", [G * TS, 16])
        chosen = in_k("chosen", [G * TS, NSTR])
        bias = in_k("bias", [P, GR])
        peak2 = in_k("peak2", [P, 2, GR])
        peak_row = in_k("peak_row", [GR, 2])
        peak_diag = in_k("peak_diag", [GR, 2, GR])
        sum2 = in_k("sum2", [P, 2, GR])
        coef = in_k("coef", [GR, 4])
        win_peak = at("win_peak", [P, GR], r_at + 16 * NS + 3072 + 512 + 768)
        NBUF = 3
        seq_rows = caches + [at("seq_rows2", [P, ST, KV], R_W)]
        win_at = (R_W1, R_W1 + (WJ * KV + 2 * G * d) * 4, R_W + ST * KV * 4)
        win_rows = [at(f"win_rows{u}", [P, WJ, KV], win_at[u]) for u in range(NBUF)]
        new_v = [at(f"new_v{u}", [TS, 2, G * d], win_at[u] + WJ * KV * 4) for u in range(NBUF)]
        gate_dram = nc.dram_tensor("gate_dram", [NS, 3 * H], F32).ap()
        out_dram = nc.dram_tensor("out_dram", [DB, GR, d], F32).ap()
        w_o = at("w_o", [P, KC, D], R_W)
        mixT = [at(f"mixT{u}", [P, KC, P], R_D + u * 4 * D) for u in range(2)]
        mixed_rows = [at("mixed_rows0", [P, D], R_D + 8 * D), at("mixed_rows1", [P, D], R_KT)]
        y_rows = [at(f"y_rows{u}", [P, D], R_KT + (1 + u) * 4 * D) for u in range(2)]
        gate_bc = at("gate_bc", [NB, D], R_X + 8 * D)
        gate_all = at("gate_all", [P, 2, D], R_X + 16 * D)
        norm_row = at("norm_row", [P, D], R_X)
        x_again = [at(f"x_again{u}", [P, D], R_W1 + (1 + u) * 4 * D) for u in range(2)]
        osq = at("osq", [P, D], R_X + 4 * D)
        assert (DB - 2) % NBUF == 0 and 24 * D <= ST * KV * 4
        ostat = at("ostat", [P, NT + 1, 4], R_X + 12 * D)
        orstd = at("orstd", [P, NT + 1, 4], R_X + 12 * D + 128)

        KT_TURNS = (ST + WJ) // 4 * 2
        TURN_ORDER = (4, 0, 1, 2, 3)
        assert ST == 16 and WJ == 4
        EXPS = ST // 4 + 1

        UNITS = NT + 1

        ps = ctx.enter_context(nc.psum_tensor("ps", [P, 8, 512], F32))

        const_made = sem("const_made")
        pool_own = sem("pool_own")
        pages_made = sem("pages_made")
        ident_made = sem("ident_made")
        page_in = sem("page_in")
        vec_in = sem("vec_in")
        phi_in = sem("phi_in")
        dve_own = sem("dve_own")
        act_own = sem("act_own")
        silu_c = sem("silu_c")
        page_cast = sem("page_cast")
        turned_small = sem("turned_small")
        vec_made = sem("vec_made")
        pe_sum = sem("pe_sum")
        pe_rows_made = sem("pe_rows_made")
        pe_bias_made = sem("pe_bias_made")
        strides_made = sem("strides_made")
        cache_in = [sem(f"cache_in{u}") for u in range(2)]
        pairs_turned = [sem(f"pairs_turned{u}") for u in range(2)]
        pairs_out = [sem(f"pairs_out{u}") for u in range(2)]
        pairs_used = sem("pairs_used")
        hidden = sem("hidden")
        comp_sum = sem("comp_sum")
        comp_k_out = sem("comp_k_out")
        comp_v_out = sem("comp_v_out")

        mix_in = sem("mix_in")
        mix_made = sem("mix_made")
        hist_out = sem("hist_out")
        ramp_made = sem("ramp_made")
        u_last_turned = sem("u_last_turned")
        u_last_out = sem("u_last_out")
        mixed = sem("mixed")
        sums_own = sem("sums_own")
        q_in = [sem(f"q_in{u}") for u in range(2)]
        passed = sem("passed")
        scores = sem("scores")
        peaks = sem("peaks")
        probs_made = sem("probs_made")
        probs_turned = sem("probs_turned")
        probs_out = [sem("probs_out0"), sem("probs_out1")]
        values = sem("values")
        values_out = sem("values_out")
        gates_in = sem("gates_in")
        gates_stored = sem("gates_stored")
        seq_in = [sem(f"seq_in{u}") for u in range(3)]
        win_in = [sem(f"win_in{u}") for u in range(3)]
        win_stored = sem("win_stored")
        new_turned = sem("new_turned")
        new_t_made = sem("new_t_made")
        staged = sem("staged")
        cscores = sem("cscores")
        cpeaks = sem("cpeaks")
        cexp = sem("cexp")
        cp_made = sem("cp_made")
        cp_turned = sem("cp_turned")
        cp_out = sem("cp_out")
        chosen_made = sem("chosen_made")
        keys_turned = sem("keys_turned")
        keys_out = sem("keys_out")
        cvalues_out = sem("cvalues_out")
        seq_scores = sem("seq_scores")
        rest_scores = sem("rest_scores")
        peaks_made = sem("peaks_made")
        peaks_turned = sem("peaks_turned")
        diag_made = sem("diag_made")
        peaks_spread = sem("peaks_spread")
        shifted = sem("shifted")
        seq_exp = sem("seq_exp")
        sums_made = sem("sums_made")
        seq_used = sem("seq_used")
        seq_values = sem("seq_values")
        cvalues = sem("cvalues")
        out_made = sem("out_made")
        out_stored = [sem(f"out_stored{u}") for u in range(3)]
        nsa_in = sem("nsa_in")
        w_o_in = sem("w_o_in")
        norm_in = sem("norm_in")
        gate_turned = sem("gate_turned")
        gate_copied = sem("gate_copied")
        gate_spread = sem("gate_spread")
        gate_made = sem("gate_made")
        pool_values = sem("pool_values")
        osums = sem("osums")
        omeans = sem("omeans")
        oroots = sem("oroots")
        mixed_made = sem("mixed_made")
        mixed_turned = sem("mixed_turned")
        mixT_made = [sem("mixT_made0"), sem("mixT_made1")]
        projected = sem("projected")
        y_sum = sem("y_sum")
        ysq = sem("ysq")
        ymeans = sem("ymeans")
        yroots = sem("yroots")
        y_made = sem("y_made")
        y_stored = [sem(f"y_stored{u}") for u in range(2)]
        x_again_in = [sem(f"x_again_in{u}") for u in range(2)]
        passed_dve = sem("passed_dve")
        x_in = sem("x_in")
        sumsq_made = sem("sumsq_made")
        rstd_root = sem("rstd_root")
        ms_made = sem("ms_made")
        xhat_made = sem("xhat_made")
        cs_made = sem("cs_made")
        wcols_in = [sem(f"wcols_in{u}") for u in range(2)]
        ada_used = sem("ada_used")
        ada_made = sem("ada_made")
        x_turned = sem("x_turned")
        x_out = [sem("x_out0"), sem("x_out1")]
        job_done = sem("job_done")
        job_out = [sem("job_out0"), sem("job_out1")]
        stored = sem("stored")
        cmp_stored = sem("cmp_stored")
        xp_in = sem("xp_in")
        q_moved = sem("q_moved")
        xp_turned = sem("xp_turned")
        xp_out = [sem("xp_out0"), sem("xp_out1")]
        hid_p_sum = sem("hid_p_sum")
        hid_p_made = sem("hid_p_made")
        pcomp_sum = sem("pcomp_sum")
        pcomp_made = sem("pcomp_made")
        kt_turned = sem("kt_turned")
        kt_made = [sem("kt_made0"), sem("kt_made1")]
        gates_made = sem("gates_made")

        block = ctx.enter_context(nc.Block())

        @block.gpsimd
        def _(pool):
            own_step = Steps(pool, pool_own)

            def gather_cache(b):
                pool.indirect_dma_start(
                    out=caches[b % 2][:].rearrange("p j c -> p (j c)"), out_offset=None, in_=cmp_rows,
                    in_offset=bass.IndirectOffsetOnAxis(ap=stride_i[:, b:b + 1], axis=0),
                ).then_inc(cache_in[b % 2], 16)

            def select(out, in_, pattern, base, cm, op, fill):
                own_step.done(pool.affine_select(out=out, in_=in_, compare_op=op, fill=fill, base=base,
                                                 pattern=pattern, channel_multiplier=cm))

            pool.memset(sel_page[:], 1.0)
            pool.iota(page_i[:, DB:DB + 1], pattern=[[0, 1]], base=0, channel_multiplier=1)
            own_step.done(pool.iota(stride_i[:, 0:1], pattern=[[0, 1]], base=0, channel_multiplier=1))
            select(sel_page[:], sel_page[:], [[1, P]], 0, -PPS, ALU.is_ge, 0.0)
            select(sel_page[:], sel_page[:], [[-1, P]], PPS - 1, PPS, ALU.is_ge, 0.0)
            pool.tensor_copy(page_f[:, DB:DB + 1], page_i[:, DB:DB + 1])
            pool.tensor_copy(stride_f[:, DB:DB + 1], stride_i[:, 0:1])
            pool.drain().then_inc(pages_made, 1)
            pool.memset(ident[:], 0.0)
            pool.memset(ones[:], 1.0)
            pool.memset(sel_prompt[:], 0.0)
            pool.memset(sel_seq[:], 1.0)
            pool.memset(sel_sum_r[:], 0.0)
            pool.memset(sel_rep_r[:], 0.0)
            pool.memset(causal[:], 0.0)
            pool.memset(cmp_mask[:], 0.0)
            pool.memset(cmp_any[:], 1.0)
            pool.memset(pool_bd[:], 0.0)
            own_step.done(pool.memset(win_mask[:], 0.0))
            select(ident[:], ident[:], [[-1, P]], 0, 1, ALU.not_equal, 1.0)
            pool.drain().then_inc(ident_made, 1)
            pool.wait_ge(strides_made, 1)
            gather_cache(0)
            pool.wait_ge(wcols_in[0], 16)
            gather_cache(1)
            select(sel_prompt[:], sel_prompt[:], [[0, P]], 0, 1, ALU.not_equal, 1.0)
            select(sel_seq[:], sel_seq[:], [[1, NS]], TS, -TS, ALU.is_ge, 0.0)
            select(sel_seq[:], sel_seq[:], [[-1, NS]], -1, TS, ALU.is_ge, 0.0)
            for r in range(R):
                select(sel_sum_r[:], sel_sum_r[:], [[-R * TS, G], [-1, TS]], -r * TS, 1, ALU.not_equal, 1.0)
            select(sel_rep_r[:], sel_rep_r[:], [[-TS, G], [0, R], [-1, TS]], 0, 1, ALU.not_equal, 1.0)
            select(causal[:], causal[:], [[-1, P]], 0, 1, ALU.is_ge, NEG)
            select(cmp_mask[:], cmp_mask[:], [[P, NT], [-ST, PC]], -(SPAN - 1), 1, ALU.is_ge, NEG)
            select(cmp_any[:], cmp_any[:], [[P, NT]], -(SPAN - 1), 1, ALU.is_ge, 0.0)
            select(win_mask[:, 0:WJ], win_mask[:, 0:WJ], [[1, WJ], [0, H], [-1, TS]], -1, WJ, ALU.is_ge, NEG)
            select(win_mask[:, WJ], win_mask[:, WJ], [[0, H], [1, TS]], 0, -1, ALU.is_ge, NEG)
            own_step.done(pool.iota(ramp_i[:], pattern=[[0, PW // P], [1, HIST + 1]], base=1, channel_multiplier=0))
            own_step.done(pool.tensor_copy(ramp[:], ramp_i[:]))
            pool.drain().then_inc(const_made, 1)
            for b in range(2, DB):
                pool.wait_ge(pairs_turned[1], (b - 1) * JP)
                gather_cache(b)

            def gather_selection(b):
                pool.indirect_dma_start(
                    out=seq_rows[b % NBUF][:].rearrange("p j c -> p (j c)"), out_offset=None, in_=slc_rows,
                    in_offset=bass.IndirectOffsetOnAxis(ap=stride_i[:, b:b + 1], axis=0),
                ).then_inc(seq_in[b % NBUF], 16)

            pool.wait_ge(pcomp_made, 1)
            for e in range(2):
                pool.wait_ge(job_out[e], count[e])
            pool.wait_ge(u_last_turned, 1)
            for a in sums:
                pool.memset(a[:, :, 0:PAD], 0.0)
            own_step.done(pool.tensor_copy(sums[0][:, :, PAD:PAD + 1], uT[:, :, 0:1]))
            own_step.done(pool.tensor_tensor(sums[0][:, :, PAD + 1:], uT[:, :, 1:], uT[:, :, 0:T - 1], ALU.add))
            own_step.done(pool.tensor_tensor(seq_sums[0][:, :, :, 1:], u_seq[:, :, :, 1:],
                                             u_seq[:, :, :, 0:HIST + TS - 1], ALU.add))

            def double(dst, src, parts, m, step):
                pool.tensor_tensor(sums[dst][parts, m, PAD:], sums[src][parts, m, PAD:],
                                   sums[src][parts, m, PAD - step:PAD + T - step], ALU.add)
                first = 2 * step - 1
                own_step.done(pool.tensor_tensor(seq_sums[dst][parts, m, :, first:], seq_sums[src][parts, m, :, first:],
                                                 seq_sums[src][parts, m, :, first - step:HIST + TS - step], ALU.add))

            low, high, whole = slice(0, d), slice(d, P), slice(0, P)
            double(1, 0, high, 0, 2)
            double(1, 0, whole, 1, 2)
            double(0, 1, whole, 1, 4)
            double(1, 0, high, 1, 8)
            for n, w in enumerate(POOL_WINDOWS):
                m, parts = n // 2, (low, high)[n % 2]
                a, b = sums[n % 2][parts, m, PAD:], seq_sums[n % 2][parts, m, :, HIST:]
                pool.tensor_scalar(b, b, 1.0 / w, None, ALU.mult)
                own_step.done(pool.tensor_scalar(a, a, 1.0 / w, None, ALU.mult))
            for n in range(len(POOL_WINDOWS)):
                m, parts = n // 2, (low, high)[n % 2]
                a = sums[n % 2][parts, m, PAD:PAD + HIST + 1]
                own_step.done(pool.tensor_tensor(a, a, ramp[parts, m], ALU.mult))
            for n in range(len(POOL_WINDOWS)):
                m, parts = n // 2, (low, high)[n % 2]
                u = uT[parts, m]
                pool.tensor_tensor(u, sums[n % 2][parts, m, PAD:], u, ALU.subtract)
                last = pool.tensor_tensor(mix_seq[parts, m].rearrange("p (b t) -> p b t", t=TS),
                                          seq_sums[n % 2][parts, m, :, HIST:], u_seq[parts, m, :, HIST:], ALU.subtract)
            pool.drain().then_inc(mixed, 1)
            for b in range(2):
                gather_selection(b)
            for b in range(2, DB):
                if b < NBUF:
                    pool.wait_ge(values_out, 2 + G * R * UNITS)
                else:
                    pool.wait_ge(seq_used, b - NBUF + 1)
                gather_selection(b)

        N_STORED = 1 + 2 * (DB + 1) + 1 + 1 + DB + 1

        @block.sync
        def _(sp):
            def store_y(t):
                rows, y = ((P, y_prompt[0, t * P:(t + 1) * P]) if t < NT else
                           (NS, y_sample.rearrange("b t c -> (b t) c")))
                sp.wait_ge(y_made, t + 1)
                sp.dma_start(y, y_rows[t % 2][0:rows]).then_inc(y_stored[t % 2], 16)

            def vec_load(out, in_):
                sp.dma_start(out, in_).then_inc(vec_in, 16)

            sp.dma_start(page_i[:, 0:DB], page_table.rearrange("b i -> i b"), allow_slow_non_contiguous=True).then_inc(page_in, 16)
            w1_rows = phi_w1.rearrange("l (c j) k d h -> j k d (l c) h", j=2)
            for j in range(2):
                for k in range(2):
                    sp.dma_start(w1[j * d:(j + 1) * d, :, k, :], w1_rows[j, k]).then_inc(phi_in, 16)
            sp.dma_start(w2[:], phi_w2.rearrange("l k h d -> h (l k) d")).then_inc(phi_in, 16)
            vec_load(c_rows[0:1, :], c_prompt)
            vec_load(c_rows[1:NB, :], c_sample)
            r = 0
            for src, n in ((b_ada, 3 * KC), (norm_w, KC), (gn_pool, PW // P), (gn_nsa, NW // P)):
                vec_load(vec[r:r + n, :], src.rearrange("l (n p) -> (l n) p", p=P))
                r += n
            pe_rows = phi_pe.rearrange("l (c j) k d -> k (l c) j d", j=2)
            for k in range(2):
                vec_load(vec[r + k * 2 * JP:r + (k + 1) * 2 * JP, :].rearrange("c (j d) -> c j d", j=2), pe_rows[k])
            sp.dma_start(x_rows[:, 0:NT, :], x_prompt[0].rearrange("(t p) c -> p t c", p=P)).then_inc(x_in, 16)
            sp.dma_start(x_rows[0:NS, NT, :], x_sample.rearrange("b t c -> (b t) c")).then_inc(x_in, 16)
            sp.wait_ge(ident_made, 1)
            for n in range(len(POOL_WINDOWS)):
                a, b = n % 2 * d, n // 2
                sp.dma_start(pool_bd[a:a + d, b, a:a + d], pool_w[0, n]).then_inc(mix_in, 16)
            sp.dma_start(scale_row[:], pool_scale[0:1, :].to_broadcast([P, PW])).then_inc(mix_in, 16)
            sp.dma_start(hist_rows[:], state_pool[0].rearrange("b h c -> (b h) c")).then_inc(mix_in, 16)
            n_ada = 3 * D // 512
            for n in range(n_ada + len(IN_BLOCKS)):
                if n >= 2:
                    if n - 2 < n_ada:
                        sp.wait_ge(ada_used, n - 1)
                    else:
                        sp.wait_ge(job_done, block_jobs[n - 2 - n_ada])
                c0, width = (n * 512, 512) if n < n_ada else IN_BLOCKS[n - n_ada]
                src = (w_ada if n < n_ada else w_in)[0, :, c0:c0 + width]
                sp.dma_start(wcols[n % 2][:, :, 0:width], src.rearrange("(c p) n -> p c n", p=P)).then_inc(wcols_in[n % 2], 16)
                if n - n_ada == 3:
                    sp.wait_ge(job_out[1], by[first_job[1] - 1][1])
                    sp.dma_start(new_cmp_p[0, 0].rearrange("(t p) k g d -> p t (k g d)", p=P),
                                 cmp_new[:, 0:NT, :]).then_inc(cmp_stored, 16)
                    sp.dma_start(new_cmp_s[0].rearrange("b t k g d -> (b t) (k g d)"),
                                 cmp_new[0:NS, NT, :]).then_inc(stored, 16)
                if n - n_ada == 4:
                    sp.wait_ge(cmp_stored, 16)
                    sp.dma_start(xp[:].rearrange("p j c -> p (j c)"),
                                 new_cmp_p[0, 0].rearrange("(s j) k g d -> s (j k g d)", j=ST)).then_inc(xp_in, 16)
            sp.wait_ge(job_out[1], by[first_job[3] - 1][1])
            for n, (prompt, sample) in enumerate(((new_slc_p, new_slc_s[0]), (new_win_p, new_win_s[0, :, WIN - TS:]))):
                sp.dma_start(prompt[0, 0].rearrange("(t p) k g d -> p t (k g d)", p=P),
                             kv[:, 0:NT, n * KV:(n + 1) * KV]).then_inc(stored, 16)
                for b in range(DB):
                    sp.dma_start(sample[b].rearrange("t k g d -> t (k g d)"),
                                 kv[b * TS:(b + 1) * TS, NT, n * KV:(n + 1) * KV]).then_inc(stored, 16)
            sp.dma_start(new_win_s[0, :, 0:WIN - TS].rearrange("b t k g d -> b (t k g d)"),
                         state_win_kv[0, :, TS:WIN].rearrange("b t k g d -> b (t k g d)")).then_inc(stored, 16)
            sp.wait_ge(job_out[1], by[first_job[5] - 1][1] if by[first_job[5] - 1][0] == 1 else count[1])
            for to in range(2):
                for fr in range(2):
                    sp.dma_start(q_heads[to * d:(to + 1) * d, fr:H:2, :], qS[fr * d:(fr + 1) * d, :, :]).then_inc(q_moved, 16)
            sp.wait_ge(job_done, block_jobs[-1])
            with sp.Fori(0, G) as g:
                for r in range(R):
                    sp.wait_ge(scores, g * (UNITS * R) + (UNITS * r + UNITS))
                    sp.dma_start(q_head[r % 2][:], qT[r % 2 * d:(r % 2 + 1) * d, bass.ds(g * (R // 2) + r // 2, 1), :]
                                 .rearrange("p a t -> p (a t)")).then_inc(q_in[r % 2], 16)
            sp.wait_ge(u_last_out, 1)
            sp.dma_start(new_pool_p[0, 0], u_last[0:HIST, 0, :]).then_inc(stored, 16)
            for b in range(DB):
                sp.dma_start(new_pool_s[0, b, HIST - TS:], u_last[b * TS:(b + 1) * TS, 1, :]).then_inc(stored, 16)
            sp.dma_start(new_pool_s[0, :, 0:HIST - TS], state_pool[0, :, TS:]).then_inc(stored, 16)
            sp.wait_ge(gates_made, 1)
            sp.dma_start(gate_dram, gates[0:NS, NT, :]).then_inc(gates_stored, 16)
            sp.wait_ge(gates_stored, 16)
            for h in range(H):
                sp.dma_start(gate_rows[h * TS:(h + 1) * TS], gate_dram[:, 3 * h:3 * h + 3]
                             .rearrange("(b t) a -> t b a", t=TS)).then_inc(gates_in, 16)
            sp.wait_ge(mixed, 1)
            sp.wait_ge(stored, 16 * N_STORED)
            def load_window(b):
                u = b % NBUF
                sp.dma_start(win_rows[u][:].rearrange("p j c -> p (j c)"),
                             state_win_kv[0, b].rearrange("(p j) k g d -> p (j k g d)", j=WJ)).then_inc(win_in[u], 16)
                for n, rows in enumerate((new_slc_s[0], new_win_s[0, :, WIN - TS:])):
                    sp.dma_start(new_v[u][:, n, :], rows[b, :, 1].rearrange("t g d -> t (g d)")).then_inc(win_in[u], 16)

            for b in range(DB + NBUF):
                if b < DB:
                    if b == 2:
                        sp.wait_ge(values_out, 2 + G * R * UNITS)
                    if b >= NBUF:
                        sp.wait_ge(seq_used, b - NBUF + 1)
                    load_window(b)
                if b >= NBUF:
                    n = b - NBUF
                    sp.wait_ge(out_made, n + 1)
                    sp.dma_start(out_dram[n], out_rows[n % NBUF][:]).then_inc(out_stored[n % NBUF], 16)
                    if n == DB - 2:
                        sp.dma_start(norm_row[:], final_norm.rearrange("(a n) -> a n", a=1).to_broadcast([P, D]))\
                            .then_inc(norm_in, 16)
                    if n == DB - NBUF:
                        sp.dma_start(w_o[:], w_out[0].rearrange("(c p) n -> p c n", p=P)).then_inc(w_o_in, 16)
            for u in range(NBUF):
                sp.wait_ge(out_stored[u], 16 * (len(range(u, DB, NBUF)) + 1))
            for b in range(DB):
                sp.dma_start(nsa[b * TS:(b + 1) * TS, NT, :].rearrange("t (h c) -> t h c", c=d),
                             out_dram[b].rearrange("(h t) c -> t h c", t=TS)).then_inc(nsa_in, 16)
            for t in range(NT + 1):
                rows, x = ((P, x_prompt[0, t * P:(t + 1) * P]) if t < NT else
                           (NS, x_sample.rearrange("b t c -> (b t) c")))
                if t >= 2:
                    sp.wait_ge(y_made, t - 1)
                sp.dma_start(x_again[t % 2][0:rows], x).then_inc(x_again_in[t % 2], 16)
                if t >= 1:
                    store_y(t - 1)
            store_y(NT)
            for u in range(2):
                sp.wait_ge(y_stored[u], 16 * ((NT + 2 - u) // 2))

        @block.tensor
        def _(pe):
            pe.wait_ge(pages_made, 1)
            pe.wait_ge(page_cast, 1)
            pe.matmul(ps[:, 1, 0:DB + 1], sel_page[:], page_f[:], start=True, stop=True).then_inc(turned_small, 1)
            pe.wait_ge(ident_made, 1)
            pe.wait_ge(vec_in, 16 * 8)
            pe.transpose(ps[:, 0, 0:NVEC], vec[:], ident[0:NVEC, 0:NVEC]).then_inc(turned_small, 1)
            pe.wait_ge(silu_c, 1)
            for c in range(KC):
                last = pe.transpose(ps[:, 2, c * NB:(c + 1) * NB], c_silu[:, c * P:(c + 1) * P], ident[0:NB, 0:NB])
            last.then_inc(turned_small, 1)
            pe.wait_ge(vec_made, 1)
            pe.wait_ge(phi_in, 16 * 5)
            pe0 = 5 * KC
            for c in range(2 * JP):
                last = pe.matmul(ps[0:2, 3, 0:2 * HID], vec_t[:, pe0 + c:pe0 + 2 * JP + c + 1:2 * JP],
                                 w1[:, c].rearrange("p k h -> p (k h)"), start=(c == 0), stop=(c == 2 * JP - 1))
            last.then_inc(pe_sum, 1)
            pe.wait_ge(pe_rows_made, 1)
            for k in range(2):
                last = pe.transpose(ps[:, 3, 2 * HID + 2 * k:2 * HID + 2 * k + 2], pe_rows_sum[:, k * HID:(k + 1) * HID],
                                    ident[0:2, 0:2])
            last.then_inc(pe_sum, 1)
            pe.wait_ge(pe_bias_made, 1)
            def ada_block(n):
                pe.wait_ge(wcols_in[n % 2], 16 * (n // 2 + 1))
                if n >= 2:
                    pe.wait_ge(comp_v_out, 2)
                for q in range(4):
                    m = G * d + (n * 4 + q) * NB
                    for c in range(KC):
                        last = pe.matmul(ps[:, 7, m:m + NB], wcols[n % 2][:, c, q * P:(q + 1) * P],
                                         cs_t[:, c, :], start=(c == 0), stop=(c == KC - 1))
                last.then_inc(ada_used, 1)

            def second_layer(b):
                pe.wait_ge(hidden, b * 2 + 3)
                pe.wait_ge(comp_k_out, b + 1)
                pe.wait_ge(comp_v_out, b + 1)
                pe.matmul(ps[0:d, 6, 0:G * NC], w2[:, 0, :], hid[:, 0].rearrange("p g n -> p (g n)"),
                          start=True, stop=True)
                for g in range(G):
                    last = pe.matmul(ps[0:NC, 7, g * d:(g + 1) * d], hid[:, 1, g, :], w2[:, 1, :],
                                     start=True, stop=True)
                last.then_inc(comp_sum, 1)

            def compress(i, u, first=False, ada_at={}):
                b = i * 2 + u
                pe.wait_ge(cache_in[u], i * 16 + 16)
                for s in range(JP + 1):
                    if s in ada_at:
                        ada_block(ada_at[s])
                    if s < JP:
                        n = i * (2 * JP) + (u * JP + s)
                        for j in range(2):
                            bank = 2 * j + s % 2
                            pe.wait_ge(pairs_out[j], n + 1)
                            for c in range(KV // P):
                                last = pe.transpose(ps[:, bank, c * P:(c + 1) * P],
                                                    caches[u][:, 2 * s + j, c * P:(c + 1) * P], ident[:])
                            last.then_inc(pairs_turned[j], 1)
                    if s == 1 and not first:
                        second_layer(b - 1)
                    if s == 0:
                        pe.wait_ge(hidden, b * 2 + 1)
                    if s > 0:
                        n = i * (2 * JP) + (u * JP + s - 1)
                        for j in range(2):
                            pe.wait_ge(pairs_out[j], n + 3)
                        for k in range(2):
                            for m in range(2):
                                last = pe.matmul(ps[:, 4 + k, 0:G * NC].rearrange("p (g n) -> p g n", g=G),
                                                 w1[:, m * JP + s - 1, k, :],
                                                 xt[(s - 1) % NXT][:, k * G:(k + 1) * G, m:m + NC],
                                                 start=(s == 1 and m == 0), stop=(s == JP and m == 1))
                        last.then_inc(pairs_used, 1)

            n_ada = 3 * D // 512
            assert n_ada == 6
            pe.wait_ge(cs_made, 1)
            compress(0, 0, first=True)
            for e in range(2):
                pe.wait_ge(pairs_out[e], JP + 2)
            pe.wait_ge(mix_in, 16 * 6)
            for m in range(PW // P):
                last = pe.transpose(ps[:, 0, m * DB * HIST:(m + 1) * DB * HIST], hist_rows[:, m * P:(m + 1) * P],
                                    ident[0:DB * HIST, 0:DB * HIST])
            last.then_inc(turned_small, 1)
            for n in range(2):
                ada_block(n)
            pe.wait_ge(hist_out, 1)
            compress(0, 1, ada_at={3: 2, 5: 3, 7: 4})
            ada_block(5)
            with pe.Fori(0, DB // 2 - 1) as i:
                for u in range(2):
                    compress(i + 1, u)
            second_layer(DB - 1)
            for e in range(2):
                pe.wait_ge(pairs_out[e], DB * JP + 2)
            pe.wait_ge(xhat_made, 1)
            for n in range(2 * (NT + 1)):
                t, half = n // 2, n % 2
                rows = P if t < NT else NS
                if n >= 4:
                    pe.wait_ge(x_out[1 - half], n // 2 - 1)
                for c in range(4):
                    ch = half * 4 + c
                    last = pe.transpose(ps[:, 1 + n % 4, c * rows:(c + 1) * rows],
                                        x_rows[0:rows, t, ch * P:(ch + 1) * P], ident[0:rows, 0:rows])
                last.then_inc(x_turned, 1)
            def compress_prompt():
                pe.wait_ge(xp_in, 16)
                for e in range(2):
                    pe.wait_ge(job_out[e], max(by[j][1] for j in range(xp_job) if by[j][0] == e))
                for s in range(JP):
                    for j in range(2):
                        if s >= 3:
                            pe.wait_ge(xp_out[j], s - 2)
                        for c in range(KV // P):
                            last = pe.transpose(ps[:, xp_bank[s % 3][j], c * PSTR:(c + 1) * PSTR],
                                                xp[:, 2 * s + j, c * P:(c + 1) * P], ident[0:PSTR, 0:PSTR])
                        last.then_inc(xp_turned, 1)
                for c in range(JP):
                    for e in range(2):
                        pe.wait_ge(xp_out[e], c + 1)
                    for k in range(2):
                        for m in range(2):
                            last = pe.matmul(ps[:, hid_p_bank[k], 0:G * PC].rearrange("p (g n) -> p g n", g=G),
                                             w1[:, m * JP + c, k, :], xpt[:, c, k * G:(k + 1) * G, m:m + PC],
                                             start=(c == 0 and m == 0), stop=(c == JP - 1 and m == 1))
                last.then_inc(hid_p_sum, 1)

            pe.wait_ge(x_out[0], NT)
            pe.wait_ge(x_out[1], NT + 2)
            pe.wait_ge(hidden, 1 + 2 * DB)
            pe.wait_ge(comp_k_out, 1 + DB)
            pe.wait_ge(comp_v_out, 1 + DB)
            for j, (n, turned, col, width, t, what, _) in enumerate(jobs):
                if j == xp_job:
                    compress_prompt()
                if j % 8 in hid_p_bank and xp_job <= j < xp_job + 8:
                    pe.wait_ge(hid_p_made, hid_p_bank.index(j % 8) + 1)
                if j == first_job[n]:
                    pe.wait_ge(wcols_in[(n + n_ada) % 2], 16 * ((n + n_ada) // 2 + 1))
                if j >= 8:
                    pe.wait_ge(job_out[by[j - 8][0]], by[j - 8][1])
                w = wcols[(n + n_ada) % 2]
                for c in range(KC):
                    flags = dict(start=(c == 0), stop=(c == KC - 1))
                    if turned:
                        rows = slice(0, T) if what == "prompt" else slice(T, T + NS)
                        last = pe.matmul(ps[:, j % 8, 0:rows.stop - rows.start], w[:, c, col:col + P], hT[:, c, rows], **flags)
                    else:
                        rows = P if t < NT else NS
                        last = pe.matmul(ps[0:rows, j % 8, 0:width], hT[:, c, t * P:t * P + rows],
                                         w[:, c, col:col + width], **flags)
                last.then_inc(job_done, 1)
            for e in range(2):
                pe.wait_ge(job_out[e], count[e])
            pe.wait_ge(hid_p_made, 2)
            pe.matmul(ps[0:d, 7, 0:G * PC], w2[:, 0, :], hid_p[:, 0].rearrange("p g n -> p (g n)"),
                      start=True, stop=True)
            for g in range(G):
                last = pe.matmul(ps[0:PC, 7, P + g * d:P + (g + 1) * d], hid_p[:, 1, g, :], w2[:, 1, :], start=True, stop=True)
            last.then_inc(pcomp_sum, 1)
            for m in range(PW // P):
                pe.transpose(ps[0:HIST, 6, m * P:(m + 1) * P], uT[:, m, T - HIST:], ident[:])
                last = pe.transpose(ps[0:NS, 6, PW + m * P:PW + (m + 1) * P], uS[:, m, :], ident[:])
            last.then_inc(u_last_turned, 1)
            for n in range(2 * G):
                s, g = divmod(n, G)
                for t in range(NT):
                    last = pe.transpose(ps[0:d, n, t * P:(t + 1) * P], kv[:, t, s * KV + g * d:s * KV + (g + 1) * d], ident[:])
                last.then_inc(kt_turned, 1)
            pe.wait_ge(u_last_out, 1)
            for e in range(2):
                pe.wait_ge(kt_made[e], G)
            pe.wait_ge(pcomp_made, 1)
            N = R * UNITS

            def attend_step(g, step, more=True):
                if more:
                    r, t = divmod(step % N, UNITS)
                    t -= 1
                    q = q_head[r % 2]
                    pe.wait_ge(probs_made, g * N + (step + 1))
                    if t < 0:
                        pe.wait_ge(q_in[r % 2], g * (16 * R // 2) + (16 * (r // 2 + 1) + step // N * (16 * R // 2)))
                    pe.sem_inc(passed, 1)
                    if t < 0:
                        for tt in range(NT):
                            last = pe.matmul(ps[:, step % 2 * 2, tt * PC:(tt + 1) * PC], q[:, tt * P:(tt + 1) * P],
                                             pcomp_k[:, bass.ds((g + step // N) * PC, PC)], start=True, stop=True)
                    else:
                        for s in range(2):
                            last = pe.matmul(ps[:, step % 2 * 2 + s, 0:(t + 1) * P], q[:, t * P:(t + 1) * P],
                                             kT[:, s, bass.ds(g + step // N, 1), 0:(t + 1) * P].rearrange("p a n -> p (a n)"),
                                             start=True, stop=True)
                    last.then_inc(scores, 1)
                if step >= 2 and (more or step < N + 2):
                    n = step - 2
                    t = n % UNITS - 1
                    pe.wait_ge(probs_made, g * N + (n + 3))
                    for e in range(2):
                        pe.wait_ge(probs_out[e], g * N + (n + 1))
                    if t < 0:
                        for tt in range(NT):
                            last = pe.transpose(ps[0:PC, 4 + tt // 2, tt % 2 * P:(tt % 2 + 1) * P],
                                                cprobs[n % 2][:, tt, :], ident[:])
                    else:
                        for s in range(2):
                            for k in range(t + 1):
                                last = pe.transpose(ps[:, 4 + s, k * P:(k + 1) * P],
                                                    probs[n % 2][:, s, k * P:(k + 1) * P], ident[:])
                    last.then_inc(probs_turned, 1)
                if step >= 3:
                    n = step - 3
                    t = n % UNITS - 1
                    for e in range(2):
                        pe.wait_ge(probs_out[e], g * N + (n + 2))
                    pe.wait_ge(values_out, g * N + (n + 1))
                    pe.sem_inc(passed, 1)
                    bank = ps[:, 6 + n % 2, :]
                    if t < 0:
                        for tt in range(NT):
                            last = pe.matmul(bank[:, tt * d:(tt + 1) * d], cprobs_t[n % 2][:, tt, :],
                                             pcomp_v[0:PC, bass.ds(g * d, d)], start=True, stop=True)
                    else:
                        for s in range(2):
                            for k in range(t + 1):
                                last = pe.matmul(bank[:, s * d:(s + 1) * d], probs_t[n % 2][:, s, k, :],
                                                 kv[:, k, bass.ds(g * d + (s * KV + KV // 2), d)],
                                                 start=(k == 0), stop=(k == t))
                    last.then_inc(values, 1)

            for step in range(3):
                attend_step(0, step)
            with pe.Fori(0, G - 1) as g:
                for step in range(3, N + 3):
                    attend_step(g, step)
            for step in range(3, N + 3):
                attend_step(G - 1, step, more=step < N)
            pe.wait_ge(values_out, 2 + G * N)
            pe.wait_ge(probs_out[0], 1 + G * N)
            pe.wait_ge(probs_out[1], 1 + G * N)
            for n in range(2):
                pe.transpose(ps[:, 7, n * NS:(n + 1) * NS], kv[0:NS, NT, n * KV:n * KV + P], ident[0:NS, 0:NS])
                last = pe.transpose(ps[0:d, 7, (2 + n) * NS:(3 + n) * NS], kv[0:NS, NT, n * KV + P:n * KV + P + d],
                                    ident[0:NS, 0:NS])
            last.then_inc(new_turned, 1)
            pe.wait_ge(new_t_made, 1)
            pe.wait_ge(mixed, 1)
            def compressed_scores(b):
                pe.wait_ge(staged, b + 1)
                pe.sem_inc(passed, 1)
                for g in range(G):
                    lhs = (q01[0:d, 0:R * TS], q01[d:P, R * TS:], q2[0:d, 0:R * TS])[g]
                    keys = (ckeys[0:d, 0, 0:NC], ckeys[d:P, 0, 0:NC], ckeys[0:d, 1, 0:NC])[g]
                    last = pe.matmul(ps[g * R * TS:(g + 1) * R * TS, 0, 0:NC], lhs, keys, start=True, stop=True)
                last.then_inc(cscores, 1)

            def turn_keys(b, u, nth, m):
                j4 = TURN_ORDER[m]
                rows, j0 = (seq_rows[u], 4 * j4) if j4 < ST // 4 else (win_rows[u], 0)
                if m == 0:
                    pe.wait_ge(win_in[u], nth * 48 + 48)
                if m == 1:
                    pe.wait_ge(seq_in[u], nth * 16 + 16)
                for two in range(2):
                    if m > 0:
                        pe.wait_ge(keys_out, b * KT_TURNS + (2 * m + two - 1))
                    pe.sem_inc(passed, 1)
                    for j in range(4):
                        if two:
                            last = pe.transpose(ps[0:d, 6, j * P:(j + 1) * P], rows[:, j0 + j, P:P + d], ident[:])
                        else:
                            last = pe.transpose(ps[:, 5, j * P:(j + 1) * P], rows[:, j0 + j, 0:P], ident[:])
                    last.then_inc(keys_turned, 1)

            def turn_compressed(b):
                pe.wait_ge(keys_out, (b + 1) * KT_TURNS)
                pe.wait_ge(cp_made, b + 1)
                pe.transpose(ps[0:NC, 6, 0:GR], cp[:], ident[0:GR, 0:GR])
                pe.matmul(ps[0:G * TS, 6, P:P + NC], sel_sum_r[:].rearrange("p g t -> p (g t)"), cp[:],
                          start=True, stop=True).then_inc(cp_turned, 1)

            def attend(b, u, next_nth):
                more = next_nth is not None
                def new_scores(n):
                    bank = ps[:, 3 + n, 4 * GR:5 * GR]
                    pe.matmul(bank[:, 0:2 * R * TS], new_pad01[:, n, :], q01[:], start=True, stop=True)
                    return pe.matmul(bank[:, 2 * R * TS:], new_pad2[:, n, :], q2[0:d, 0:R * TS], start=True, stop=True)

                for j2 in range((ST + WJ) // 2):
                    if j2 == ST // 4:
                        pe.wait_ge(cp_out, b + 1)
                        pe.sem_inc(passed, 1)
                        pe.matmul(ps[0:GR, 7, 0:G * d], cp_t[:], comp_v[0:NC, bass.ds(b, 1), :].rearrange("p a c -> p (a c)"),
                                  start=True, stop=True).then_inc(cvalues, 1)
                    if j2 == ST // 2:
                        new_scores(0).then_inc(seq_scores, 1)
                    win = j2 >= ST // 2
                    jj = j2 - ST // 2 if win else j2
                    bank = ps[:, 4 if win else jj // 2, :]
                    at0 = 2 * jj * GR if win else jj % 2 * 2 * GR
                    k01, k2 = (wkey_t01, wkey_t2) if win else (key_t01, key_t2)
                    for a in range(2):
                        pe.matmul(bank[:, at0 + a * GR:at0 + a * GR + 2 * R * TS], k01[:, 2 * jj + a, :], q01[:],
                                  start=True, stop=True)
                    pe.matmul(bank[:, at0:at0 + 2 * GR].rearrange("p (a c) -> p a c", a=2)[:, :, 2 * R * TS:],
                              k2[:, jj, :], q2[:], start=True, stop=True)
                new_scores(1)
                pe.wait_ge(chosen_made, b + 1)
                pe.wait_ge(cvalues_out, b + 1)
                pe.matmul(ps[:, 7, 2 * P:2 * P + GR], chosen[:], sel_rep_r[:].rearrange("p g r t -> p (g r t)"),
                          start=True, stop=True).then_inc(rest_scores, 1)
                if more:
                    for m in range(2):
                        turn_keys(b + 1, (u + 1) % NBUF, next_nth, m)
                else:
                    for c in range(KC):
                        last = pe.transpose(ps[0:NB, 5 + c // 4, c % 4 * P:(c % 4 + 1) * P], ada_t[:, 2 * KC + c, :],
                                            ident[:])
                    last.then_inc(gate_turned, 1)
                pe.wait_ge(peaks_made, b + 1)
                for n in range(2):
                    last = pe.transpose(ps[0:GR, 7, n * P:(n + 1) * P], peak2[:, n, :], ident[:])
                last.then_inc(peaks_turned, 1)
                if more:
                    turn_keys(b + 1, (u + 1) % NBUF, next_nth, 2)
                pe.wait_ge(diag_made, b + 1)
                pe.matmul(ps[:, 7, 2 * P:2 * P + 2 * GR], ones[0:GR, :], peak_diag[:].rearrange("p a c -> p (a c)"),
                          start=True, stop=True).then_inc(peaks_spread, 1)
                if more:
                    turn_keys(b + 1, (u + 1) % NBUF, next_nth, 3)
                for a in range(ST // 4):
                    pe.wait_ge(seq_exp, b * EXPS + (a + 1))
                    for j in range(4 * a, 4 * a + 4):
                        pe.matmul(ps[0:GR, 7, 0:G * d], sc[:, j, :], seq_rows[u][:, j, KV // 2:], start=(j == 0), stop=False)
                    if more and a == 1:
                        turn_keys(b + 1, (u + 1) % NBUF, next_nth, 4)
                    elif more and a == 2:
                        compressed_scores(b + 1)
                pe.wait_ge(seq_exp, b * EXPS + EXPS)
                pe.matmul(ps[0:GR, 7, 0:G * d], sc[0:TS, ST, :], new_v[u][:, 0, :], start=False, stop=True)
                for j in range(WJ):
                    pe.matmul(ps[0:GR, 7, G * d:2 * G * d], sc[:, SL + j, :], win_rows[u][:, j, KV // 2:],
                              start=(j == 0), stop=False)
                pe.matmul(ps[0:GR, 7, G * d:2 * G * d], sc[0:TS, SL + WJ, :], new_v[u][:, 1, :],
                          start=False, stop=True).then_inc(seq_used, 1)
                if not more:
                    pe.wait_ge(gate_copied, 1)
                    for n in range(2):
                        for s in range(2):
                            rows, sel = ((P, sel_prompt), (NS, sel_seq))[s]
                            last = pe.matmul(ps[0:rows, 2 * s + n, :], sel[:], gate_bc[:, n * 512:(n + 1) * 512],
                                             start=True, stop=True)
                    last.then_inc(gate_spread, 1)
                pe.wait_ge(sums_made, b + 1)
                for n in range(2):
                    last = pe.matmul(ps[0:GR, 7, 2 * G * d + n:2 * G * d + n + 1], sum2[:, n, :], ones[:, 0:1],
                                     start=True, stop=True)
                last.then_inc(seq_values, 1)
                if more:
                    turn_compressed(b + 1)

            compressed_scores(0)
            for m in range(len(TURN_ORDER)):
                turn_keys(0, 0, 0, m)
            turn_compressed(0)
            with pe.Fori(0, DB // NBUF) as i:
                for u in range(NBUF):
                    attend(i * NBUF + u, u, i + (u + 1) // NBUF)
            for b in range(DB // NBUF * NBUF, DB):
                attend(b, b % NBUF, (b + 1) // NBUF if b + 1 < DB else None)
            pe.wait_ge(out_made, DB)
            pe.wait_ge(w_o_in, 16)
            for t in range(NT + 3):
                if t <= NT:
                    rows = P if t < NT else NS
                    if t >= 1:
                        pe.wait_ge(mixed_made, t)
                    if t == 0:
                        pe.wait_ge(gate_made, 1)
                    for m in range(PW // P):
                        mix = uT[:, m, t * P:(t + 1) * P] if t < NT else mix_seq[:, m, :]
                        last = pe.matmul(ps[0:rows, 0, m * P:(m + 1) * P], mix, pool_bd[:, m, :], start=True, stop=True)
                    last.then_inc(pool_values, 1)
                if 1 <= t <= NT + 1:
                    n = t - 1
                    rows = P if n < NT else NS
                    pe.wait_ge(mixed_made, n + 1)
                    for half in range(2):
                        if n >= 1:
                            pe.wait_ge(mixT_made[half], n)
                        for c in range(4):
                            ch = half * 4 + c
                            last = pe.transpose(ps[:, 1 + half, c * rows:(c + 1) * rows],
                                                mixed_rows[n % 2][0:rows, ch * P:(ch + 1) * P], ident[0:rows, 0:rows])
                        last.then_inc(mixed_turned, 1)
                if t >= 2:
                    n = t - 2
                    rows = P if n < NT else NS
                    for half in range(2):
                        pe.wait_ge(mixT_made[half], n + 1)
                    if n >= 2:
                        pe.wait_ge(y_sum, n - 1)
                    for half in range(2):
                        for c in range(KC):
                            last = pe.matmul(ps[0:rows, 3 + n % 2 * 2 + half, :], mixT[n % 2][:, c, 0:rows],
                                             w_o[:, c, half * 512:(half + 1) * 512], start=(c == 0), stop=(c == KC - 1))
                    last.then_inc(projected, 1)

        def copy_pairs(eng, copy, j, n, s):
            eng.wait_ge(pairs_turned[j], n + 1)
            eng.wait_ge(pairs_used, n + 1)
            bank = ps[:, 2 * j + s % 2, 0:KV].rearrange("p (c n) -> p c n", n=P)
            slot = xt[s % NXT][:].rearrange("p (c h) n -> p c h n", h=2)
            copy(slot[j * d:(j + 1) * d, :, 0, :], bank[0:d])
            copy(slot[j * d:(j + 1) * d, :, 1, :], bank[d:P]).then_inc(pairs_out[j], 1)

        def copy_jobs(eng, e):
            copy = eng.copy if e == 0 else eng.tensor_copy
            for j, (n, turned, col, width, t, what, c) in enumerate(jobs):
                if j == xp_job:
                    copy_prompt_pairs(eng, copy, e)
                    if e == 0:
                        for k in range(2):
                            eng.wait_ge(hid_p_sum, 1)
                            eng.activation(hid_p[:, k].rearrange("p g n -> p (g n)"), ps[:, hid_p_bank[k], 0:G * PC],
                                           ACT.Gelu_apprx_tanh, bias=pe_bias[:, k:k + 1]).then_inc(hid_p_made, 1)
                if by[j][0] != e:
                    continue
                eng.wait_ge(job_done, j + 1)
                bank = ps[:, j % 8, :]
                rows = P if t is None or t < NT else NS
                if turned and c < PW:
                    if what == "prompt":
                        last = copy(uT[:, c // P, :], bank[:, 0:T])
                    else:
                        copy(uS[:, c // P, :], bank[:, 0:NS])
                        last = copy(u_seq[:, c // P, :, HIST:], bank[:, 0:NS].rearrange("p (b t) -> p b t", t=TS))
                elif turned:
                    last = copy((qT if what == "prompt" else qS)[:, (c - C_Q) // P, :],
                                bank[:, 0:T if what == "prompt" else NS])
                elif n == 0:
                    last = copy(cmp_new[0:rows, t, :], bank[0:rows, 0:KV])
                elif n < 3:
                    last = copy(kv[0:rows, t, (n - 1) * KV:(n - 1) * KV + width], bank[0:rows, 0:width])
                else:
                    c_gate = c - PW if c < C_Q else c - C_ZN + PW
                    last = eng.activation(z_gate[0:rows, t, c_gate:c_gate + width], bank[0:rows, 0:width], ACT.Silu)
                last.then_inc(job_out[e], 1)

        def copy_keys(eng, copy, e):
            eng.wait_ge(u_last_turned, 1)
            eng.wait_ge(cmp_stored, 16)
            eng.wait_ge(stored, 16)
            eng.wait_ge(q_moved, 64)
            for n in range(2 * G):
                if n % 2 != e:
                    continue
                s, g = divmod(n, G)
                eng.wait_ge(kt_turned, n + 1)
                copy(kT[:, s, g, :], ps[0:d, n, :]).then_inc(kt_made[e], 1)

        def copy_prompt_pairs(eng, copy, j):
            for s in range(JP):
                eng.wait_ge(xp_turned, 2 * s + j + 1)
                bank = ps[:, xp_bank[s % 3][j], 0:KV // P * PSTR].rearrange("p (c n) -> p c n", n=PSTR)
                slot = xpt[:, s].rearrange("p (c h) n -> p c h n", h=2)
                copy(slot[j * d:(j + 1) * d, :, 0, :], bank[0:d])
                copy(slot[j * d:(j + 1) * d, :, 1, :], bank[d:P]).then_inc(xp_out[j], 1)

        def compressed_exp(act, b):
            act.wait_ge(cpeaks, b + 1)
            act.activation(cp[:], ps[0:GR, 0, 0:NC], ACT.Exp, bias=cpeak[:, 0:1], scale=SCALE,
                           accum_out=cpeak[:, 1:2]).then_inc(cexp, 1)

        def copy_turned_keys(act, b, m):
            j4 = TURN_ORDER[m]
            for two in range(2):
                act.wait_ge(keys_turned, b * KT_TURNS + (2 * m + two + 1))
                if two:
                    dst = key_t2[:, 2 * j4:2 * j4 + 2, :] if j4 < ST // 4 else wkey_t2[:]
                    rows = ps[0:d, 6, :].rearrange("p (a h n) -> p a h n", h=2, n=P)
                    act.copy(dst[0:d], rows[:, :, 0])
                    last = act.copy(dst[d:P], rows[:, :, 1])
                else:
                    dst = key_t01[:, 4 * j4:4 * j4 + 4, :] if j4 < ST // 4 else wkey_t01[:]
                    last = act.copy(dst.rearrange("p j n -> p (j n)"), ps[:, 5, :])
                last.then_inc(keys_out, 1)

        def sequence_exp(act, b, more):
            if more:
                for m in range(3):
                    copy_turned_keys(act, b + 1, m)
            for a in range(EXPS):
                act.wait_ge(shifted, b * EXPS + (a + 1))
                part = sc[:, 4 * a:4 * a + 4, :] if a < ST // 4 else sc[:, ST:, :]
                part = part.rearrange("p j c -> p (j c)")
                act.activation(part, part, ACT.Exp, scale=SCALE).then_inc(seq_exp, 1)
            if more:
                for m in range(3, len(TURN_ORDER)):
                    copy_turned_keys(act, b + 1, m)
                compressed_exp(act, b + 1)

        @block.scalar
        def _(act):
            own_step = Steps(act, act_own)
            act.sem_inc(pairs_out[0], 2)
            act.sem_inc(pairs_used, NXT)
            act.sem_inc(hidden, 1)
            act.sem_inc(probs_made, 2)
            act.sem_inc(probs_out[1], 1)
            act.wait_ge(vec_in, 16 * 8)
            act.activation(c_silu[:], c_rows[:], ACT.Silu).then_inc(silu_c, 1)
            act.wait_ge(pe_bias_made, 1)

            def copy_values(b):
                act.wait_ge(comp_sum, b + 1)
                act.copy(comp_v[0:NC, b, :], ps[0:NC, 7, 0:G * d]).then_inc(comp_v_out, 1)

            def compress(i, u, first=False):
                b = i * 2 + u
                for s in range(JP):
                    copy_pairs(act, act.copy, 0, i * (2 * JP) + (u * JP + s), s)
                    if s == 1 and not first:
                        copy_values(b - 1)
                act.wait_ge(pairs_used, i * (2 * JP) + ((u + 1) * JP + NXT))
                for k in range(2):
                    act.activation(hid[:, k].rearrange("p g n -> p (g n)"), ps[:, 4 + k, 0:G * NC],
                                   ACT.Gelu_apprx_tanh, bias=pe_bias[:, k:k + 1]).then_inc(hidden, 1)

            compress(0, 0, first=True)
            act.wait_ge(sumsq_made, 1)
            act.wait_ge(x_in, 32)
            for t in range(NT + 1):
                rows = P if t < NT else NS
                own_step.done(act.activation(x_sq[0:rows], x_rows[0:rows, t, :], ACT.Square,
                                             accum_out=sumsq[0:rows, t:t + 1]))
            act.drain().then_inc(sumsq_made, 1)
            act.wait_ge(ms_made, 1)
            act.sqrt(rstd[:], rstd[:]).then_inc(rstd_root, 1)
            compress(0, 1)
            with act.Fori(0, DB // 2 - 1) as i:
                for u in range(2):
                    compress(i + 1, u)
            copy_values(DB - 1)
            act.wait_ge(ada_made, 1)
            for t in range(NT):
                act.wait_ge(x_turned, 2 * t + 2)
                for c in range(4):
                    last = act.activation(hT[:, 4 + c, t * P:(t + 1) * P], ps[:, 1 + (2 * t + 1) % 4, c * P:(c + 1) * P],
                                          ACT.Identity, bias=ada_t[:, 4 + c, 0:1], scale=ada_mul[:, 4 + c, 0:1])
                last.then_inc(x_out[0], 1)
            copy_jobs(act, 0)
            copy_keys(act, act.copy, 0)
            act.wait_ge(job_out[1], by[first_job[3] - 1][1])
            act.activation(gates[:, 0:NT], kv[:, 0:NT, 2 * KV:], ACT.Sigmoid)
            act.activation(gates[0:NS, NT], kv[0:NS, NT, 2 * KV:], ACT.Sigmoid).then_inc(gates_made, 1)
            N = R * UNITS

            def attend_step(g, step, more=True):
                if step >= 2 and (more or step < N + 2):
                    t, u = (step - 2) % UNITS - 1, step % 2
                    act.wait_ge(probs_turned, g * N + (step - 1))
                    if t < 0:
                        last = act.copy(cprobs_t[u][:, 2:4, :].rearrange("p a b -> p (a b)"), ps[0:PC, 5, 0:2 * P])
                    else:
                        last = act.copy(probs_t[u][:, 1, 0:t + 1, :].rearrange("p a b -> p (a b)"),
                                        ps[:, 5, 0:(t + 1) * P])
                    last.then_inc(probs_out[1], 1)
                if more:
                    t, u = step % UNITS - 1, step % 2
                    act.wait_ge(peaks, g * N + (step + 1))
                    if t < 0:
                        last = act.activation(cprobs[u][:], cprobs[u][:], ACT.Exp, scale=SCALE)
                    else:
                        for s in range(2):
                            last = act.activation(probs[u][:, s, 0:(t + 1) * P], ps[:, u * 2 + s, 0:(t + 1) * P],
                                                  ACT.Exp, bias=peak[u][:, s:s + 1], scale=SCALE,
                                                  accum_out=total[step % 4][:, s:s + 1])
                    last.then_inc(probs_made, 1)

            for step in range(3):
                attend_step(0, step)
            with act.Fori(0, G - 1) as g:
                for step in range(3, N + 3):
                    attend_step(g, step)
            for step in range(3, N + 3):
                attend_step(G - 1, step, more=step < N)

            compressed_exp(act, 0)
            for m in range(len(TURN_ORDER)):
                copy_turned_keys(act, 0, m)
            with act.Fori(0, DB // NBUF) as i:
                for u in range(NBUF):
                    sequence_exp(act, i * NBUF + u, True)
            for b in range(DB // NBUF * NBUF, DB):
                sequence_exp(act, b, b + 1 < DB)

            def turned_scaled(n):
                rows = P if n < NT else NS
                act.wait_ge(mixed_turned, 2 * n + 1)
                if n >= 2:
                    act.wait_ge(projected, n - 1)
                for c in range(4):
                    last = act.activation(mixT[n % 2][:, c, 0:rows], ps[:, 1, c * rows:(c + 1) * rows],
                                          ACT.Copy, scale=vec_t[:, 4 * KC + c:4 * KC + c + 1])
                last.then_inc(mixT_made[0], 1)

            act.wait_ge(gate_made, 1)
            for t in range(NT + 4):
                if t <= NT:
                    rows = P if t < NT else NS
                    if t == NT:
                        act.wait_ge(nsa_in, 16 * DB)
                    own_step.done(act.activation(osq[0:rows, 0:NW], nsa[0:rows, t, :], ACT.Square,
                                                 accum_out=ostat[0:rows, t, 1:2]))
                    act.wait_ge(pool_values, t + 1)
                    act.activation(osq[0:rows, 0:PW], ps[0:rows, 0, 0:PW], ACT.Square,
                                   accum_out=ostat[0:rows, t, 0:1]).then_inc(osums, 1)
                    act.wait_ge(omeans, t + 1)
                    act.sqrt(orstd[0:rows, t, 0:2], orstd[0:rows, t, 0:2]).then_inc(oroots, 1)
                if 1 <= t <= NT + 1:
                    turned_scaled(t - 1)
                if t >= 3:
                    n = t - 3
                    rows = P if n < NT else NS
                    act.wait_ge(y_sum, n + 1)
                    own_step.done(act.activation(osq[0:rows], y_rows[n % 2][0:rows], ACT.Square,
                                                 accum_out=ostat[0:rows, n, 2:3]))
                    act.sem_inc(ysq, 1)
                    act.wait_ge(ymeans, n + 1)
                    act.sqrt(orstd[0:rows, n, 2:3], orstd[0:rows, n, 2:3]).then_inc(yroots, 1)

        @block.vector
        def _(dve):
            own_step = Steps(dve, dve_own)
            dve.sem_inc(pairs_out[1], 2)
            dve.sem_inc(comp_k_out, 1)
            dve.sem_inc(comp_v_out, 1)
            dve.sem_inc(scores, 2 * UNITS)
            dve.sem_inc(probs_out[0], 1)
            dve.sem_inc(values_out, 2)
            for stored_u in out_stored:
                dve.sem_inc(stored_u, 16)
            dve.memset(sumsq[:], 1.0).then_inc(sumsq_made, 1)
            dve.wait_ge(page_in, 16)
            dve.wait_ge(pages_made, 1)
            dve.tensor_copy(page_f[:, 0:DB], page_i[:, 0:DB]).then_inc(page_cast, 1)
            dve.wait_ge(turned_small, 1)
            own_step.done(dve.scalar_tensor_tensor(out=stride_f[:, DB + 1:DB + 2], in0=ps[:, 1, DB:DB + 1],
                                                   scalar=-float(PPS), in1=stride_f[:, DB:DB + 1],
                                                   op0=ALU.mult, op1=ALU.add))
            own_step.done(dve.tensor_scalar(stride_f[:, 0:DB], ps[:, 1, 0:DB], float(PPS), stride_f[:, DB + 1:DB + 2],
                                            ALU.mult, ALU.add))
            dve.tensor_copy(stride_i[:], stride_f[:, 0:DB]).then_inc(strides_made, 1)
            dve.wait_ge(turned_small, 2)
            dve.tensor_copy(vec_t[:], ps[:, 0, 0:NVEC]).then_inc(vec_made, 1)
            dve.wait_ge(turned_small, 3)
            dve.tensor_copy(cs_t[:].rearrange("p c b -> p (c b)"), ps[:, 2, 0:KC * NB]).then_inc(cs_made, 1)
            dve.wait_ge(pe_sum, 1)
            dve.tensor_copy(pe_rows_sum[:], ps[0:2, 3, 0:2 * HID]).then_inc(pe_rows_made, 1)
            dve.wait_ge(pe_sum, 2)
            dve.tensor_copy(pe_bias[:], ps[:, 3, 2 * HID:2 * HID + 4:3]).then_inc(pe_bias_made, 1)

            def copy_comp_keys(b):
                dve.wait_ge(comp_sum, b + 1)
                keys = ps[0:d, 6, 0:G * NC].rearrange("p (g n) -> p g n", g=G)
                dve.tensor_copy(comp_k[0:d, b], keys[:, 0:G:2])
                dve.tensor_copy(comp_k[d:P, b, 0], keys[:, 1]).then_inc(comp_k_out, 1)

            def compress(i, u, first=False):
                b = i * 2 + u
                for s in range(JP):
                    copy_pairs(dve, dve.tensor_copy, 1, i * (2 * JP) + (u * JP + s), s)
                    if s == 1 and not first:
                        copy_comp_keys(b - 1)

            compress(0, 0, first=True)
            dve.wait_ge(const_made, 1)
            for n, w in enumerate(POOL_WINDOWS):
                a = ramp[n % 2 * d:(n % 2 + 1) * d, n // 2]
                own_step.done(dve.tensor_scalar(a, a, float(w), 1.0 / w, ALU.min, ALU.mult))
            dve.reciprocal(ramp[:], ramp[:]).then_inc(ramp_made, 1)
            dve.wait_ge(mix_in, 16 * 6)
            dve.tensor_tensor(pool_bd[:].rearrange("p a b -> p (a b)"), pool_bd[:].rearrange("p a b -> p (a b)"),
                              scale_row[:], ALU.mult).then_inc(mix_made, 1)
            dve.wait_ge(turned_small, 4)
            for m in range(PW // P):
                last = dve.tensor_copy(u_seq[:, m, :, 0:HIST],
                                       ps[:, 0, m * DB * HIST:(m + 1) * DB * HIST].rearrange("p (b h) -> p b h", h=HIST))
            last.then_inc(hist_out, 1)
            dve.wait_ge(sumsq_made, 2)
            dve.tensor_scalar(rstd[:], sumsq[:], 1.0 / D, EPS, ALU.mult, ALU.add).then_inc(ms_made, 1)
            dve.wait_ge(rstd_root, 1)
            own_step.done(dve.reciprocal(rstd[:], rstd[:]))
            for t in range(NT + 1):
                rows = P if t < NT else NS
                last = dve.tensor_scalar(x_rows[0:rows, t, :], x_rows[0:rows, t, :], rstd[0:rows, t:t + 1], None, ALU.mult)
            last.then_inc(xhat_made, 1)
            compress(0, 1)
            with dve.Fori(0, DB // 2 - 1) as i:
                for u in range(2):
                    compress(i + 1, u)
            copy_comp_keys(DB - 1)
            dve.wait_ge(ada_used, 3 * D // 512)
            dve.wait_ge(comp_v_out, 1 + DB)
            own_step.done(dve.tensor_tensor(ada_t[:], ps[:, 7, G * d:G * d + 3 * KC * NB].rearrange("p (c b) -> p c b", b=NB),
                                            vec_t[:, 0:3 * KC].unsqueeze(2).to_broadcast([P, 3 * KC, NB]), ALU.add))
            dve.scalar_tensor_tensor(out=ada_mul[:], in0=ada_t[:, KC:2 * KC, :], scalar=1.0,
                                     in1=vec_t[:, 3 * KC:4 * KC].unsqueeze(2).to_broadcast([P, KC, NB]),
                                     op0=ALU.add, op1=ALU.mult).then_inc(ada_made, 1)
            dve.wait_ge(ada_made, 1)
            for t in range(NT):
                dve.wait_ge(x_turned, 2 * t + 1)
                for c in range(4):
                    last = dve.tensor_scalar(hT[:, c, t * P:(t + 1) * P], ps[:, 1 + 2 * t % 4, c * P:(c + 1) * P],
                                             ada_mul[:, c, 0:1], ada_t[:, c, 0:1], ALU.mult, ALU.add)
                last.then_inc(x_out[1], 1)
            for half in range(2):
                dve.wait_ge(x_turned, 2 * NT + half + 1)
                rows = hT[:, half * 4:half * 4 + 4, T:T + NS].rearrange("p c (b t) -> p c b t", t=TS)
                bank = ps[:, 1 + (2 * NT + half) % 4, 0:4 * NS].rearrange("p (c b t) -> p c b t", b=DB, t=TS)

                def per_seq(a):
                    return a[:, half * 4:half * 4 + 4, 1:NB].unsqueeze(3).to_broadcast([P, 4, DB, TS])

                own_step.done(dve.tensor_tensor(rows, bank, per_seq(ada_mul), ALU.mult))
                dve.tensor_tensor(rows, rows, per_seq(ada_t), ALU.add).then_inc(x_out[1], 1)
            copy_jobs(dve, 1)
            dve.wait_ge(pcomp_sum, 1)
            dve.tensor_copy(pcomp_k[:], ps[0:d, 7, 0:G * PC])
            dve.tensor_copy(pcomp_v[0:PC], ps[0:PC, 7, P:P + G * d]).then_inc(pcomp_made, 1)
            dve.wait_ge(u_last_turned, 1)
            dve.tensor_copy(u_last[0:HIST, 0, :], ps[0:HIST, 6, 0:PW])
            dve.tensor_copy(u_last[:, 1, :], ps[0:NS, 6, PW:]).then_inc(u_last_out, 1)
            copy_keys(dve, dve.tensor_copy, 1)
            N = R * UNITS
            dve.wait_ge(gates_made, 1)
            gates_c = gates[:, 0:NT].rearrange("p t (h a) -> p t h a", a=3)[:, :, :, 0]
            own_step.done(dve.tensor_tensor(gates_c, gates_c, cmp_any[:].unsqueeze(2).to_broadcast([P, NT, H]), ALU.mult))

            def attend_step(g, step, more=True):
                weigh = step >= 3
                t, u = step % UNITS - 1, step % 2
                n = step - 3
                r, tn, un = n // UNITS, n % UNITS - 1, n % 2
                if more:
                    dve.wait_ge(scores, g * N + (step + 1 + 2 * UNITS))
                    if t < 0:
                        last = dve.tensor_tensor(cprobs[u][:], ps[:, u * 2, 0:NT * PC].rearrange("p (t n) -> p t n", n=PC),
                                                 cmp_mask[:], ALU.add)
                    else:
                        diag = ps[:, u * 2:u * 2 + 2, t * P:(t + 1) * P]
                        last = dve.tensor_tensor(diag, diag, causal[:].unsqueeze(1).to_broadcast([P, 2, P]), ALU.add)
                if weigh and tn < 0:
                    last = dve.tensor_reduce(total[n % 4][:], cprobs[un][:], AX, ALU.add)
                elif weigh:
                    last = dve.reciprocal(share[un][:, 0:2], total[n % 4][:, 0:2])
                own_step.done(last)
                if step >= 2 and (more or step < N + 2):
                    tc = (step - 2) % UNITS - 1
                    dve.wait_ge(probs_turned, g * N + (step - 1))
                    if tc < 0:
                        last = dve.tensor_copy(cprobs_t[u][:, 0:2, :].rearrange("p a b -> p (a b)"),
                                               ps[0:PC, 4, 0:2 * P])
                    else:
                        last = dve.tensor_copy(probs_t[u][:, 0, 0:tc + 1, :].rearrange("p a b -> p (a b)"),
                                               ps[:, 4, 0:(tc + 1) * P])
                    last.then_inc(probs_out[0], 1)
                if more and t < 0:
                    last = dve.tensor_reduce(peak[u][:], cprobs[u][:], AX, ALU.max)
                elif more:
                    last = dve.tensor_reduce(peak[u][:, 0:2], ps[:, u * 2:u * 2 + 2, 0:(t + 1) * P], AX, ALU.max)
                if weigh and tn < 0:
                    last = dve.reciprocal(share[un][:], total[n % 4][:])
                elif weigh:
                    last = dve.tensor_tensor(share[un][:, 0:2], share[un][:, 0:2],
                                             gates[:, tn, bass.ds(g * (3 * R) + (3 * r + 1), 2)], ALU.mult)
                own_step.done(last)
                if more and t < 0:
                    dve.tensor_tensor(cprobs[u][:], cprobs[u][:], peak[u][:].unsqueeze(2).to_broadcast([P, NT, PC]),
                                      ALU.subtract).then_inc(peaks, 1)
                elif more:
                    dve.tensor_scalar(peak[u][:, 0:2], peak[u][:, 0:2], -SCALE, None, ALU.mult).then_inc(peaks, 1)
                if weigh and tn < 0:
                    own_step.done(dve.tensor_tensor(
                        share[un][:], share[un][:],
                        gates[:, 0:NT, bass.ds(g * (3 * R) + 3 * r, 1)].rearrange("p t a -> p (t a)"), ALU.mult))
                if weigh:
                    bank = ps[:, 6 + un, :]
                    dve.wait_ge(values, g * N + (n + 1))
                    if tn < 0:
                        dve.tensor_tensor(nsa[:, 0:NT, bass.ds(g * (R * d) + r * d, d)],
                                          bank[:, 0:NT * d].rearrange("p (t c) -> p t c", c=d),
                                          share[un][:].unsqueeze(2).to_broadcast([P, NT, d]),
                                          ALU.mult).then_inc(values_out, 1)
                    else:
                        out = nsa[:, tn, bass.ds(g * (R * d) + r * d, d)]
                        for s in range(2):
                            own_step.done(dve.scalar_tensor_tensor(
                                out=out, in0=bank[:, s * d:(s + 1) * d], scalar=share[un][:, s:s + 1], in1=out,
                                op0=ALU.mult, op1=ALU.add))
                        dve.sem_inc(values_out, 1)

            for step in range(3):
                attend_step(0, step)
            with dve.Fori(0, G - 1) as g:
                own_step.enter(g, 2 * N + R * (NT * 2 + 1))
                for step in range(3, N + 3):
                    attend_step(g, step)
                own_step.leave(G - 1)
            for step in range(3, N + 3):
                attend_step(G - 1, step, more=step < N)
            dve.wait_ge(new_turned, 1)
            dve.tensor_copy(new_t01[:].rearrange("p a n -> p (a n)"), ps[:, 7, 0:2 * NS])
            dve.tensor_copy(new_t2[:].rearrange("p a n -> p (a n)"), ps[0:d, 7, 2 * NS:4 * NS]).then_inc(new_t_made, 1)
            dve.wait_ge(new_t_made, 1)
            dve.memset(q01[:], 0.0)
            dve.memset(q2[:], 0.0)
            dve.memset(new_pad01[:], 0.0)
            dve.memset(new_pad2[:], 0.0)
            own_step.done(dve.memset(groups[:], 0.0))
            dve.wait_ge(gates_in, 16 * H)
            dve.wait_ge(q_moved, 64)
            RT = R * TS
            SEQ_STEPS = 21

            def stage(b):
                for g in range(G):
                    for half in range(2):
                        if g < 2 and half != g:
                            continue
                        parts = slice(half * d, half * d + d)
                        dst = (q01 if g < 2 else q2)[parts, half * RT:(half + 1) * RT].rearrange("p (r t) -> p r t", t=TS)
                        dve.tensor_copy(dst, q_heads[parts, g * R:(g + 1) * R, bass.ds(b * TS, TS)])
                dve.tensor_copy(new_pad01[:, :, 0:TS], new_t01[:, :, bass.ds(b * TS, TS)])
                dve.tensor_copy(new_pad2[:, :, 0:TS], new_t2[:, :, bass.ds(b * TS, TS)])
                dve.tensor_copy(ckeys[0:d, :, 0:NC], comp_k[0:d, bass.ds(b, 1)].rearrange("p a s n -> p (a s) n"))
                dve.tensor_copy(ckeys[d:P, 0, 0:NC], comp_k[d:P, bass.ds(b, 1), 0].rearrange("p a n -> p (a n)"))\
                   .then_inc(staged, 1)

            def compressed_peaks(b):
                dve.wait_ge(cscores, b + 1)
                own_step.done(dve.tensor_reduce(cpeak[:, 2:3], ps[0:GR, 0, 0:NC], AX, ALU.max))
                dve.tensor_scalar(cpeak[:, 0:1], cpeak[:, 2:3], -SCALE, None, ALU.mult).then_inc(cpeaks, 1)

            def compressed_probs(b):
                dve.wait_ge(cexp, b + 1)
                own_step.done(dve.reciprocal(cpeak[:, 3:4], cpeak[:, 1:2]))
                dve.tensor_scalar(cp[:], cp[:], cpeak[:, 3:4], None, ALU.mult).then_inc(cp_made, 1)

            def choose_blocks(b, u, nth):
                dve.wait_ge(cp_turned, b + 1)
                dve.tensor_copy(cp_t[:], ps[0:NC, 6, 0:GR])
                own_step.done(dve.tensor_copy(groups[:, 1:1 + NC], ps[0:G * TS, 6, P:P + NC]))
                dve.sem_inc(cp_out, 1)
                blocks = groups[:, 0:NSTR].rearrange("p (s n) -> p s n", n=SB // ST)
                own_step.done(dve.tensor_reduce(imp[:, 0:NSEL - 1], blocks[:, :, 1:], AX, ALU.add))
                own_step.done(dve.scalar_tensor_tensor(out=imp[:, 0:NSEL - 1], in0=imp[:, 0:NSEL - 1], scalar=2.0,
                                                       in1=blocks[:, :, 0], op0=ALU.mult, op1=ALU.add))
                own_step.done(dve.tensor_tensor(
                    imp[:, 0:NSEL - 1], imp[:, 0:NSEL - 1],
                    groups[:, 1:1 + NSTR].rearrange("p (s n) -> p s n", n=SB // ST)[:, :, SB // ST - 1], ALU.add))
                dve.memset(imp[:, 0:1], FORCE)
                own_step.done(dve.memset(imp[:, NSEL - 2:NSEL], FORCE), passed_dve)
                for n in range(KEEP // 8):
                    own_step.done(dve.max(imp8[:, n * 8:(n + 1) * 8], imp[:]), passed_dve)
                    own_step.done(dve.match_replace(imp[:], imp8[:, n * 8:(n + 1) * 8], imp[:], NEG), passed_dve)
                dve.tensor_scalar(chosen[:].rearrange("p (s n) -> p s n", n=SB // ST),
                                  imp[:, 0:NSEL - 1].unsqueeze(2).to_broadcast([G * TS, NSEL - 1, SB // ST]),
                                  -1.0, NEG, ALU.is_gt, ALU.mult).then_inc(chosen_made, 1)
                dve.wait_ge(cvalues, b + 1)
                dve.wait_ge(out_stored[u], nth * 16 + 16)
                for g in range(G):
                    rows = slice(g * RT, (g + 1) * RT)
                    last = dve.tensor_scalar(out_rows[u][rows], ps[rows, 7, g * d:(g + 1) * d],
                                             gate_rows[rows, bass.ds(b, 1), 0:1].rearrange("p a c -> p (a c)"), None,
                                             ALU.mult)
                own_step.done(last)
                dve.sem_inc(cvalues_out, 1)

            selection = ps[:, 0:4, 0:4 * GR].rearrange("p a (j c) -> p a j c", c=GR)

            def attend(b, u, next_nth):
                more = next_nth is not None
                dve.wait_ge(seq_scores, b + 1)
                dve.tensor_reduce(peak2[:, 0, :], selection.rearrange("p a j c -> p c a j"), mybir.AxisListType.XY, ALU.max)
                own_step.done(dve.tensor_tensor(sc[:, ST, :], ps[:, 3, 4 * GR:5 * GR],
                                                win_mask[:, WJ].rearrange("p h t -> p (h t)"), ALU.add))
                dve.wait_ge(rest_scores, b + 1)
                dve.tensor_tensor(sc[:, SL:, :], ps[:, 4, 0:5 * GR].rearrange("p (j c) -> p j c", c=GR),
                                  win_mask[:].rearrange("p j h t -> p j (h t)"), ALU.add)
                own_step.done(dve.tensor_copy(bias[:], ps[:, 7, 2 * P:2 * P + GR]))
                own_step.done(dve.tensor_tensor(peak2[:, 0, :], peak2[:, 0, :], bias[:], ALU.add))
                dve.tensor_tensor(peak2[:, 0, :], peak2[:, 0, :], sc[:, ST, :], ALU.max)
                dve.tensor_reduce(peak2[:, 1, :], sc[:, SL:, :].rearrange("p j c -> p c j"), AX, ALU.max)\
                   .then_inc(peaks_made, 1)
                dve.wait_ge(peaks_turned, b + 1)
                own_step.done(dve.tensor_reduce(peak_row[:], ps[0:GR, 7, 0:2 * P].rearrange("p (a n) -> p a n", a=2),
                                                AX, ALU.max))
                for n in range(2):
                    last = dve.tensor_scalar(peak_diag[:, n, :], ident[0:GR, 0:GR], peak_row[:, n:n + 1], -1.0,
                                             ALU.mult, ALU.mult)
                last.then_inc(diag_made, 1)
                dve.wait_ge(peaks_spread, b + 1)
                dve.tensor_tensor(sc[:, ST, :], sc[:, ST, :], ps[:, 7, 2 * P:2 * P + GR], ALU.add)
                dve.tensor_copy(win_peak[:], ps[:, 7, 2 * P + GR:2 * P + 2 * GR])
                own_step.done(dve.tensor_tensor(bias[:], bias[:], ps[:, 7, 2 * P:2 * P + GR], ALU.add))
                for a in range(ST // 4):
                    dve.tensor_tensor(sc[:, 4 * a:4 * a + 4, :], selection[:, a], bias[:].unsqueeze(1).to_broadcast([P, 4, GR]),
                                      ALU.add).then_inc(shifted, 1)
                dve.tensor_tensor(sc[:, SL:, :], sc[:, SL:, :], win_peak[:].unsqueeze(1).to_broadcast([P, WL, GR]),
                                  ALU.add).then_inc(shifted, 1)
                if more:
                    stage(b + 1)
                    compressed_peaks(b + 1)
                else:
                    dve.wait_ge(seq_used, b)
                    dve.wait_ge(gate_turned, 1)
                    dve.tensor_copy(gate_bc[:].rearrange("p (a n) -> p a n", a=2), ps[0:NB, 5:7, :]).then_inc(gate_copied, 1)
                dve.wait_ge(seq_exp, b * EXPS + EXPS)
                dve.tensor_reduce(sum2[:, 0, :], sc[:, 0:SL, :].rearrange("p j c -> p c j"), AX, ALU.add)
                dve.tensor_reduce(sum2[:, 1, :], sc[:, SL:, :].rearrange("p j c -> p c j"), AX, ALU.add)\
                   .then_inc(sums_made, 1)
                if more:
                    compressed_probs(b + 1)
                else:
                    dve.wait_ge(gate_spread, 1)
                    dve.tensor_copy(gate_all[:, 0, :].rearrange("p (a n) -> p a n", a=2), ps[:, 0:2, :])
                    dve.tensor_copy(gate_all[0:NS, 1, :].rearrange("p (a n) -> p a n", a=2), ps[0:NS, 2:4, :])\
                       .then_inc(gate_made, 1)
                dve.wait_ge(seq_values, b + 1)
                own_step.done(dve.reciprocal(coef[:, 0:2], ps[0:GR, 7, 2 * G * d:2 * G * d + 2]))
                own_step.done(dve.tensor_tensor(coef[:, 2:4], coef[:, 0:2],
                                                gate_rows[:, bass.ds(b, 1), 1:3].rearrange("p a c -> p (a c)"), ALU.mult))
                for n in range(2):
                    for g in range(G):
                        rows = slice(g * RT, (g + 1) * RT)
                        last = dve.scalar_tensor_tensor(
                            out=out_rows[u][rows], in0=ps[rows, 7, (n * G + g) * d:(n * G + g + 1) * d],
                            scalar=coef[rows, 2 + n:3 + n], in1=out_rows[u][rows], op0=ALU.mult, op1=ALU.add)
                    own_step.done(last)
                dve.sem_inc(out_made, 1)
                if more:
                    choose_blocks(b + 1, (u + 1) % NBUF, next_nth)

            stage(0)
            compressed_peaks(0)
            compressed_probs(0)
            choose_blocks(0, 0, 0)
            with dve.Fori(0, DB // NBUF) as i:
                own_step.enter(i, NBUF * SEQ_STEPS)
                for u in range(NBUF):
                    attend(i * NBUF + u, u, i + (u + 1) // NBUF)
                own_step.leave(DB // NBUF)
            for b in range(DB // NBUF * NBUF, DB):
                attend(b, b % NBUF, (b + 1) // NBUF if b + 1 < DB else None)
            for t in range(NT + 4):
                if t <= NT:
                    rows = P if t < NT else NS
                    dve.wait_ge(osums, t + 1)
                    for n, width in enumerate((PW, NW)):
                        last = dve.tensor_scalar(orstd[0:rows, t, n:n + 1], ostat[0:rows, t, n:n + 1], 1.0 / width, EPS,
                                                 ALU.mult, ALU.add)
                    last.then_inc(omeans, 1)
                    dve.wait_ge(oroots, t + 1)
                    own_step.done(dve.reciprocal(orstd[0:rows, t, 0:2], orstd[0:rows, t, 0:2]))
                    if t >= 2:
                        dve.wait_ge(mixed_turned, 2 * (t - 1))
                    m = mixed_rows[t % 2]
                    dve.scalar_tensor_tensor(out=m[0:rows, 0:PW], in0=ps[0:rows, 0, 0:PW], scalar=orstd[0:rows, t, 0:1],
                                             in1=z_gate[0:rows, t, 0:PW], op0=ALU.mult, op1=ALU.mult)
                    dve.scalar_tensor_tensor(out=m[0:rows, PW:], in0=nsa[0:rows, t, :], scalar=orstd[0:rows, t, 1:2],
                                             in1=z_gate[0:rows, t, PW:], op0=ALU.mult, op1=ALU.mult).then_inc(mixed_made, 1)
                if 1 <= t <= NT + 1:
                    n = t - 1
                    rows = P if n < NT else NS
                    dve.wait_ge(mixed_turned, 2 * n + 2)
                    if n >= 2:
                        dve.wait_ge(projected, n - 1)
                    for c in range(4):
                        last = dve.tensor_scalar(mixT[n % 2][:, 4 + c, 0:rows], ps[:, 2, c * rows:(c + 1) * rows],
                                                 vec_t[:, 4 * KC + 4 + c:4 * KC + 5 + c], None, ALU.mult)
                    last.then_inc(mixT_made[1], 1)
                if t == 3:
                    dve.wait_ge(norm_in, 16)
                    dve.wait_ge(nsa_in, 16 * DB)
                if t >= 3:
                    n = t - 3
                    rows = P if n < NT else NS
                    y = y_rows[n % 2][0:rows]
                    dve.wait_ge(projected, n + 1)
                    if n >= 2:
                        dve.wait_ge(y_stored[n % 2], 16 * (n // 2))
                    own_step.done(dve.tensor_tensor(y.rearrange("p (a n) -> p a n", a=2),
                                                    ps[0:rows, 3 + n % 2 * 2:5 + n % 2 * 2, :],
                                                    gate_all[0:rows, n // NT, :].rearrange("p (a n) -> p a n", a=2), ALU.mult))
                    dve.wait_ge(x_again_in[n % 2], 16 * (n // 2 + 1))
                    dve.tensor_tensor(y, y, x_again[n % 2][0:rows], ALU.add).then_inc(y_sum, 1)
                    dve.wait_ge(ysq, n + 1)
                    dve.tensor_scalar(orstd[0:rows, n, 2:3], ostat[0:rows, n, 2:3], 1.0 / D, EPS,
                                      ALU.mult, ALU.add).then_inc(ymeans, 1)
                    dve.wait_ge(yroots, n + 1)
                    own_step.done(dve.reciprocal(orstd[0:rows, n, 2:3], orstd[0:rows, n, 2:3]))
                    dve.scalar_tensor_tensor(out=y, in0=y, scalar=orstd[0:rows, n, 2:3], in1=norm_row[0:rows],
                                             op0=ALU.mult, op1=ALU.mult).then_inc(y_made, 1)


_INS = ["x_prompt", "x_sample", "c_prompt", "c_sample", "cache_cmp_kv", "cache_slc_kv", "state_win_kv", "state_pool",
        "page_table", "norm_w", "w_ada", "b_ada", "w_in", "pool_w", "pool_scale", "phi_w1", "phi_pe", "phi_w2",
        "gn_pool", "gn_nsa", "w_out", "final_norm"]


def _outs(i):
    depth, batch, seq = i["w_in"].shape[0], i["x_prompt"].shape[0], i["x_prompt"].shape[1]
    rows = i["cache_cmp_kv"].shape[3:]
    win, hist = i["state_win_kv"].shape, i["state_pool"].shape
    new = (depth, *i["x_sample"].shape[:2], *rows)
    prompt = (depth, batch, seq, *rows)
    return [i["x_prompt"].shape, i["x_sample"].shape, prompt, new, prompt, new,
            (depth, batch, min(win[2], seq), *rows), win, (depth, batch, *hist[2:]), hist]


def kernel(**inputs):
    import numpy as np
    import concourse.bacc as bacc
    from concourse.bass_utils import run_bass_kernel_spmd

    nc = bacc.Bacc("TRN2", target_bir_lowering=False, num_devices=1)
    arrays, args = {}, []
    for name in _INS:
        a = np.ascontiguousarray(inputs[name])
        arrays[f"in_{name}"] = a
        args.append(nc.dram_tensor(f"in_{name}", a.shape, mybir.dt.from_np(a.dtype), kind="ExternalInput").ap())
    shapes = _outs({name: inputs[name] for name in _INS})
    for n, shape in enumerate(shapes):
        args.append(nc.dram_tensor(f"out_{n}", shape, F32, kind="ExternalOutput").ap())
    program(nc, *args)
    r = run_bass_kernel_spmd(nc, [arrays], core_ids=[0])
    return tuple(r.results[0][f"out_{n}"] for n in range(len(shapes)))
```
